# Optimizing a Trainium2 kernel written in Bass

```python
import math
import jax, jax.numpy as jnp
from jax import lax
import numpy as np

D_MODEL = 1024
BATCH = 1
SEQ = 1024
DEPTH = 2

SSM_WIDTH = D_MODEL // 2
SSM_GROUP = 16
SSM_GROUPS = SSM_WIDTH // SSM_GROUP
SSM_STATE = 64
DT_MIN = 1e-3
DT_MAX = 1e-1
N_HEADS = 8
QK_NOPE = 64
QK_ROPE = 32
QK_DIM = QK_NOPE + QK_ROPE
V_DIM = 64
Q_LORA = 256
KV_LORA = 128
ROPE_BASE = 10000.0
Q_BLOCK = 128
D_FF = -(-8 * D_MODEL // (3 * 256)) * 256
N_MOD = 6
EPS = 1e-6
IN_SIZES = (SSM_WIDTH, Q_LORA, KV_LORA, QK_ROPE, D_MODEL, D_MODEL)
IN_COLS = SSM_WIDTH + Q_LORA + KV_LORA + QK_ROPE + 2 * D_MODEL

kernel_name = "hybrid_s5_mla_adaln_trunk"

def rms_norm(x, g):
    xf = x.astype(jnp.float32)
    y = xf * lax.rsqrt(jnp.mean(xf * xf, axis=-1, keepdims=True) + EPS)
    return (y * g.astype(jnp.float32)).astype(x.dtype)

def rope(x, cos, sin):
    x1, x2 = jnp.split(x, 2, axis=-1)
    return jnp.concatenate([x1 * cos - x2 * sin, x2 * cos + x1 * sin], axis=-1)

def _ssm_combine(left, right):
    a1r, a1i, b1r, b1i = left
    a2r, a2i, b2r, b2i = right
    return (a2r * a1r - a2i * a1i,
            a2r * a1i + a2i * a1r,
            a2r * b1r - a2i * b1i + b2r,
            a2r * b1i + a2i * b1r + b2i)

def s5_mixer(u, a_re, a_im, log_dt, b_re, b_im, c_re, c_im, d_skip, w_glu, b_glu):
    f32 = jnp.float32
    bsz, L, _ = u.shape
    dt = jnp.exp(log_dt.astype(f32))[:, None]
    ar = a_re.astype(f32)
    ai = a_im.astype(f32)
    mag = jnp.exp(ar * dt)
    abar_re = mag * jnp.cos(ai * dt)
    abar_im = mag * jnp.sin(ai * dt)
    den = ar * ar + ai * ai
    nr = abar_re - 1.0
    ni = abar_im
    coef_re = ((nr * ar + ni * ai) / den)[..., None]
    coef_im = ((ni * ar - nr * ai) / den)[..., None]
    br = b_re.astype(f32)
    bi = b_im.astype(f32)
    bbar_re = coef_re * br - coef_im * bi
    bbar_im = coef_re * bi + coef_im * br
    ug = u.reshape(bsz, L, SSM_GROUPS, SSM_GROUP).astype(f32)
    bu_re = jnp.einsum('blgm,gpm->blgp', ug, bbar_re)
    bu_im = jnp.einsum('blgm,gpm->blgp', ug, bbar_im)
    a_seq_re = jnp.broadcast_to(abar_re[None, None], (1, L, SSM_GROUPS, SSM_STATE))
    a_seq_im = jnp.broadcast_to(abar_im[None, None], (1, L, SSM_GROUPS, SSM_STATE))
    _, _, h_re, h_im = lax.associative_scan(
        _ssm_combine, (a_seq_re, a_seq_im, bu_re, bu_im), axis=1)
    y = (jnp.einsum('blgp,gmp->blgm', h_re, c_re.astype(f32))
         - jnp.einsum('blgp,gmp->blgm', h_im, c_im.astype(f32))
         + d_skip.astype(f32).reshape(SSM_GROUPS, SSM_GROUP) * ug)
    y = jax.nn.gelu(y.reshape(bsz, L, SSM_WIDTH)).astype(u.dtype)
    return y * jax.nn.sigmoid(y @ w_glu + b_glu)

def mla_mixer(cq_in, ckv_in, kr_in, positions, cos, sin, q_norm_g, w_uq, kv_norm_g, w_uk, w_uv):
    bsz, L, _ = cq_in.shape
    cq = rms_norm(cq_in, q_norm_g)
    q = (cq @ w_uq).reshape(bsz, L, N_HEADS, QK_DIM)
    q = jnp.concatenate([q[..., :QK_NOPE],
                         rope(q[..., QK_NOPE:], cos[:, :, None], sin[:, :, None])], axis=-1)
    ckv = rms_norm(ckv_in, kv_norm_g)
    k_nope = (ckv @ w_uk).reshape(bsz, L, N_HEADS, QK_NOPE)
    v = (ckv @ w_uv).reshape(bsz, L, N_HEADS, V_DIM)
    k_pe = rope(kr_in[:, :, None, :], cos[:, :, None], sin[:, :, None])
    k = jnp.concatenate([k_nope, jnp.broadcast_to(k_pe, (bsz, L, N_HEADS, QK_ROPE))], axis=-1)
    scale = QK_DIM ** -0.5
    nb = L // Q_BLOCK
    qb = q.reshape(bsz, nb, Q_BLOCK, N_HEADS, QK_DIM).transpose(1, 0, 2, 3, 4)
    pb = positions.reshape(bsz, nb, Q_BLOCK).transpose(1, 0, 2)
    neg = jnp.finfo(jnp.float32).min

    def attend_block(args):
        qi, pi = args
        s = jnp.einsum('bqhd,bkhd->bhqk', qi, k).astype(jnp.float32) * scale
        mask = positions[:, None, None, :] <= pi[:, None, :, None]
        p = jax.nn.softmax(jnp.where(mask, s, neg), axis=-1).astype(v.dtype)
        return jnp.einsum('bhqk,bkhd->bqhd', p, v)

    o = lax.map(attend_block, (qb, pb))
    return o.transpose(1, 0, 2, 3, 4).reshape(bsz, L, N_HEADS * V_DIM)

def setup_inputs(seed: int = 0) -> dict:
    key = jax.random.key(seed)
    ks = jax.random.split(key, 32)
    nrm = jax.random.normal
    Lr = DEPTH
    G, P, M = SSM_GROUPS, SSM_STATE, SSM_GROUP
    x = nrm(ks[0], (BATCH, SEQ, D_MODEL), jnp.float32)
    c = nrm(ks[1], (BATCH, D_MODEL), jnp.float32)
    offset = jax.random.randint(ks[2], (BATCH, 1), 0, 4096, dtype=jnp.int32)
    positions = offset + jnp.arange(SEQ, dtype=jnp.int32)[None, :]
    n_idx = jnp.arange(P, dtype=jnp.float32)
    inv2 = 0.5 ** 0.5
    return {
        "x": x,
        "c": c,
        "positions": positions,
        "w_ada": nrm(ks[3], (Lr, D_MODEL, N_MOD * D_MODEL)) * (0.5 * D_MODEL ** -0.5),
        "b_ada": nrm(ks[4], (Lr, N_MOD * D_MODEL)) * 0.01,
        "norm1_g": 1.0 + 0.01 * nrm(ks[5], (Lr, D_MODEL)),
        "w_in": nrm(ks[6], (Lr, D_MODEL, IN_COLS)) * D_MODEL ** -0.5,
        "ssm_a_re": -0.5 * jnp.exp(0.02 * nrm(ks[7], (Lr, G, P))),
        "ssm_a_im": math.pi * n_idx[None, None, :] + 0.01 * nrm(ks[8], (Lr, G, P)),
        "ssm_log_dt": jax.random.uniform(ks[9], (Lr, G), jnp.float32, math.log(DT_MIN), math.log(DT_MAX)),
        "ssm_b_re": nrm(ks[10], (Lr, G, P, M)) * (inv2 * M ** -0.5),
        "ssm_b_im": nrm(ks[11], (Lr, G, P, M)) * (inv2 * M ** -0.5),
        "ssm_c_re": nrm(ks[12], (Lr, G, M, P)) * (inv2 * P ** -0.5),
        "ssm_c_im": nrm(ks[13], (Lr, G, M, P)) * (inv2 * P ** -0.5),
        "ssm_d": nrm(ks[14], (Lr, SSM_WIDTH)),
        "w_glu": nrm(ks[15], (Lr, SSM_WIDTH, SSM_WIDTH)) * SSM_WIDTH ** -0.5,
        "b_glu": nrm(ks[16], (Lr, SSM_WIDTH)) * 0.01,
        "w_a_out": nrm(ks[17], (Lr, SSM_WIDTH, D_MODEL)) * SSM_WIDTH ** -0.5,
        "q_norm_g": 1.0 + 0.01 * nrm(ks[18], (Lr, Q_LORA)),
        "w_uq": nrm(ks[19], (Lr, Q_LORA, N_HEADS * QK_DIM)) * Q_LORA ** -0.5,
        "kv_norm_g": 1.0 + 0.01 * nrm(ks[20], (Lr, KV_LORA)),
        "w_uk": nrm(ks[21], (Lr, KV_LORA, N_HEADS * QK_NOPE)) * KV_LORA ** -0.5,
        "w_uv": nrm(ks[22], (Lr, KV_LORA, N_HEADS * V_DIM)) * KV_LORA ** -0.5,
        "w_b_out": nrm(ks[23], (Lr, N_HEADS * V_DIM, D_MODEL)) * (N_HEADS * V_DIM) ** -0.5,
        "w_out": nrm(ks[24], (Lr, D_MODEL, D_MODEL)) * D_MODEL ** -0.5,
        "norm2_g": 1.0 + 0.01 * nrm(ks[25], (Lr, D_MODEL)),
        "w_gate": nrm(ks[26], (Lr, D_MODEL, D_FF)) * D_MODEL ** -0.5,
        "w_up": nrm(ks[27], (Lr, D_MODEL, D_FF)) * D_MODEL ** -0.5,
        "w_down": nrm(ks[28], (Lr, D_FF, D_MODEL)) * D_FF ** -0.5,
        "final_g": 1.0 + 0.01 * nrm(ks[29], (D_MODEL,)),
    }

def reference(x, c, positions, w_ada, b_ada, norm1_g, w_in, ssm_a_re, ssm_a_im, ssm_log_dt,
              ssm_b_re, ssm_b_im, ssm_c_re, ssm_c_im, ssm_d, w_glu, b_glu, w_a_out,
              q_norm_g, w_uq, kv_norm_g, w_uk, w_uv, w_b_out, w_out, norm2_g,
              w_gate, w_up, w_down, final_g):
    inv_freq = ROPE_BASE ** (-jnp.arange(0, QK_ROPE, 2, dtype=jnp.float32) / QK_ROPE)
    ang = positions.astype(jnp.float32)[..., None] * inv_freq
    cos = jnp.cos(ang).astype(x.dtype)
    sin = jnp.sin(ang).astype(x.dtype)
    split_pts = [int(s) for s in np.cumsum(IN_SIZES)[:-1]]
    c_act = jax.nn.silu(c)
    for l in range(DEPTH):
        mod = (c_act @ w_ada[l] + b_ada[l])[:, None, :]
        sh1, sc1, g1, sh2, sc2, g2 = jnp.split(mod, N_MOD, axis=-1)
        h = rms_norm(x, norm1_g[l]) * (1.0 + sc1) + sh1
        z = h @ w_in[l]
        u, cq_in, ckv_in, kr_in, gate_a, gate_b = jnp.split(z, split_pts, axis=-1)
        y_a = s5_mixer(u, ssm_a_re[l], ssm_a_im[l], ssm_log_dt[l], ssm_b_re[l], ssm_b_im[l],
                       ssm_c_re[l], ssm_c_im[l], ssm_d[l], w_glu[l], b_glu[l]) @ w_a_out[l]
        y_b = mla_mixer(cq_in, ckv_in, kr_in, positions, cos, sin, q_norm_g[l], w_uq[l],
                        kv_norm_g[l], w_uk[l], w_uv[l]) @ w_b_out[l]
        merged = jax.nn.sigmoid(gate_a) * y_a + jax.nn.sigmoid(gate_b) * y_b
        x = x + g1 * (merged @ w_out[l])
        h = rms_norm(x, norm2_g[l]) * (1.0 + sc2) + sh2
        x = x + g2 * ((jax.nn.silu(h @ w_gate[l]) * (h @ w_up[l])) @ w_down[l])
    return rms_norm(x, final_g)


_drawn_inputs = setup_inputs


def setup_inputs(seed=0):
    import zlib

    import numpy as np

    out = dict(_drawn_inputs(seed))
    spreads = {}
    factors = {'b_ada': 4.471,
     'norm1_g': 8.0,
     'ssm_a_re': 64.0,
     'ssm_a_im': 64.0,
     'ssm_log_dt': 64.0,
     'ssm_b_re': 64.0,
     'ssm_b_im': 64.0,
     'ssm_c_re': 64.0,
     'ssm_c_im': 64.0,
     'b_glu': 34.476,
     'q_norm_g': 8.0,
     'kv_norm_g': 8.0,
     'norm2_g': 8.0,
     'final_g': 33.738}
    for name, (base, spread) in spreads.items():
        noise = np.random.default_rng([zlib.crc32(name.encode()), seed]).standard_normal(out[name].shape)
        drawn = base * np.exp(spread * noise) if base else spread * noise
        out[name] = __import__('jax').numpy.asarray(drawn.astype(out[name].dtype))
    for name, factor in factors.items():
        out[name] = (out[name] * factor).astype(out[name].dtype)
    return out
```

```python
from contextlib import ExitStack
import math

import numpy as np
import concourse.bass as bass
from concourse import mybir
from concourse.alu_op_type import AluOpType as ALU

ACT = mybir.ActivationFunctionType
F32 = mybir.dt.float32
F32R = mybir.dt.float32r
BF16 = mybir.dt.bfloat16
I32 = mybir.dt.int32

P = 128
EPS = 1e-6
QK_NOPE, QK_ROPE, V_DIM = 64, 32, 64
QK_DIM = QK_NOPE + QK_ROPE
MASKED = 1e30
TWO_PI_PARTS = (6.28125, 0.0019350051879882812, 3.0199159819567e-07)
ROUND = 12582912.0
MAX_ANGLE = 3.1415925
ROPE_ROWS = 6
CONSTS = 19
DVE_CONSTS = 7
S_MAG, S_MAG8, S_AD, S_AD8, S_DT, S_K, S_T1, S_T2, S_NR, S_DEN, S_CR, S_CI, S_SCI = range(6, 19)
S5_EXP_READY, S5_ANGLES_READY, S5_DVE_STEPS = 6, 30, 136
ROW_B_ADA, ROW_N1, ROW_N2, ROW_BGLU, ROW_QN, ROW_KVN, ROW_C, ROW_FG, ROWS = 0, 48, 56, 64, 68, 70, 71, 79, 87


class Count:

    def __init__(self, sem, per_layer, before=0):
        self.sem, self.per_layer, self.before = sem, per_layer, before

    def at(self, l, n):
        return l * self.per_layer + (n + self.before)


def rope_rows():
    r = np.arange(P)
    freq = (10000.0 ** (-np.arange(0, QK_ROPE, 2, dtype=np.float32).astype(np.float64) / QK_ROPE)).astype(np.float32)
    first_half = (r % QK_ROPE) < QK_ROPE // 2
    scale = QK_DIM ** -0.5
    t = np.zeros((P, ROPE_ROWS), np.float32)
    t[:, 0] = freq[r % (QK_ROPE // 2)]
    t[:, 1] = np.where((r >= 64) & (r < 96), -scale, 0)
    t[:, 2] = np.where(r >= 96, np.where(first_half, scale, -scale), 0)
    t[:, 3] = np.where(r < 64, -scale, 0)
    t[:, 4] = (r < 64).astype(np.float32)
    t[:, 5] = np.where(r >= 64, np.where(first_half, -1, 1), 0)
    return t


def trunk(nc, x, c, positions, w_ada, b_ada, norm1_g, w_in, ssm_a_re, ssm_a_im, ssm_log_dt, ssm_b_re,
          ssm_b_im, ssm_c_re, ssm_c_im, ssm_d, w_glu, b_glu, w_a_out, q_norm_g, w_uq, kv_norm_g, w_uk,
          w_uv, w_b_out, w_out, norm2_g, w_gate, w_up, w_down, final_g, rope_const, out):
    DEPTH, D, _ = w_ada.shape
    SEQ = x.shape[1]
    KT = D // P
    TT = SEQ // P
    HALF = SEQ // 2
    SSM = w_glu.shape[1]
    G, N_STATE, M = ssm_b_re.shape[1:]
    CH = 8
    NC = SEQ // CH
    Q_LORA, KV_LORA = w_uq.shape[1], w_uk.shape[1]
    HEADS = w_uk.shape[2] // QK_NOPE
    PAIRS = HEADS // 2
    FT = w_gate.shape[2] // P
    CHUNKS = FT // 2
    SPLIT = (0, SSM, SSM + Q_LORA, SSM + Q_LORA + KV_LORA, SSM + Q_LORA + KV_LORA + QK_ROPE)
    assert (D, SEQ, SSM, G, N_STATE, M, Q_LORA, KV_LORA, HEADS) == (1024, 1024, 512, 32, 64, 16, 256, 128, 8)
    assert CH * M == P and FT % 2 == 0 and CHUNKS % 2 == 1

    U_U = 0
    U_GATE = 4
    U_CQ, U_CKV, U_KR = 20, 22, 23
    U_HEAD = 24
    U_GLU = 32
    U_MERGE = 34
    U_OUT = 42
    U_FFN = 50
    UNITS = U_FFN + 3 * FT
    assert UNITS % 2 == 0

    xs_dram = nc.dram_tensor("xs_scratch", (P, KT, SEQ), F32, kind="Internal").ap()
    gate_dram = nc.dram_tensor("gate_scratch", (2 * KT, P, SEQ), F32, kind="Internal").ap()
    u_dram = nc.dram_tensor("u_scratch", (P, G, CH, M), F32, kind="Internal").ap()

    ctx = ExitStack()
    with ctx:
        base = (nc.sbuf_base + 63) // 64 * 64
        where = [base]
        itemsize = {F32: 4, F32R: 4, BF16: 2, I32: 4}

        def sb(name, shape, dt=F32):
            size = itemsize[dt] * int(np.prod(shape[1:]))
            t = nc.alloc_sbuf_tensor_at(name, list(shape), dt, offset=where[0])
            where[0] += (size + 31) // 32 * 32
            assert where[0] <= nc.sbuf_usable_end, (name, where[0])
            return t

        ident = sb("ident", [P, P])
        ones_col = sb("ones_col", [P, 1])
        mean_col = sb("mean_col", [P, 1])
        eps_col = sb("eps_col", [P, 1])
        sgn = sb("sgn", [P, 1])
        nsgn = sb("nsgn", [P, 1])
        rope_sb = sb("rope_sb", [P, ROPE_ROWS])
        cols = sb("cols", [P, DEPTH, ROWS])
        pcol = sb("pcol", [P, ROWS])
        c_act = sb("c_act", [P, KT])
        mod = sb("mod", [P, 6, KT])
        a1 = sb("a1", [P, KT])
        a2 = sb("a2", [P, KT])
        std = sb("std", [P, 2, TT])
        rstd = sb("rstd", [P, 2, TT])
        neg_max = sb("neg_max", [P, 2])
        row_sum = sb("row_sum", [P, 2])
        row_inv = sb("row_inv", [P, 2])
        mask = sb("mask", [P, TT, SEQ], BF16)
        tq = sb("tq", [P, SEQ])
        tk = sb("tk", [P, SEQ])
        raw = sb("raw", [P, 2, 1024])
        whi = sb("whi", [P, 2, 1024], F32R)
        wlo = sb("wlo", [P, 2, 1024], F32R)
        b_st = sb("b_st", [P, G, M])
        b_sw = sb("b_sw", [P, G, M])
        c_raw = sb("c_raw", [P, 2, 4, P])
        a_raw = sb("a_raw", [G, 2, 2, N_STATE])
        d_raw = sb("d_raw", [G, CH, M])
        ldt = sb("ldt", [P, G])
        zero = where[0]
        K = 1024

        def place(kib):
            where[0] = zero + kib * K

        place(0)
        ada_raw = sb("ada_raw", [P, 2, 1024])
        ada_acc = sb("ada_acc", [P, 1024])
        place(12)
        latn_hi = sb("latn_hi", [P, 3, SEQ], F32R)
        k_hi = sb("k_hi", [P, 2, SEQ], F32R)
        place(128)
        latn_lo = sb("latn_lo", [P, 3, SEQ], F32R)
        k_lo = sb("k_lo", [P, 2, SEQ], F32R)
        place(32)
        h_hi = sb("h_hi", [P, KT, SEQ], F32R)
        h_lo = sb("h_lo", [P, KT, SEQ], F32R)
        x_sb = sb("x_sb", [P, KT, SEQ])
        place(96)
        uc = sb("uc", [P, G, CH, M])
        place(96)
        lat = sb("lat", [P, 3, SEQ])
        lat_sq = sb("lat_sq", [P, 3, SEQ])
        lat_rb = sb("lat_rb", [P, 2, SEQ])
        place(32)
        kr_t = sb("kr_t", [P, 2, SEQ])
        place(128)
        gst = sb("gst", [P, 2, SEQ])
        t_ring = sb("t_ring", [P, 2, SEQ])
        rb = sb("rb", [P, SEQ])
        place(0)
        v_hi = sb("v_hi", [P, TT, P], F32R)
        v_lo = sb("v_lo", [P, TT, P], F32R)
        q_f = sb("q_f", [P, SEQ])
        place(32)
        q_hi = sb("q_hi", [P, 2, SEQ], F32R)
        q_lo = sb("q_lo", [P, 2, SEQ], F32R)
        probs = sb("probs", [P, 3, SEQ])
        pt_hi = sb("pt_hi", [P, 2, TT, 2 * P], F32R)
        pt_lo = sb("pt_lo", [P, 2, TT, 2 * P], F32R)
        assert where[0] <= zero + 96 * K
        place(96)
        o_hi = sb("o_hi", [P, PAIRS, SEQ], F32R)
        o_lo = sb("o_lo", [P, PAIRS, SEQ], F32R)
        place(0)
        yc = sb("yc", [P, CH, SSM])
        be = sb("be", [P, 2, 4, 15, M])
        m_v2 = sb("m_v2", [P, 2, 4, CH, M])
        m_1 = sb("m_1", [P, 2, 4, CH, M])
        m_2 = sb("m_2", [P, 2, 4, CH, M])
        m_tmp = sb("m_tmp", [P, 2, 4, CH, M])
        mt_1 = sb("mt_1", [P, 2, 4, P])
        mt_2 = sb("mt_2", [P, 2, 4, P])
        toe = sb("toe", [P, 2, 4, P])
        ub = sb("ub", [P, 2, 4, P])
        ut = sb("ut", [P, 2, 4, NC])
        rot_b = sb("rot_b", [P, 2, 4, NC])
        z_tmp = sb("z_tmp", [P, 3, 4, NC])
        g_sb = sb("g_sb", [P, 4, NC])
        pq = sb("pq", [P, 2, 4, NC + 1])
        pw = sb("pw", [P, 4, G, CH + 1])
        pw_down = sb("pw_down", [P, 4, G, CH])
        rot1 = sb("rot1", [P, 2, G, 16])
        assert where[0] <= zero + 96 * K
        place(128)
        c_st = sb("c_st", [P, G, M])
        c_sw = sb("c_sw", [P, G, M])
        c_n = sb("c_n", [P, G, M])
        bb = sb("bb", [P, G, M])
        bb_sw = sb("bb_sw", [P, G, M])
        d_t = sb("d_t", [P, G])
        a_t = sb("a_t", [P, 2, G])
        sm = sb("sm", [P, 20, G])
        trig = sb("trig", [P, 6, G])
        rot16 = sb("rot16", [P, 2, G, 8])
        assert where[0] <= zero + 148 * K
        place(16)
        yt = sb("yt", [P, 4, SEQ])
        y_hi = sb("y_hi", [P, 4, SEQ], F32R)
        y_lo = sb("y_lo", [P, 4, SEQ], F32R)
        glu_s = sb("glu_s", [P, 2, SEQ])
        place(0)
        yg_hi = sb("yg_hi", [P, 4, SEQ], F32R)
        place(128)
        yg_lo = sb("yg_lo", [P, 4, SEQ], F32R)
        m_sum = sb("m_sum", [P, SEQ])
        place(16)
        gl = sb("gl", [P, 2, SEQ])
        m_ab = sb("m_ab", [P, 2, SEQ])
        mg_hi = sb("mg_hi", [P, KT, SEQ], F32R)
        mg_lo = sb("mg_lo", [P, KT, SEQ], F32R)
        place(0)
        hid_hi = sb("hid_hi", [P, 2, 2, SEQ], F32R)
        hid_lo = sb("hid_lo", [P, 2, 2, SEQ], F32R)
        place(128)
        silu = sb("silu", [P, 2, SEQ])
        place(32)
        x_in = sb("x_in", [P, TT, D])
        prow = sb("prow", [P, DEPTH, P])
        pos_i = sb("pos_i", [P, SEQ], I32)
        pos_f = sb("pos_f", [P, SEQ])
        posq_i = sb("posq_i", [P, TT], I32)
        posq_i2 = sb("posq_i2", [P, TT], I32)
        posq_f = sb("posq_f", [P, 2, TT])
        ang = sb("ang", [P, SEQ])
        ang_k = sb("ang_k", [P, SEQ])
        half = sb("half", [P, SEQ])
        sin_t = sb("sin_t", [P, SEQ])
        assert where[0] <= zero + 96 * K
        place(12)
        pos_i2 = sb("pos_i2", [P, SEQ], I32)
        pos_lo = sb("pos_lo", [P, SEQ])
        mask_t = sb("mask_t", [P, SEQ])
        place(32)
        fin = sb("fin", [P, KT, SEQ])
        o_row = sb("o_row", [P, 2, D])

        ps = ctx.enter_context(nc.psum_tensor("ps", [P, 8, 512], F32))

        def pair(b, lo=0, hi=P):
            return ps[lo:hi, b:b + 2, :].rearrange("p a b -> p (a b)")

        credits = []

        def count(name, per_layer, before=0, credit=0):
            counter = Count(ctx.enter_context(nc.semaphore(name)), per_layer, before + credit)
            if credit:
                credits.append((counter, credit))
            return counter

        SLOT = 32 * (UNITS // 2)
        raw_loaded = [count("raw0_loaded", SLOT), count("raw1_loaded", SLOT)]
        w_hi_done = count("w_hi_done", UNITS)
        w_lo_done = count("w_lo_done", UNITS, credit=1)
        unit_used = count("unit_used", UNITS, credit=1)
        waited = count("waited", 0)
        const_loaded = count("const_loaded", 0)
        x_in_loaded = count("x_in_loaded", 0)
        pool_const = count("pool_const", 0)
        dve_const = count("dve_const", 0)
        act_const = count("act_const", 0)
        angles_ready = count("angles_ready", 0)
        cols_mm = count("cols_mm", 0)
        xt_mm = count("xt_mm", 0)
        xt_act = count("xt_act", 0)
        xt_dve = count("xt_dve", 0)
        x_spilled = count("x_spilled", 16)
        sq_ready = count("sq_ready", 2 * KT)
        sq_used = count("sq_used", 2 * KT)
        std_ready = count("std_ready", 2)
        rstd_ready = count("rstd_ready", 2)
        rb_mm = count("rb_mm", 2)
        rb_ready = count("rb_ready", 2)
        t_ready = count("t_ready", 2 * KT)
        h_hi_done = count("h_hi_done", 2 * KT)
        h_ready = count("h_ready", 2 * KT, credit=1)
        pcol_ready = count("pcol_ready", 1)
        u_mm = count("u_mm", CH - 1)
        z_act = count("z_act", 4 + 2 * KT)
        u_ev_dve = count("u_ev_dve", 4)
        u_spilled = count("u_spilled", 16)
        gst_spilled = [count("gst0_spilled", 16 * KT, credit=1), count("gst1_spilled", 16 * KT, credit=1)]
        ada_loaded = [count("ada0_loaded", 16 * 24, 16 * 8), count("ada1_loaded", 16 * 24, 16 * 8)]
        ada_used = count("ada_used", 48, 16)
        mod_mm = count("mod_mm", 6, 2)
        mod_ready = count("mod_ready", 6, 2)
        a1_ready = count("a1_ready", 1, 1)
        a2_ready = count("a2_ready", 1)
        lat_sq_ready = count("lat_sq_ready", 3)
        lat_ss = count("lat_ss", 2)
        lat_std = count("lat_std", 1)
        lat_rstd = count("lat_rstd", 1)
        lat_rb_mm = count("lat_rb_mm", 2)
        lat_rb_ready = count("lat_rb_ready", 2)
        lat_t = count("lat_t", 3)
        lat_hi_done = count("lat_hi_done", 3)
        lat_ready = count("lat_ready", 3)
        kr_done = count("kr_done", 3)
        kr_hi_done = count("kr_hi_done", 2)
        kr_ready = count("kr_ready", 2)
        v_mm = count("v_mm", 2 * PAIRS)
        v_hi_done = count("v_hi_done", 2 * PAIRS)
        v_ready = count("v_ready", 2 * PAIRS)
        k_mm = count("k_mm", PAIRS)
        k_hi_done = count("k_hi_done", 2 * PAIRS)
        k_ready = count("k_ready", 2 * PAIRS)
        q_mm = count("q_mm", 2 * PAIRS)
        q_rot = count("q_rot", 2 * PAIRS)
        q_hi_done = count("q_hi_done", 2 * PAIRS)
        q_ready = count("q_ready", 2 * PAIRS)
        s_mm = count("s_mm", 16 * PAIRS)
        s_max = count("s_max", 16 * PAIRS)
        p_exp = count("p_exp", 16 * PAIRS, credit=1)
        p_inv = count("p_inv", 16 * PAIRS)
        p_ready = count("p_ready", 16 * PAIRS)
        pt_mm = count("pt_mm", 32 * PAIRS)
        pt_hi_done = count("pt_hi_done", 32 * PAIRS)
        pt_ready = count("pt_ready", 32 * PAIRS, credit=1)
        pv_mm = count("pv_mm", 8 * PAIRS, credit=1)
        o_hi_done = count("o_hi_done", 4 * PAIRS)
        o_ready = count("o_ready", 4 * PAIRS, credit=1)
        s5_loaded = count("s5_loaded", 16 * 14)
        s5_pe = count("s5_pe", 9, credit=1)
        s5_dve = count("s5_dve", S5_DVE_STEPS)
        s5_act = count("s5_act", 3)
        be_zero = count("be_zero", 1)
        mat_step = count("mat_step", 9 * 8, credit=1)
        ub_loaded = [count("ub0_loaded", 16 * 4), count("ub1_loaded", 16 * 4)]
        s5_tr = count("s5_tr", 3 * 8)
        s5_tr_ev = count("s5_tr_ev", 3 * 8, credit=1)
        toe_mm = count("toe_mm", 8, credit=2)
        toe_ready = count("toe_ready", 8, credit=1)
        v12_mm = count("v12_mm", 8)
        rot_step = count("rot_step", 18 * 8, credit=1)
        y_gelu = count("y_gelu", 8, credit=1)
        yt_mm = count("yt_mm", 8)
        yt_ev = count("yt_ev", 8)
        y_hi_done = count("y_hi_done", 4)
        y_ready = count("y_ready", 4)
        glu_mm = count("glu_mm", 2)
        glu_sig = count("glu_sig", 4)
        glu_mul = count("glu_mul", 4, credit=1)
        yg_hi_done = count("yg_hi_done", 4)
        yg_ready = count("yg_ready", 4)
        gl_loaded = count("gl_loaded", 32 * KT)
        mg_free = count("mg_free", KT, credit=2)
        mg_step = count("mg_step", 2 * KT)
        mg_hi_done = count("mg_hi_done", KT)
        mg_ready = count("mg_ready", KT)
        x_back = count("x_back", 16)
        wo_ev = count("wo_ev", KT, credit=2)
        silu_done = count("silu_done", FT)
        up_done = count("up_done", FT)
        hid_hi_done = count("hid_hi_done", FT)
        hid_ready = count("hid_ready", FT, credit=1)
        dn_mm = count("dn_mm", 6 * CHUNKS)
        dn_ev = count("dn_ev", KT * CHUNKS, credit=KT)
        fin_t = count("fin_t", 0)
        fin_mm = count("fin_mm", 0)
        fin_ev = count("fin_ev", 0)
        out_done = [count("out0_done", 0), count("out1_done", 0)]

        def wait(eng, counter, l, n):
            eng.wait_ge(counter.sem, counter.at(l, n))

        def apart(eng):
            eng.sem_inc(waited.sem, 1)

        def raw_slot(n):
            return raw[:, n % 2, :]

        def unit_ready(eng, l, n, q=0):
            eng.wait_ge(w_lo_done.sem, w_lo_done.at(l, n + 1) + 2 * q)

        def plain(view):
            return [(lambda t: t, view)]

        def head_pieces(parity_cols):
            def dst(a, b):
                return lambda t: t[:, 0:2 * P].rearrange("p (k n) -> p k n", k=2)[:, :, a:b]

            def src(a, b):
                return lambda t: t[:, 0:2 * QK_DIM].rearrange("p (k n) -> p k n", k=2)[:, :, a:b]
            return [(dst(0, 96), src(0, 96)), (dst(96, 112), src(80, 96)), (dst(112, 128), src(64, 80)),
                    (lambda t: t[:, 256:384], lambda t: t[:, 192:320])]

        PLAIN = [(lambda t: t, lambda t: t)]
        HEAD = head_pieces(None)

        def kr_pieces():
            def src(a, b):
                return lambda t: t[:, 0:KT * QK_ROPE].rearrange("p (k n) -> p k n", k=KT)[:, :, a:b]

            def dst(a, b):
                return lambda t: t.rearrange("p (k n) -> p k n", k=KT)[:, :, a:b]
            return [(dst(0, 32), src(0, 32)), (dst(32, 64), src(0, 32)),
                    (dst(64, 80), src(16, 32)), (dst(80, 96), src(0, 16)),
                    (dst(96, 112), src(16, 32)), (dst(112, 128), src(0, 16))]

        KR = kr_pieces()

        def split_hi(act, l, n, q=0, pieces=PLAIN):
            s = n % 2
            act.wait_ge(raw_loaded[s].sem, raw_loaded[s].at(l, 32 * (n // 2 + 1)) + 32 * q)
            act.wait_ge(unit_used.sem, unit_used.at(l, max(n - 1, 0)) + 2 * q)
            for dst, src in pieces:
                last = act.activation(dst(whi[:, s, :]), src(raw[:, s, :]), ACT.Copy)
            last.then_inc(w_hi_done.sem, 1)

        def split_lo(pool, l, n, q=0, pieces=PLAIN):
            s = n % 2
            pool.wait_ge(w_hi_done.sem, w_hi_done.at(l, n + 1) + 2 * q)
            for dst, src in pieces:
                last = pool.tensor_tensor(dst(wlo[:, s, :]), src(raw[:, s, :]), dst(whi[:, s, :].bitcast(F32)),
                                          ALU.subtract)
            last.then_inc(w_lo_done.sem, 1)

        def load_unit(sp, l, n, parts, q=0):
            s = n % 2
            sp.wait_ge(w_lo_done.sem, w_lo_done.at(l, max(n - 1, 0)) + 2 * q)
            assert len(parts) == 2
            for dst, src in parts:
                sp.dma_start(dst, src).then_inc(raw_loaded[s].sem, 16)

        def products(pe, outs, w_h, w_l, xs, first, last):
            for o, (x_h, _) in zip(outs, xs):
                pe.matmul(o, w_h, x_h, start=first, stop=False)
            for o, (_, x_l) in zip(outs, xs):
                pe.matmul(o, w_h, x_l, start=False, stop=False)
            return [pe.matmul(o, w_l, x_h, start=False, stop=last) for o, (x_h, _) in zip(outs, xs)]

        def halves(hi, lo, k):
            return [(hi[:, k, t * HALF:(t + 1) * HALF], lo[:, k, t * HALF:(t + 1) * HALF]) for t in range(2)]

        def tile_products(pe, s, bank, hi, lo, kts, n_cols=P, col=0, first=True, last=True):
            kts = list(kts)
            view_h = whi[:, s, :].rearrange("p (k n) -> p k n", n=n_cols)
            view_l = wlo[:, s, :].rearrange("p (k n) -> p k n", n=n_cols)
            for wk, xk in kts:
                end = products(pe, [ps[:, bank, :], ps[:, bank + 1, :]], view_h[:, wk, col:col + P],
                               view_l[:, wk, col:col + P], halves(hi, lo, xk),
                               first and wk == kts[0][0], last and wk == kts[-1][0])
            return end

        block = ctx.enter_context(nc.Block())

        @block.sync
        def _(sp):
            for dst, src in ((rope_sb[:, :], rope_const),
                             (prow[0:ROW_N1, 0, :], b_ada[0].rearrange("(r p) -> r p", p=P))):
                sp.dma_start(dst, src).then_inc(const_loaded.sem, 16)
            for l in range(DEPTH):
                rows = [(ROW_N1, norm1_g[l]), (ROW_N2, norm2_g[l]), (ROW_BGLU, b_glu[l]), (ROW_QN, q_norm_g[l]),
                        (ROW_KVN, kv_norm_g[l]), (ROW_C, c[0]), (ROW_FG, final_g)]
                if l:
                    rows.append((ROW_B_ADA, b_ada[l]))
                for r, v in rows:
                    n = v.shape[0] // P
                    sp.dma_start(prow[r:r + n, l, :], v.rearrange("(r p) -> r p", p=P)).then_inc(const_loaded.sem, 16)
            sp.dma_start(pos_i[:, :], positions[0].rearrange("(o n) -> o n", o=1).broadcast_to([P, SEQ]))\
                .then_inc(const_loaded.sem, 16)
            sp.dma_start(posq_i[:, :], positions[0].rearrange("(t p) -> p t", p=P), allow_slow_non_contiguous=True).then_inc(const_loaded.sem, 16)

            def load_ada(l, m, k, at_l, number):
                s = k % 2
                if number is not None:
                    sp.wait_ge(ada_used.sem, number)
                    apart(sp)
                sp.dma_start(ada_raw[:, s, :], w_ada[l][k * P:(k + 1) * P, m]).then_inc(ada_loaded[s].sem, 16)

            for m in range(2):
                for k in range(KT):
                    n = m * KT + k
                    load_ada(0, slice(m * D, (m + 1) * D), k, 0, n - 1 if n >= 2 else None)
                    if n == 3:
                        for t in range(TT):
                            sp.dma_start(x_in[:, t, :], x[0, t * P:(t + 1) * P, :]).then_inc(x_in_loaded.sem, 16)

            with sp.Fori(0, DEPTH) as l:
                w_in_l = w_in[l]

                def u_unit(n):
                    src = w_in_l[2 * n * P:(2 * n + 2) * P, 0:SSM]
                    return [(raw[:, n % 2, k * SSM:(k + 1) * SSM], src[k * P:(k + 1) * P, :]) for k in range(2)]

                def tile_unit(n, w, col, kts=KT):
                    src = w[:, col].rearrange("(k p) n -> p k n", p=P)
                    dst = raw[:, n % 2, 0:kts * P].rearrange("p (k n) -> p k n", k=kts)
                    h = kts // 2
                    return [(dst[:, 0:h, :], src[:, 0:h, :]), (dst[:, h:kts, :], src[:, h:kts, :])]

                load_unit(sp, l, 0, u_unit(0))
                load_unit(sp, l, 1, u_unit(1))
                wait(sp, glu_mul, l, 0)
                apart(sp)
                for half_of, (re, im) in enumerate(((ssm_b_re, ssm_b_im), (ssm_b_im, ssm_b_re))):
                    dst = (b_st, b_sw)[half_of]
                    sp.dma_start(dst[0:64, :, :], re[l].rearrange("g p m -> p g m")).then_inc(s5_loaded.sem, 16)
                    sp.dma_start(dst[64:P, :, :], im[l].rearrange("g p m -> p g m")).then_inc(s5_loaded.sem, 16)
                for half_of, (re, im) in enumerate(((ssm_c_re, ssm_c_im), (ssm_c_im, ssm_c_re))):
                    for side, v in enumerate((re, im)):
                        sp.dma_start(c_raw[:, half_of, :, side * 64:(side + 1) * 64],
                                     v[l].rearrange("(t g) m p -> (g m) t p", t=4)).then_inc(s5_loaded.sem, 16)
                for i, v in enumerate((ssm_a_re, ssm_a_im)):
                    for dup in range(2):
                        sp.dma_start(a_raw[:, i, dup, :], v[l]).then_inc(s5_loaded.sem, 16)
                sp.dma_start(ldt[:, :], ssm_log_dt[l].rearrange("(o g) -> o g", o=1).broadcast_to([P, G]))\
                    .then_inc(s5_loaded.sem, 16)
                sp.dma_start(d_raw[:, :, :], ssm_d[l].rearrange("(g o m) -> g o m", o=1, m=M)
                             .broadcast_to([G, CH, M])).then_inc(s5_loaded.sem, 16)
                load_unit(sp, l, 2, u_unit(2))
                load_unit(sp, l, 3, u_unit(3))
                wait(sp, dn_ev, l, 0)
                apart(sp)
                with sp.Fori(0, 4) as i:
                    for j in range(4):
                        load_unit(sp, l, U_GATE + j, tile_unit(j, w_in_l, bass.ds((i * 4 + j) * P + SPLIT[4], P)), 2 * i)
                        for k in (2 * j, 2 * j + 1):
                            load_ada(l, bass.ds((i + 2) * D, D), k, l, ada_used.at(l, k - 1) + KT * i)
                load_unit(sp, l, U_CQ, tile_unit(U_CQ, w_in_l, slice(SPLIT[1], SPLIT[1] + P)))
                load_unit(sp, l, U_CQ + 1, tile_unit(U_CQ + 1, w_in_l, slice(SPLIT[1] + P, SPLIT[1] + 2 * P)))
                load_unit(sp, l, U_CKV, tile_unit(U_CKV, w_in_l, slice(SPLIT[2], SPLIT[2] + P)))
                src = w_in_l[:, SPLIT[3]:SPLIT[4]].rearrange("(k p) n -> p k n", p=P)
                dst = raw[:, U_KR % 2, 0:KT * QK_ROPE].rearrange("p (k n) -> p k n", k=KT)
                load_unit(sp, l, U_KR, [(dst[:, 0:4, :], src[:, 0:4, :]), (dst[:, 4:8, :], src[:, 4:8, :])])
                apart(sp)
                with sp.Fori(0, PAIRS) as i:
                    for j in range(2):
                        uq = w_uq[l][:, bass.ds((2 * i + j) * QK_DIM, QK_DIM)].rearrange("(k p) n -> p k n", p=P)
                        pair_w = (w_uk, w_uv)[j][l][:, bass.ds(i * P, P)]
                        load_unit(sp, l, U_HEAD + j,
                                  [(raw[:, j, 0:2 * QK_DIM].rearrange("p (k n) -> p k n", k=2), uq),
                                   (raw[:, j, 2 * QK_DIM:2 * QK_DIM + P], pair_w)], i)
                for a in range(2):
                    src = w_glu[l][:, 2 * a * P:(2 * a + 2) * P].rearrange("(k p) n -> p k n", p=P)
                    dst = raw[:, a, :].rearrange("p (k n) -> p k n", k=4)
                    load_unit(sp, l, U_GLU + a, [(dst[:, 0:2, :], src[:, 0:2, :]), (dst[:, 2:4, :], src[:, 2:4, :])])
                wait(sp, pv_mm, l, 8 * PAIRS)
                apart(sp)
                wait(sp, u_spilled, l, 16)
                apart(sp)
                with sp.Fori(0, 4) as i:
                    for j in range(2):
                        sp.wait_ge(s5_pe.sem, s5_pe.at(l, j) + 2 * i)
                        src = u_dram[:, bass.ds((2 * i + j) * 4, 4)].rearrange("c g j m -> c g (j m)")
                        sp.dma_start(ub[:, j, :, :], src).then_inc(ub_loaded[j].sem, 16)
                apart(sp)
                with sp.Fori(0, 4) as i:
                    for j in range(2):
                        col = bass.ds((2 * i + j) * P, P)
                        dst = raw[:, j, :].rearrange("p (k n) -> p k n", k=8)
                        load_unit(sp, l, U_MERGE + j,
                                  [(dst[:, 0:4, :], w_a_out[l][:, col].rearrange("(k p) n -> p k n", p=P)),
                                   (dst[:, 4:8, :], w_b_out[l][:, col].rearrange("(k p) n -> p k n", p=P))], i)
                        if j == 0:
                            wait(sp, glu_mul, l, 4)
                            wait(sp, gst_spilled[0], l, 16 * KT)
                            wait(sp, gst_spilled[1], l, 16 * KT)
                        sp.wait_ge(mg_free.sem, mg_free.at(l, j) + 2 * i)
                        for side in range(2):
                            src = gate_dram[bass.ds(2 * i + (j + side * KT), 1)].rearrange("o p n -> (o p) n")
                            sp.dma_start(gl[:, side, :], src).then_inc(gl_loaded.sem, 16)
                apart(sp)
                with sp.Fori(0, 2) as i:
                    for j in range(4):
                        load_unit(sp, l, U_OUT + j, tile_unit(j, w_out[l], bass.ds((i * 4 + j) * P, P)), 2 * i)
                        if j == 1:
                            wait(sp, unit_used, l, U_OUT)
                        for k in ((), range(0, 4), (4, 5), (6, 7))[j]:
                            load_ada(1 - l, bass.ds(i * D, D), k, l, ada_used.at(l, 4 * KT + k - 1) + KT * i)

                def ffn_unit(n, w, col):
                    return tile_unit(n, w[l], col)

                def down_unit(n, rows, d):
                    src = w_down[l][rows, d * 4 * P:(d + 1) * 4 * P].rearrange("(k p) n -> k p n", p=P)
                    return [(raw[:, n % 2, k * 4 * P:(k + 1) * 4 * P], src[k]) for k in range(2)]

                for a in range(2):
                    for w_i, w in enumerate((w_gate, w_up)):
                        n = U_FFN + 2 * a + w_i
                        load_unit(sp, l, n, ffn_unit(n, w, slice(a * P, (a + 1) * P)))
                apart(sp)
                with sp.Fori(0, (CHUNKS - 1) // 2) as i:
                    for cc in range(2):
                        n = U_FFN + 4 + 6 * cc
                        for a in range(2):
                            for w_i, w in enumerate((w_gate, w_up)):
                                col = bass.ds((i * 4 + (2 + 2 * cc + a)) * P, P)
                                load_unit(sp, l, n + 2 * a + w_i, ffn_unit(n + 2 * a + w_i, w, col), 6 * i)
                        for d in range(2):
                            rows = bass.ds((i * 4 + 2 * cc) * P, 2 * P)
                            load_unit(sp, l, n + 4 + d, down_unit(n + 4 + d, rows, d), 6 * i)
                for d in range(2):
                    rows = slice((FT - 2) * P, FT * P)
                    load_unit(sp, l, UNITS - 2 + d, down_unit(d, rows, d))
            for t in range(TT):
                sp.wait_ge(fin_ev.sem, t + 1)
                sp.dma_start(out[0, t * P:(t + 1) * P, :], o_row[:, t % 2, :]).then_inc(out_done[t % 2].sem, 16)
            for s in out_done:
                sp.wait_ge(s.sem, 16 * (TT // 2))

        @block.gpsimd
        def _(pool):
            pool.memset(ident[:, :], 0.0).then_inc(pool_const.sem, 1)
            pool.wait_ge(pool_const.sem, 1)
            pool.affine_select(out=ident[:, :], in_=ident[:, :], compare_op=ALU.not_equal, fill=1.0, base=0,
                               pattern=[[-1, P]], channel_multiplier=1).then_inc(pool_const.sem, 1)
            with pool.Fori(0, DEPTH) as l:
                for n in range(U_GATE):
                    split_lo(pool, l, n)
                apart(pool)
                with pool.Fori(0, 4) as i:
                    for j in range(4):
                        split_lo(pool, l, U_GATE + j, 2 * i)
                for n in (U_CQ, U_CQ + 1, U_CKV):
                    split_lo(pool, l, n)
                split_lo(pool, l, U_KR, 0, KR)

                apart(pool)
                with pool.Fori(0, PAIRS) as i:
                    for j in range(2):
                        split_lo(pool, l, U_HEAD + j, i, HEAD)
                split_lo(pool, l, U_GLU)
                split_lo(pool, l, U_GLU + 1)

                wait(pool, pv_mm, l, 8 * PAIRS)
                apart(pool)
                pool.memset(be[:, :, :, CH:, :], 0.0).then_inc(be_zero.sem, 1)
                wait(pool, s5_dve, l, S5_DVE_STEPS)
                apart(pool)
                with pool.Fori(0, 4) as i:
                    for j in range(2):
                        pool.wait_ge(toe_mm.sem, toe_mm.at(l, j - 1) + 2 * i)
                        grp = bass.ds((i * 2 + j) * 4, 4)
                        step = [9 * j]

                        def by_powers(v, powers):
                            return v[:, grp, powers].unsqueeze(3).broadcast_to([P, 4, CH, M])

                        def by_channels(v):
                            return v[:, grp, :].unsqueeze(2).broadcast_to([P, 4, CH, M])

                        def combine(dst, p_a, v_a, p_b, v_b, powers, op):
                            pool.wait_ge(mat_step.sem, mat_step.at(l, step[0]) + 18 * i)
                            pool.tensor_tensor(m_tmp[:, 0], by_powers(p_a, powers), by_channels(v_a), ALU.mult)\
                                .then_inc(mat_step.sem, 1)
                            pool.tensor_tensor(m_tmp[:, 1], by_powers(p_b, powers), by_channels(v_b), ALU.mult)\
                                .then_inc(mat_step.sem, 1)
                            pool.wait_ge(mat_step.sem, mat_step.at(l, step[0] + 2) + 18 * i)
                            pool.tensor_tensor(dst, m_tmp[:, 0], m_tmp[:, 1], op).then_inc(mat_step.sem, 1)
                            step[0] += 3

                        down = slice(0, CH)
                        re, im, nre, sim = (pw_down[:, t] for t in range(4))
                        combine(be[:, j, :, 0:CH, :], re, bb, sim, bb_sw, down, ALU.add)
                        combine(m_v2[:, j], nre, bb_sw, im, bb, down, ALU.add)
                        up = slice(1, CH + 1)
                        re, im, nre, sim = (pw[:, t] for t in range(4))
                        pool.wait_ge(s5_pe.sem, s5_pe.at(l, j) + 2 * i)
                        combine(m_1[:, j], nre, c_st, im, c_sw, up, ALU.subtract)
                apart(pool)
                with pool.Fori(0, 4) as i:
                    for j in range(2):
                        split_lo(pool, l, U_MERGE + j, i)
                apart(pool)
                with pool.Fori(0, 4) as i:
                    for j in range(2):
                        split_lo(pool, l, U_OUT + j, i)
                apart(pool)
                with pool.Fori(0, 3 * FT // 6) as i:
                    for j in range(6):
                        split_lo(pool, l, U_FFN + j, 3 * i)

        @block.tensor
        def _(pe):
            pe.wait_ge(pool_const.sem, 2)
            pe.wait_ge(const_loaded.sem, 16 * CONSTS)
            for d in range(DEPTH):
                last = pe.transpose(ps[:, 0, d * P:d * P + ROWS], prow[0:ROWS, d, :], ident[0:ROWS, 0:ROWS])
            last.then_inc(cols_mm.sem, 1)
            pe.wait_ge(x_in_loaded.sem, 16 * TT)
            for k in range(KT):
                b = 2 + 2 * (k % 2)
                if k >= 2:
                    pe.wait_ge((xt_act, xt_dve)[k % 2].sem, k // 2)
                for t in range(TT):
                    last = pe.transpose(ps[:, b + t // 4, (t % 4) * P:(t % 4 + 1) * P],
                                        x_in[:, t, k * P:(k + 1) * P], ident[:, :])
                last.then_inc(xt_mm.sem, 1)

            def mod_products():
                for n in range(KT):
                    last = pe.matmul(ps[:, 7, n:n + 1], ada_acc[:, n * P:(n + 1) * P], ones_col[:, :],
                                     start=True, stop=True)
                last.then_inc(mod_mm.sem, 1)

            for m in range(2):
                pe.wait_ge(ada_used.sem, KT * (m + 1))
                pe.wait_ge(mod_ready.sem, m)
                mod_products()

            def norm(l, occ):
                for k in range(KT):
                    wait(pe, sq_ready, l, KT * occ + k + 1)
                    for t in range(TT):
                        last = pe.matmul(ps[:, 6, t:t + 1], t_ring[:, k % 2, t * P:(t + 1) * P], mean_col[:, :],
                                         start=(k == 0 and t == 0), stop=(k == KT - 1), skip_group_check=True)
                    last.then_inc(sq_used.sem, 1)
                wait(pe, rstd_ready, l, occ + 1)
                for t in range(TT):
                    last = pe.matmul(ps[:, 4 + t // 4, (t % 4) * P:(t % 4 + 1) * P],
                                     rstd[:, 0, t:t + 1].broadcast_to([P, P]), ident[:, :], start=True, stop=True)
                last.then_inc(rb_mm.sem, 1)

            with pe.Fori(0, DEPTH) as l:
                norm(l, 0)
                wait(pe, rb_ready, l, 1)
                wait(pe, mod_ready, l, 0)
                for n in range(U_GATE):
                    unit_ready(pe, l, n)
                    for kk in range(2):
                        k = 2 * n + kk
                        wait(pe, h_ready, l, k + 1)
                        w_h, w_l = (w[:, n % 2, kk * SSM:(kk + 1) * SSM] for w in (whi, wlo))
                        for j in range(CH):
                            x_h, x_l = h_hi[:, k, j::CH], h_lo[:, k, j::CH]
                            pe.matmul(ps[:, j, :], x_h, w_h, start=(k == 0), stop=False)
                            pe.matmul(ps[:, j, :], x_h, w_l, start=False, stop=False)
                            last = pe.matmul(ps[:, j, :], x_l, w_h, start=False, stop=(k == KT - 1))
                            if k == KT - 1 and j < CH - 1:
                                last.then_inc(u_mm.sem, 1)
                    last.then_inc(unit_used.sem, 1)
                wait(pe, u_ev_dve, l, 4)
                apart(pe)
                with pe.Fori(0, 4) as i:
                    for j in range(4):
                        b = 2 * (j % 2)
                        unit_ready(pe, l, U_GATE + j, 2 * i)
                        pe.wait_ge(z_act.sem, z_act.at(l, j + 3) + 4 * i)
                        end = tile_products(pe, j % 2, b, h_hi, h_lo, [(k, k) for k in range(KT)])
                        end[1].then_inc(unit_used.sem, 1)
                    pe.wait_ge(ada_used.sem, ada_used.at(l, KT) + KT * i)
                    pe.wait_ge(mod_ready.sem, mod_ready.at(l, 0) + i)
                    mod_products()
                wait(pe, z_act, l, 4 + 2 * KT)
                wait(pe, mod_ready, l, 4)
                for u in range(U_CQ, U_KR + 1):
                    unit_ready(pe, l, u)
                    end = tile_products(pe, u % 2, 2 * (u - U_CQ), h_hi, h_lo, [(k, k) for k in range(KT)])
                    end[1].then_inc(unit_used.sem, 1)
                for side, tiles in enumerate(((0, 1), (2,))):
                    wait(pe, lat_sq_ready, l, tiles[-1] + 1)
                    for a in tiles:
                        for t in range(TT):
                            last = pe.matmul(ps[:, 2 * side, t:t + 1], lat_sq[:, a, t * P:(t + 1) * P], mean_col[:, :],
                                             start=(a == tiles[0] and t == 0), stop=(a == tiles[-1]),
                                             skip_group_check=True)
                    last.then_inc(lat_ss.sem, 1)
                wait(pe, lat_rstd, l, 1)
                for side in range(2):
                    for t in range(TT):
                        last = pe.matmul(ps[:, 2 * side + t // 4, (t % 4) * P:(t % 4 + 1) * P],
                                         rstd[:, side, t:t + 1].broadcast_to([P, P]), ident[:, :],
                                         start=True, stop=True)
                    last.then_inc(lat_rb_mm.sem, 1)

                wait(pe, lat_ready, l, 3)
                wait(pe, kr_ready, l, 2)
                wait(pe, lat_rb_ready, l, 2)

                even, odd = U_HEAD % 2, 1 - U_HEAD % 2

                def queries(s, bank):
                    w_h, w_l = whi[:, s, :], wlo[:, s, :]
                    for k in range(2):
                        end = products(pe, [ps[:, bank, :], ps[:, bank + 1, :]], w_h[:, k * P:(k + 1) * P],
                                       w_l[:, k * P:(k + 1) * P], halves(latn_hi, latn_lo, k), k == 0, k == 1)
                    end[1].then_inc(q_mm.sem, 1)

                def even_queries(i, ahead):
                    unit_ready(pe, l, U_HEAD + 2 * ahead, i)
                    if ahead:
                        pe.wait_ge(p_exp.sem, p_exp.at(l, 15) + 16 * i)
                    queries(even, 0)

                def both_keys(i, ahead):
                    if ahead:
                        pe.wait_ge(p_exp.sem, p_exp.at(l, 16) + 16 * i)
                    for t in range(2):
                        last = products(pe, [ps[:, 2 + t, :]], whi[:, even, 256:384], wlo[:, even, 256:384],
                                        [halves(latn_hi, latn_lo, 2)[t]], True, True)[0]
                    last.then_inc(k_mm.sem, 1)

                def attention_pair(i, last_pair):
                    def scores(g):
                        head = g // 8
                        q = slice((g % 8) * P, (g % 8 + 1) * P)
                        b = 2 * (g % 2)
                        if g >= 2:
                            pe.wait_ge(p_exp.sem, p_exp.at(l, g - 1) + 16 * i)
                        for t in range(2):
                            kk = slice(t * HALF, (t + 1) * HALF)
                            first = pe.matmul(ps[:, b + t, :], q_hi[:, head, q], k_hi[:, head, kk], start=True, stop=False)
                            if t == 0 and g in (0, 3):
                                first.then_inc(unit_used.sem, 1)
                            pe.matmul(ps[:, b + t, :], q_hi[:, head, q], k_lo[:, head, kk], start=False, stop=False)
                            last = pe.matmul(ps[:, b + t, :], q_lo[:, head, q], k_hi[:, head, kk], start=False, stop=True)
                        last.then_inc(s_mm.sem, 1)

                    def transposes(g):
                        pe.wait_ge(p_ready.sem, p_ready.at(l, g + 1) + 16 * i)
                        for t in range(2):
                            if g:
                                pe.wait_ge(pt_ready.sem, pt_ready.at(l, 2 * g - 1 + t) + 32 * i)
                            for k in range(4):
                                kt = 4 * t + k
                                last = pe.transpose(ps[:, 4 + t, k * P:(k + 1) * P], probs[:, g % 3, kt * P:(kt + 1) * P],
                                                    ident[:, :])
                            last.then_inc(pt_mm.sem, 1)

                    def outputs(n, part):
                        m = n // 2
                        if part == 0:
                            if n % 2 == 0 and m >= 2:
                                pe.wait_ge(o_ready.sem, o_ready.at(l, m - 1) + 4 * i)
                            pe.wait_ge(pt_ready.sem, pt_ready.at(l, 4 * (n + 1)) + 32 * i)
                        out_ = ps[:, 6 + m % 2, (n % 2) * 2 * P:(n % 2 + 1) * 2 * P]
                        for k in range(4 * part, 4 * part + 4):
                            last = products(pe, [out_], v_hi[:, k, :], v_lo[:, k, :],
                                            [(pt_hi[:, n % 2, k, :], pt_lo[:, n % 2, k, :])],
                                            k == 0, k == TT - 1)[0]
                        if part:
                            last.then_inc(pv_mm.sem, 1)

                    def values():
                        unit_ready(pe, l, U_HEAD + 1, i)
                        pe.wait_ge(pt_ready.sem, pt_ready.at(l, 0) + 32 * i)
                        for t in range(TT):
                            tok = slice(t * P, (t + 1) * P)
                            bank = ps[:, 4 + t // 4, (t % 4) * P:(t % 4 + 1) * P]
                            pe.matmul(bank, latn_hi[:, 2, tok], whi[:, odd, 256:384], start=True, stop=False)
                            pe.matmul(bank, latn_hi[:, 2, tok], wlo[:, odd, 256:384], start=False, stop=False)
                            last = pe.matmul(bank, latn_lo[:, 2, tok], whi[:, odd, 256:384], start=False, stop=True)
                            if t % 4 == 3:
                                last.then_inc(v_mm.sem, 1)

                    for g in range(20):
                        if 2 <= g <= 17:
                            if g == 2:
                                pe.wait_ge(v_ready.sem, v_ready.at(l, 2) + 2 * i)
                            transposes(g - 2)
                        if g < 2:
                            pe.wait_ge(q_ready.sem, q_ready.at(l, 1) + 2 * i)
                            pe.wait_ge(k_ready.sem, k_ready.at(l, 2) + 2 * i)
                        if g == 8:
                            pe.wait_ge(q_ready.sem, q_ready.at(l, 2) + 2 * i)
                        if g < 16:
                            scores(g)
                        if g == 0:
                            values()
                        if g == 1:
                            pe.wait_ge(o_ready.sem, o_ready.at(l, 0) + 4 * i)
                            queries(odd, 6)
                        if g == 16 and not last_pair:
                            even_queries(i, 1)
                        if g == 17 and not last_pair:
                            both_keys(i, 1)
                        if g >= 4:
                            if g == 4:
                                pe.wait_ge(q_rot.sem, q_rot.at(l, 2) + 2 * i)
                            outputs((g - 4) // 2, g % 2)

                even_queries(0, 0)
                both_keys(0, 0)
                apart(pe)
                with pe.Fori(0, PAIRS - 1) as i:
                    attention_pair(i, False)
                attention_pair(PAIRS - 1, True)

                wait(pe, o_ready, l, 4 * PAIRS)
                wait(pe, s5_loaded, l, 16 * 14)
                apart(pe)
                for i in range(2):
                    pe.transpose(ps[:, 0, i * G:(i + 1) * G], a_raw[:, i, :, :].rearrange("g a p -> g (a p)"),
                                 ident[0:G, 0:G])
                pe.transpose(ps[:, 0, 2 * G:3 * G], d_raw[:, :, :].rearrange("g j m -> g (j m)"), ident[0:G, 0:G])
                for s in range(2):
                    for t in range(4):
                        last = pe.transpose(ps[:, 1 + s, t * P:(t + 1) * P], c_raw[:, s, t, :], ident[:, :])
                last.then_inc(s5_pe.sem, 1)
                wait(pe, s5_dve, l, S5_DVE_STEPS)
                wait(pe, be_zero, l, 1)
                apart(pe)
                def batch_inputs(b, i):
                    j = b % 2
                    pe.wait_ge(mat_step.sem, mat_step.at(l, 9 * b + 6) + 18 * i)
                    pe.wait_ge(s5_tr_ev.sem, s5_tr_ev.at(l, 3 * b) + 6 * i)
                    for side in range(2):
                        for g in range(4):
                            src = be[:, j, g, 0:CH, :] if side == 0 else m_v2[:, j, g, :, :]
                            last = pe.transpose(ps[:, side, g * P:(g + 1) * P],
                                                src.rearrange("p j m -> p (j m)"), ident[:, :])
                        last.then_inc(s5_tr.sem, 1)
                    pe.wait_ge(ub_loaded[j].sem, ub_loaded[j].at(l, 16 * (b // 2 + 1)) + 16 * i)
                    for g in range(4):
                        last = pe.transpose(ps[:, 3, g * P:(g + 1) * P], ub[:, j, g, :], ident[:, :])
                    last.then_inc(s5_tr.sem, 1)
                    pe.wait_ge(toe_ready.sem, toe_ready.at(l, b) + 2 * i)
                    flat = be[:, j, :, :, :].rearrange("p g b m -> p g (b m)")
                    for g in range(4):
                        for jj in range(CH):
                            lo = (CH - 1 - jj) * M
                            last = pe.matmul(ps[:, 2, g * P + jj * M:g * P + (jj + 1) * M], flat[:, g, lo:lo + P],
                                             c_n[:, bass.ds((i * 2 + b) * 4 + g, 1), :].rearrange("p o m -> p (o m)"),
                                             start=True, stop=True)
                    last.then_inc(toe_mm.sem, 1)
                    pe.wait_ge(s5_tr_ev.sem, s5_tr_ev.at(l, 3 * b + 3) + 6 * i)
                    pe.wait_ge(rot_step.sem, rot_step.at(l, 18 * b) + 36 * i)
                    for side, mt in enumerate((mt_1, mt_2)):
                        for g in range(4):
                            last = pe.matmul(ps[:, 4 + side, g * P:(g + 1) * P], mt[:, j, g, :], ut[:, j, g, :],
                                             start=True, stop=True)
                    last.then_inc(v12_mm.sem, 1)

                def batch_outputs(b, i):
                    j = b % 2
                    pe.wait_ge(mat_step.sem, mat_step.at(l, 9 * b + 9) + 18 * i)
                    pe.wait_ge(toe_ready.sem, toe_ready.at(l, b + 1) + 2 * i)
                    pe.wait_ge(rot_step.sem, rot_step.at(l, 18 * b + 18) + 36 * i)
                    pe.wait_ge(y_gelu.sem, y_gelu.at(l, max(b - 1, 0)) + 2 * i)
                    for g in range(4):
                        o = ps[:, 6 + j, g * P:(g + 1) * P]
                        pe.matmul(o, ut[:, j, g, :], toe[:, j, g, :], start=True, stop=False)
                        pe.matmul(o, pq[:, 0, g, 0:NC], m_1[:, j, g, :, :].rearrange("p j m -> p (j m)"),
                                  start=False, stop=False)
                        last = pe.matmul(o, pq[:, 1, g, 0:NC], m_2[:, j, g, :, :].rearrange("p j m -> p (j m)"),
                                         start=False, stop=True)
                    last.then_inc(s5_pe.sem, 1)

                batch_inputs(0, 0)
                apart(pe)
                with pe.Fori(0, 3) as i:
                    for b in range(2):
                        batch_inputs(b + 1, i)
                        batch_outputs(b, i)
                batch_inputs(1, 3)
                batch_outputs(0, 3)
                batch_outputs(1, 3)
                wait(pe, y_gelu, l, 8)
                for q in range(4):
                    for s in range(2):
                        for jj in range(4):
                            last = pe.transpose(ps[:, 2 * q + s, jj * P:(jj + 1) * P],
                                                yc[:, 4 * s + jj, q * P:(q + 1) * P], ident[:, :])
                        last.then_inc(yt_mm.sem, 1)
                wait(pe, y_ready, l, 4)
                for a in range(2):
                    unit_ready(pe, l, U_GLU + a)
                    for nn in range(2):
                        end = tile_products(pe, a, 4 * a + 2 * nn, y_hi, y_lo, [(k, k) for k in range(4)],
                                            n_cols=2 * P, col=nn * P)
                        end[1].then_inc((glu_mm, unit_used)[nn].sem, 1)
                wait(pe, yg_ready, l, 4)
                apart(pe)
                with pe.Fori(0, 4) as i:
                    for j in range(2):
                        unit_ready(pe, l, U_MERGE + j, i)
                        pe.wait_ge(mg_free.sem, mg_free.at(l, j - 1) + 2 * i)
                        tile_products(pe, j, 4 * j, yg_hi, yg_lo, [(k, k) for k in range(4)])
                        end = tile_products(pe, j, 4 * j + 2, o_hi, o_lo, [(4 + k, k) for k in range(4)])
                        end[1].then_inc(unit_used.sem, 1)
                wait(pe, mg_ready, l, KT)
                apart(pe)
                with pe.Fori(0, 2) as i:
                    for j in range(4):
                        unit_ready(pe, l, U_OUT + j, 2 * i)
                        pe.wait_ge(wo_ev.sem, wo_ev.at(l, j - 1) + 4 * i)
                        end = tile_products(pe, j % 2, 2 * (j % 2), mg_hi, mg_lo, [(k, k) for k in range(KT)])
                        end[1].then_inc(unit_used.sem, 1)
                    pe.wait_ge(ada_used.sem, ada_used.at(l, 5 * KT) + KT * i)
                    pe.wait_ge(mod_ready.sem, mod_ready.at(l, 4) + i)
                    mod_products()
                norm(l, 1)

                def up_products(cc, n, q, c_static, c_reg):
                    for a in range(2):
                        for w_i in range(2):
                            b = 4 * a + 2 * w_i
                            u = n + 2 * a + w_i
                            unit_ready(pe, l, u, q)
                            if c_reg is not None:
                                if a == 0:
                                    pe.wait_ge(up_done.sem, up_done.at(l, 2 * c_static - 1) + c_reg * 2)
                                    pe.wait_ge(dn_ev.sem, dn_ev.at(l, 8 * (c_static - 2) + 7 + w_i) + c_reg * 8)
                                else:
                                    pe.wait_ge(up_done.sem, up_done.at(l, 2 * c_static) + c_reg * 2)
                            end = tile_products(pe, u % 2, b, h_hi, h_lo, [(k, k) for k in range(KT)])
                            end[1].then_inc(unit_used.sem, 1)

                def down_products(buf, n, q, c_static, c_reg, last_chunk):
                    pe.wait_ge(hid_ready.sem, hid_ready.at(l, 2 * c_static + 2) + c_reg * 2)
                    for d in range(2):
                        unit_ready(pe, l, n + d, q)
                        for nn in range(4):
                            t = 4 * d + nn
                            b = 2 * (t % 2)
                            if t < 2:
                                pe.wait_ge(up_done.sem, up_done.at(l, 2 * c_static + (2 if last_chunk else 3)) + c_reg * 2)
                                pe.wait_ge(dn_ev.sem, dn_ev.at(l, 8 * (c_static - 1) + 7 + t) + c_reg * 8)
                            else:
                                pe.wait_ge(dn_ev.sem, dn_ev.at(l, 8 * c_static + t - 1) + c_reg * 8)
                            s = (n + d) % 2
                            xs_h, xs_l = hid_hi[:, buf], hid_lo[:, buf]
                            for k in range(2):
                                col = k * 4 * P + nn * P
                                end = products(pe, [ps[:, b, :], ps[:, b + 1, :]], whi[:, s, col:col + P],
                                               wlo[:, s, col:col + P], halves(xs_h, xs_l, k), k == 0, k == 1)
                            end[1].then_inc((dn_mm if nn < 3 else unit_used).sem, 1)

                wait(pe, h_ready, l, 2 * KT)
                wait(pe, rb_ready, l, 2)
                wait(pe, mod_ready, l, 6)
                up_products(0, U_FFN, 0, 0, None)
                apart(pe)
                with pe.Fori(0, (CHUNKS - 1) // 2) as i:
                    for cc in range(2):
                        n = U_FFN + 4 + 6 * cc
                        up_products(1 - cc, n, 6 * i, 1 + cc, i * 2)
                        down_products(cc, n + 4, 6 * i, cc, i * 2, False)
                down_products(0, UNITS - 2, 0, CHUNKS - 1, 0, True)

            norm(DEPTH, 0)
            for t in range(TT):
                if t == 0:
                    pe.wait_ge(fin_t.sem, KT)
                if t >= 2:
                    pe.wait_ge(fin_ev.sem, t - 1)
                b = 2 * (t % 2)
                for k in range(KT):
                    last = pe.transpose(ps[:, b + k // 4, (k % 4) * P:(k % 4 + 1) * P], fin[:, k, t * P:(t + 1) * P],
                                        ident[:, :])
                last.then_inc(fin_mm.sem, 1)

        @block.scalar
        def _(act):
            def copy(dst, src):
                return act.activation(dst, src, ACT.Copy)

            act.wait_ge(dve_const.sem, DVE_CONSTS + 1)
            act.activation(c_act[:, :], cols[:, 0, ROW_C:ROW_C + KT], ACT.Silu).then_inc(act_const.sem, 1)
            for k in range(0, KT, 2):
                act.wait_ge(xt_mm.sem, k + 1)
                copy(x_sb[:, k, :], pair(2)).then_inc(xt_act.sem, 1)
            act.wait_ge(angles_ready.sem, 1)
            act.activation(sin_t[:, :], ang[:, :], ACT.Sin).then_inc(act_const.sem, 1)
            act.activation(ang_k[:, :], half[:, :], ACT.Sin).then_inc(act_const.sem, 1)

            def norm(l, occ, shift):
                for k in range(KT):
                    if k < 2:
                        wait(act, h_ready, l, KT * occ)
                    else:
                        wait(act, sq_used, l, KT * occ + k - 1)
                    if occ:
                        wait(act, wo_ev, l, k + 1)
                    else:
                        wait(act, dn_ev, l, 0)
                    act.activation(t_ring[:, k % 2, :], x_sb[:, k, :], ACT.Square).then_inc(sq_ready.sem, 1)
                wait(act, sq_used, l, KT * (occ + 1))
                act.activation(std[:, 0, :], ps[:, 6, 0:TT], ACT.Sqrt, bias=eps_col[:, :]).then_inc(std_ready.sem, 1)
                wait(act, rb_mm, l, occ + 1)
                copy(rb[:, :], pair(4)).then_inc(rb_ready.sem, 1)
                if shift is not None:
                    for k in range(KT):
                        wait(act, t_ready, l, KT * occ + k + 1)
                        act.activation(h_hi[:, k, :], t_ring[:, k % 2, :], ACT.Identity,
                                       bias=mod[:, shift, k:k + 1]).then_inc(h_hi_done.sem, 1)

            with act.Fori(0, DEPTH) as l:
                split_hi(act, l, 0)
                split_hi(act, l, 1)
                act.wait_ge(xt_act.sem, KT // 2)
                act.wait_ge(xt_dve.sem, KT // 2)
                wait(act, dn_ev, l, 0)
                act.dma_start(xs_dram, x_sb[:, :, :]).then_inc(x_spilled.sem, 16)
                norm(l, 0, 0)
                for n in range(3):
                    split_hi(act, l, n + 2)
                wait(act, x_spilled, l, 16)
                for j in range(4):
                    wait(act, u_mm, l, j + 1)
                    copy(uc[:, :, j, :], ps[:, j, :].rearrange("p (g m) -> p g m", m=M)).then_inc(z_act.sem, 1)
                split_hi(act, l, 5)
                wait(act, z_act, l, 4)
                wait(act, u_ev_dve, l, 4)
                act.dma_start(u_dram, uc[:, :, :, :]).then_inc(u_spilled.sem, 16)
                apart(act)
                with act.Fori(0, 4) as i:
                    for j in range(4):
                        split_hi(act, l, U_GATE + j + 2, 2 * i)
                        act.wait_ge(unit_used.sem, unit_used.at(l, U_GATE + j + 1) + 4 * i)
                        act.wait_ge(gst_spilled[j % 2].sem, gst_spilled[j % 2].at(l, 16 * (j // 2)) + 32 * i)
                        act.activation(gst[:, j % 2, :], pair(2 * (j % 2)), ACT.Sigmoid).then_inc(z_act.sem, 1)
                        act.wait_ge(z_act.sem, z_act.at(l, 5 + j) + 4 * i)
                        act.dma_start(gate_dram[bass.ds(4 * i + j, 1)].rearrange("o p n -> (o p) n"), gst[:, j % 2, :])\
                            .then_inc(gst_spilled[j % 2].sem, 16)
                wait(act, u_spilled, l, 16)
                for a in range(3):
                    split_hi(act, l, U_CQ + a + 2, 0, (PLAIN, KR, HEAD)[a])
                    wait(act, unit_used, l, U_CQ + a + 1)
                    copy(lat[:, a, :], pair(2 * a))
                    act.activation(lat_sq[:, a, :], pair(2 * a), ACT.Square,
                                   scale=math.sqrt(D / (Q_LORA, Q_LORA, KV_LORA)[a])).then_inc(lat_sq_ready.sem, 1)
                split_hi(act, l, U_HEAD + 1, 0, HEAD)
                for side in range(2):
                    wait(act, lat_ss, l, side + 1)
                    last = act.activation(std[:, side, :], ps[:, 2 * side, 0:TT], ACT.Sqrt, bias=eps_col[:, :])
                last.then_inc(lat_std.sem, 1)
                for side in range(2):
                    wait(act, lat_rb_mm, l, side + 1)
                    copy(lat_rb[:, side, :], pair(2 * side)).then_inc(lat_rb_ready.sem, 1)
                for a in range(3):
                    wait(act, lat_t, l, a + 1)
                    copy(latn_hi[:, a, :], lat[:, a, :]).then_inc(lat_hi_done.sem, 1)
                wait(act, kr_done, l, 3)
                for head in range(2):
                    copy(k_hi[64:P, head, :], kr_t[64:P, 0, :]).then_inc(kr_hi_done.sem, 1)

                def even_queries_and_keys(i, ahead):
                    act.wait_ge(q_rot.sem, q_rot.at(l, 2 * ahead + 1) + 2 * i)
                    copy(q_hi[:, 0, :], q_f[:, :]).then_inc(q_hi_done.sem, 1)
                    act.wait_ge(k_mm.sem, k_mm.at(l, ahead + 1) + i)
                    for head in range(2):
                        copy(k_hi[0:64, head, :], pair(2, 64 * head, 64 * head + 64)).then_inc(k_hi_done.sem, 1)

                def attention_pair(i, last_pair):
                    def head_output(m):
                        rows = slice(64 * (m // 2), 64 * (m // 2) + 64)
                        cols_ = slice((m % 2) * HALF, (m % 2 + 1) * HALF)
                        act.wait_ge(pv_mm.sem, pv_mm.at(l, 2 * (m + 1)) + 8 * i)
                        copy(o_hi[rows, bass.ds(i, 1), cols_].rearrange("p o n -> p (o n)"), ps[rows, 6 + m % 2, :])\
                            .then_inc(o_hi_done.sem, 1)

                    for g in range(18):
                        if g >= 2:
                            tile = g - 2
                            if tile >= 4 and tile % 2 == 0:
                                act.wait_ge(pv_mm.sem, pv_mm.at(l, tile // 2 - 1) + 8 * i)
                            for t in range(2):
                                act.wait_ge(pt_mm.sem, pt_mm.at(l, 2 * tile + t + 1) + 32 * i)
                                copy(pt_hi[:, tile // 2 % 2, 4 * t:4 * t + 4, (tile % 2) * P:(tile % 2 + 1) * P],
                                     ps[:, 4 + t, :].rearrange("p (k n) -> p k n", k=4)).then_inc(pt_hi_done.sem, 1)
                        if 1 <= g <= 16:
                            r = g - 1
                            act.wait_ge(p_inv.sem, p_inv.at(l, r + 1) + 16 * i)
                            act.activation(probs[:, r % 3, :], probs[:, r % 3, :], ACT.Copy,
                                           scale=row_inv[:, r % 2:r % 2 + 1]).then_inc(p_ready.sem, 1)
                        if g < 16:
                            act.wait_ge(s_max.sem, s_max.at(l, g + 1) + 16 * i)
                            if g >= 3:
                                act.wait_ge(pt_mm.sem, pt_mm.at(l, 2 * (g - 2)) + 32 * i)
                            act.activation(probs[:, g % 3, :], pair(2 * (g % 2)), ACT.Exp, bias=neg_max[:, g % 2:g % 2 + 1],
                                           scale=-1.0, accum_out=row_sum[:, g % 2:g % 2 + 1]).then_inc(p_exp.sem, 1)
                        if g == 0:
                            for t in range(2):
                                act.wait_ge(v_mm.sem, v_mm.at(l, t + 1) + 2 * i)
                                copy(v_hi[:, 4 * t:4 * t + 4, :], ps[:, 4 + t, :].rearrange("p (k n) -> p k n", k=4))\
                                    .then_inc(v_hi_done.sem, 1)
                        if g == 2:
                            act.wait_ge(q_rot.sem, q_rot.at(l, 2) + 2 * i)
                            copy(q_hi[:, 1, :], q_f[:, :]).then_inc(q_hi_done.sem, 1)
                        if g in (1, 4):
                            if last_pair:
                                split_hi(act, l, U_GLU + g // 4)
                            else:
                                split_hi(act, l, U_HEAD + 2 + g // 4, i, HEAD)
                        if g >= 8 and g % 4 == 0:
                            head_output((g - 8) // 4)
                    if not last_pair:
                        even_queries_and_keys(i, 1)
                    head_output(3)

                even_queries_and_keys(0, 0)
                apart(act)
                with act.Fori(0, PAIRS - 1) as i:
                    attention_pair(i, False)
                attention_pair(PAIRS - 1, True)

                wait(act, s5_loaded, l, 16 * 14)
                wait(act, s5_pe, l, 1)
                act.activation(sm[:, S_DT, :], ldt[:, :], ACT.Exp).then_inc(s5_act.sem, 1)
                wait(act, s5_dve, l, S5_EXP_READY)
                act.activation(sm[:, S_MAG:S_MAG + 2, :], sm[:, S_AD:S_AD + 2, :], ACT.Exp).then_inc(s5_act.sem, 1)
                wait(act, s5_dve, l, S5_ANGLES_READY)
                act.activation(trig[:, :, :], sm[:, 0:6, :], ACT.Sin).then_inc(s5_act.sem, 1)
                def batch_inputs(b, i):
                    for s, (dst, bank) in enumerate(((mt_1, 0), (mt_2, 1), (ut, 3))):
                        act.wait_ge(s5_tr.sem, s5_tr.at(l, 3 * b + s + 1) + 6 * i)
                        copy(dst[:, b % 2, :, :], ps[:, bank, :].rearrange("p (g n) -> p g n", g=4))\
                            .then_inc(s5_tr_ev.sem, 1)

                def batch_outputs(b, i):
                    act.wait_ge(s5_pe.sem, s5_pe.at(l, b + 2) + 2 * i)
                    act.activation(yc[:, :, bass.ds((2 * i + b) * 4 * M, 4 * M)].rearrange("p j (g m) -> p j g m", m=M),
                                   ps[:, 6 + b % 2, :].rearrange("p (g j m) -> p j g m", g=4, m=M),
                                   ACT.Gelu_apprx_tanh).then_inc(y_gelu.sem, 1)

                batch_inputs(0, 0)
                apart(act)
                with act.Fori(0, 3) as i:
                    for b in range(2):
                        batch_inputs(b + 1, i)
                        batch_outputs(b, i)
                batch_inputs(1, 3)
                batch_outputs(0, 3)
                batch_outputs(1, 3)
                for q in range(4):
                    for s in range(2):
                        wait(act, yt_mm, l, 2 * q + s + 1)
                        copy(yt[:, q, :].rearrange("p (c j) -> p j c", j=CH)[:, 4 * s:4 * s + 4, :],
                             ps[:, 2 * q + s, :].rearrange("p (j c) -> p j c", j=4)).then_inc(yt_ev.sem, 1)
                for q in range(4):
                    wait(act, yt_ev, l, 2 * q + 2)
                    copy(y_hi[:, q, :], yt[:, q, :]).then_inc(y_hi_done.sem, 1)
                def glu_hi(n):
                    wait(act, glu_mul, l, n + 1)
                    copy(yg_hi[:, n, :], glu_s[:, n % 2, :]).then_inc(yg_hi_done.sem, 1)

                for n in range(4):
                    if n % 2:
                        if n == 1:
                            split_hi(act, l, U_MERGE)
                        wait(act, unit_used, l, U_GLU + n // 2 + 1)
                    else:
                        wait(act, glu_mm, l, n // 2 + 1)
                    if n >= 2:
                        wait(act, yg_ready, l, n - 1)
                    act.activation(glu_s[:, n % 2, :], pair(2 * n), ACT.Sigmoid,
                                   bias=pcol[:, ROW_BGLU + n:ROW_BGLU + n + 1]).then_inc(glu_sig.sem, 1)
                    if n:
                        glu_hi(n - 1)
                glu_hi(3)
                split_hi(act, l, U_MERGE + 1)
                apart(act)
                with act.Fori(0, 4) as i:
                    for j in range(2):
                        split_hi(act, l, U_MERGE + j + 2, i)
                        act.wait_ge(mg_step.sem, mg_step.at(l, 2 * j + 2) + 4 * i)
                        copy(mg_hi[:, bass.ds(2 * i + j, 1), :].rearrange("p o n -> p (o n)"), m_sum[:, :])\
                            .then_inc(mg_hi_done.sem, 1)
                wait(act, unit_used, l, U_OUT)
                wait(act, x_spilled, l, 16)
                act.dma_start(x_sb[:, :, :], xs_dram).then_inc(x_back.sem, 16)
                apart(act)
                with act.Fori(0, 2) as i:
                    for j in range(4):
                        split_hi(act, l, U_OUT + j + 2, 2 * i)
                norm(l, 1, 3)

                def up_part(n, q, c_static, c_reg, buf):
                    for a in range(2):
                        split_hi(act, l, n + 2 * a + 2, q)
                        act.wait_ge(unit_used.sem, unit_used.at(l, n + 2 * a + 1) + 2 * q)
                        act.wait_ge(hid_ready.sem, hid_ready.at(l, max(2 * (c_static - 1) + a + 1, 0)) + 2 * c_reg)
                        act.activation(silu[:, a, :], pair(4 * a), ACT.Silu).then_inc(silu_done.sem, 1)
                        split_hi(act, l, n + 2 * a + 3, q)
                        act.wait_ge(up_done.sem, up_done.at(l, 2 * c_static + a + 1) + 2 * c_reg)
                        copy(hid_hi[:, buf, a, :], silu[:, a, :]).then_inc(hid_hi_done.sem, 1)

                up_part(U_FFN, 0, 0, 0, 0)
                apart(act)
                with act.Fori(0, (CHUNKS - 1) // 2) as i:
                    for cc in range(2):
                        n = U_FFN + 4 + 6 * cc
                        up_part(n, 6 * i, 1 + cc, 2 * i, 1 - cc)
                        for d in range(2):
                            split_hi(act, l, n + 6 + d, 6 * i)

            norm(DEPTH, 0, None)
            for t in range(TT):
                act.wait_ge(fin_mm.sem, t + 1)
                if t >= 2:
                    act.wait_ge(out_done[t % 2].sem, 16 * (t // 2))
                copy(o_row[:, t % 2, :], pair(2 * (t % 2))).then_inc(fin_ev.sem, 1)

        @block.vector
        def _(dve):
            def lo_of(out, value, hi):
                return dve.tensor_tensor(out, value, hi.bitcast(F32), ALU.subtract)

            dve.memset(ones_col[:, :], 1.0).then_inc(dve_const.sem, 1)
            dve.memset(mean_col[:, :], 1.0 / D).then_inc(dve_const.sem, 1)
            dve.memset(eps_col[:, :], EPS).then_inc(dve_const.sem, 1)
            for rows, v in ((slice(0, 64), -1.0), (slice(64, P), 1.0)):
                dve.memset(sgn[rows, :], v).then_inc(dve_const.sem, 1)
                dve.memset(nsgn[rows, :], -v).then_inc(dve_const.sem, 1)
            for counter, n in credits:
                dve.sem_inc(counter.sem, n)
            dve.wait_ge(cols_mm.sem, 1)
            dve.tensor_copy(cols[:, :, :], ps[:, 0, 0:DEPTH * P].rearrange("p (d r) -> p d r", d=DEPTH)[:, :, 0:ROWS])\
                .then_inc(dve_const.sem, 1)

            def ada_product(l, n, k, at_q=0):
                s = k % 2
                dve.wait_ge(ada_loaded[s].sem, ada_loaded[s].at(l, 16 * (n // 2 + 1)) + 8 * at_q)
                dve.wait_ge(ada_used.sem, ada_used.at(l, n) + at_q)
                if k == 0:
                    last = dve.tensor_scalar(ada_acc[:, :], ada_raw[:, s, :], c_act[:, 0:1], None, ALU.mult)
                else:
                    last = dve.scalar_tensor_tensor(ada_acc[:, :], ada_raw[:, s, :], c_act[:, k:k + 1], ada_acc[:, :],
                                                    ALU.mult, ALU.add)
                last.then_inc(ada_used.sem, 1)

            def modulation(l, n, at_q, dst, bias):
                dve.wait_ge(mod_mm.sem, mod_mm.at(l, n + 1) + at_q)
                apart(dve)
                dve.tensor_tensor(dst, ps[:, 7, 0:KT], bias, ALU.add).then_inc(mod_ready.sem, 1)

            dve.wait_ge(pool_const.sem, 2)
            dve.wait_ge(act_const.sem, 1)
            dve.wait_ge(dve_const.sem, DVE_CONSTS + 1)
            for m in range(2):
                for k in range(KT):
                    ada_product(-1, 4 * KT + m * KT + k, k)
                    if m == 0 and k % 2:
                        dve.wait_ge(xt_mm.sem, k + 1)
                        dve.tensor_copy(x_sb[:, k, :], pair(4)).then_inc(xt_dve.sem, 1)
                modulation(-1, 4 + m, 0, mod[:, m, :], cols[:, 0, ROW_B_ADA + m * KT:ROW_B_ADA + (m + 1) * KT])
            dve.wait_ge(mod_ready.sem, 2)
            dve.scalar_tensor_tensor(a1[:, :], mod[:, 1, :], 1.0, cols[:, 0, ROW_N1:ROW_N1 + KT], ALU.add, ALU.mult)\
                .then_inc(a1_ready.sem, 1)

            dve.wait_ge(const_loaded.sem, 16 * CONSTS)
            steps = [DVE_CONSTS + 1]

            def link(inst):
                inst.then_inc(dve_const.sem, 1)
                steps[0] += 1
                dve.wait_ge(dve_const.sem, steps[0])

            def reduce_angle(counted, src, tmp, dst):
                counted(dve.tensor_scalar(tmp, src, 1.0 / (2 * math.pi), ROUND, ALU.mult, ALU.add))
                counted(dve.tensor_scalar(tmp, tmp, ROUND, None, ALU.subtract))
                for part in TWO_PI_PARTS:
                    counted(dve.scalar_tensor_tensor(dst, tmp, -part, src, ALU.mult, ALU.add))
                    src = dst
                counted(dve.tensor_scalar(dst, dst, MAX_ANGLE, -MAX_ANGLE, ALU.min, ALU.max))

            link(dve.tensor_copy(pos_f[:, :], pos_i[:, :]))
            link(dve.tensor_scalar(ang[:, :], pos_f[:, :], rope_sb[:, 0:1], None, ALU.mult))
            reduce_angle(link, ang[:, :], ang_k[:, :], ang[:, :])
            link(dve.tensor_scalar(half[:, :], ang[:, :], 0.5, None, ALU.mult))
            dve.sem_inc(angles_ready.sem, 1)
            link(dve.tensor_scalar(pos_i2[:, :], pos_i[:, :], 16, None, ALU.arith_shift_right))
            link(dve.tensor_copy(pos_f[:, :], pos_i2[:, :]))
            link(dve.tensor_scalar(pos_i2[:, :], pos_i[:, :], 65535, None, ALU.bitwise_and))
            link(dve.tensor_copy(pos_lo[:, :], pos_i2[:, :]))
            link(dve.tensor_scalar(posq_i2[:, :], posq_i[:, :], 16, None, ALU.arith_shift_right))
            link(dve.tensor_copy(posq_f[:, 0, :], posq_i2[:, :]))
            link(dve.tensor_scalar(posq_i2[:, :], posq_i[:, :], 65535, None, ALU.bitwise_and))
            link(dve.tensor_copy(posq_f[:, 1, :], posq_i2[:, :]))
            for t in range(TT):
                link(dve.tensor_scalar(mask_t[:, :], pos_f[:, :], posq_f[:, 0, t:t + 1], 65536.0, ALU.subtract, ALU.mult))
                link(dve.scalar_tensor_tensor(mask_t[:, :], pos_lo[:, :], posq_f[:, 1, t:t + 1], mask_t[:, :],
                                              ALU.subtract, ALU.add))
                link(dve.tensor_scalar(mask[:, t, :], mask_t[:, :], 0.0, MASKED, ALU.is_gt, ALU.mult))
            dve.wait_ge(act_const.sem, 3)
            link(dve.tensor_tensor(ang_k[:, :], ang_k[:, :], ang_k[:, :], ALU.mult))
            link(dve.tensor_scalar(ang_k[:, :], ang_k[:, :], -2.0, 1.0, ALU.mult, ALU.add))
            link(dve.tensor_scalar(tq[:, :], ang_k[:, :], rope_sb[:, 1:2], rope_sb[:, 3:4], ALU.mult, ALU.add))
            link(dve.scalar_tensor_tensor(tq[:, :], sin_t[:, :], rope_sb[:, 2:3], tq[:, :], ALU.mult, ALU.add))
            link(dve.tensor_scalar(tk[:, :], ang_k[:, :], rope_sb[:, 4:5], None, ALU.mult))
            link(dve.scalar_tensor_tensor(tk[:, :], sin_t[:, :], rope_sb[:, 5:6], tk[:, :], ALU.mult, ALU.add))

            def norm(l, occ, gain):
                wait(dve, std_ready, l, occ + 1)
                dve.reciprocal(rstd[:, 0, :], std[:, 0, :]).then_inc(rstd_ready.sem, 1)
                wait(dve, rb_ready, l, occ + 1)

                def scaled(k):
                    if k >= 2:
                        wait(dve, h_ready, l, KT * occ + k - 1)
                    dve.scalar_tensor_tensor(t_ring[:, k % 2, :], x_sb[:, k, :], gain[:, k:k + 1], rb[:, :],
                                             ALU.mult, ALU.mult).then_inc(t_ready.sem, 1)

                scaled(0)
                for k in range(KT):
                    if k + 1 < KT:
                        scaled(k + 1)
                    wait(dve, h_hi_done, l, KT * occ + k + 1)
                    dve.scalar_tensor_tensor(h_lo[:, k, :], t_ring[:, k % 2, :], mod[:, 3 * occ, k:k + 1],
                                             h_hi[:, k, :].bitcast(F32), ALU.add, ALU.subtract).then_inc(h_ready.sem, 1)

            with dve.Fori(0, DEPTH) as l:
                dve.tensor_copy(pcol[:, :], cols[:, bass.ds(l, 1), :].rearrange("p o r -> p (o r)")).then_inc(pcol_ready.sem, 1)
                wait(dve, a1_ready, l, 0)
                wait(dve, pcol_ready, l, 1)
                norm(l, 0, a1)
                wait(dve, x_spilled, l, 16)
                for j in range(4, CH):
                    if j < CH - 1:
                        wait(dve, u_mm, l, j + 1)
                    else:
                        wait(dve, unit_used, l, U_GATE)
                    dve.tensor_copy(uc[:, :, j, :], ps[:, j, :].rearrange("p (g m) -> p g m", m=M)).then_inc(u_ev_dve.sem, 1)
                apart(dve)
                with dve.Fori(0, 4) as i:
                    for k in range(KT):
                        ada_product(l, k, k, KT * i)
                    modulation(l, 0, i, mod[:, bass.ds(i + 2, 1), :].rearrange("p o k -> p (o k)"),
                               pcol[:, bass.ds((i + 2) * KT, KT)])
                wait(dve, mod_ready, l, 4)
                dve.scalar_tensor_tensor(a2[:, :], mod[:, 4, :], 1.0, pcol[:, ROW_N2:ROW_N2 + KT], ALU.add, ALU.mult)\
                    .then_inc(a2_ready.sem, 1)
                wait(dve, lat_std, l, 1)
                dve.reciprocal(rstd[:, :, :], std[:, :, :]).then_inc(lat_rstd.sem, 1)
                for a in range(3):
                    wait(dve, lat_rb_ready, l, a // 2 + 1)
                    dve.scalar_tensor_tensor(lat[:, a, :], lat[:, a, :], pcol[:, ROW_QN + a:ROW_QN + a + 1],
                                             lat_rb[:, a // 2, :], ALU.mult, ALU.mult).then_inc(lat_t.sem, 1)
                for s in range(2):
                    wait(dve, gst_spilled[s], l, 16 * KT)
                for a in range(3):
                    wait(dve, lat_hi_done, l, a + 1)
                    lo_of(latn_lo[:, a, :], lat[:, a, :], latn_hi[:, a, :]).then_inc(lat_ready.sem, 1)
                wait(dve, unit_used, l, U_KR + 1)
                dve.tensor_tensor(kr_t[64:P, 0, :], pair(6, 0, 64), tk[0:64, :], ALU.mult).then_inc(kr_done.sem, 1)
                dve.tensor_tensor(kr_t[64:P, 1, :], pair(6, 64, P), tk[64:P, :], ALU.mult).then_inc(kr_done.sem, 1)
                wait(dve, kr_done, l, 2)
                dve.tensor_tensor(kr_t[64:P, 0, :], kr_t[64:P, 0, :], kr_t[64:P, 1, :], ALU.add).then_inc(kr_done.sem, 1)
                for head in range(2):
                    wait(dve, kr_hi_done, l, head + 1)
                    lo_of(k_lo[64:P, head, :], kr_t[64:P, 0, :], k_hi[64:P, head, :]).then_inc(kr_ready.sem, 1)

                def queries(i, head, ahead=0):
                    dve.wait_ge(q_mm.sem, q_mm.at(l, 2 * ahead + head + 1) + 2 * i)
                    dve.tensor_tensor(q_f[:, :], pair(6 * head), tq[:, :], ALU.mult).then_inc(q_rot.sem, 1)

                def queries_lo(i, head, ahead=0):
                    dve.wait_ge(q_hi_done.sem, q_hi_done.at(l, 2 * ahead + head + 1) + 2 * i)
                    lo_of(q_lo[:, head, :], q_f[:, :], q_hi[:, head, :]).then_inc(q_ready.sem, 1)

                def keys_lo(i, ahead=0):
                    for head in range(2):
                        dve.wait_ge(k_hi_done.sem, k_hi_done.at(l, 2 * ahead + head + 1) + 2 * i)
                        lo_of(k_lo[0:64, head, :], pair(2, 64 * head, 64 * head + 64), k_hi[0:64, head, :])\
                            .then_inc(k_ready.sem, 1)

                def attention_pair(i, last_pair):
                    def head_output(m):
                        rows = slice(64 * (m // 2), 64 * (m // 2) + 64)
                        cols_ = slice((m % 2) * HALF, (m % 2 + 1) * HALF)
                        dve.wait_ge(o_hi_done.sem, o_hi_done.at(l, m + 1) + 4 * i)
                        lo_of(o_lo[rows, bass.ds(i, 1), cols_].rearrange("p o n -> p (o n)"), ps[rows, 6 + m % 2, :],
                              o_hi[rows, bass.ds(i, 1), cols_].rearrange("p o n -> p (o n)")).then_inc(o_ready.sem, 1)

                    for g in range(18):
                        if 1 <= g <= 16:
                            r = g - 1
                            dve.wait_ge(p_exp.sem, p_exp.at(l, r + 1) + 16 * i)
                            if r >= 2:
                                dve.wait_ge(p_ready.sem, p_ready.at(l, r - 1) + 16 * i)
                            dve.reciprocal(row_inv[:, r % 2:r % 2 + 1], row_sum[:, r % 2:r % 2 + 1]).then_inc(p_inv.sem, 1)
                        if g >= 2:
                            tile = g - 2
                            for t in range(2):
                                dve.wait_ge(pt_hi_done.sem, pt_hi_done.at(l, 2 * tile + t + 1) + 32 * i)
                                at = (slice(None), tile // 2 % 2, slice(4 * t, 4 * t + 4), slice((tile % 2) * P, (tile % 2 + 1) * P))
                                lo_of(pt_lo[at], ps[:, 4 + t, :].rearrange("p (k n) -> p k n", k=4), pt_hi[at])\
                                    .then_inc(pt_ready.sem, 1)
                        if g < 16:
                            dve.wait_ge(s_mm.sem, s_mm.at(l, g + 1) + 16 * i)
                            apart(dve)
                            s = pair(2 * (g % 2))
                            dve.tensor_tensor_reduce(out=s, in0=s, in1=mask[:, g % TT, :], scale=1.0, scalar=3e38,
                                                     op0=ALU.add, op1=ALU.min, accum_out=neg_max[:, g % 2:g % 2 + 1])\
                                .then_inc(s_max.sem, 1)
                        if g == 0:
                            for t in range(2):
                                dve.wait_ge(v_hi_done.sem, v_hi_done.at(l, t + 1) + 2 * i)
                                lo_of(v_lo[:, 4 * t:4 * t + 4, :], ps[:, 4 + t, :].rearrange("p (k n) -> p k n", k=4),
                                      v_hi[:, 4 * t:4 * t + 4, :]).then_inc(v_ready.sem, 1)
                        if g == 2:
                            queries(i, 1)
                            queries_lo(i, 1)
                        if g == 17 and not last_pair:
                            queries(i, 0, 1)
                        if g >= 8 and g % 4 == 0:
                            head_output((g - 8) // 4)
                    if not last_pair:
                        queries_lo(i, 0, 1)
                        keys_lo(i, 1)
                    head_output(3)

                queries(0, 0)
                queries_lo(0, 0)
                keys_lo(0)
                apart(dve)
                with dve.Fori(0, PAIRS - 1) as i:
                    attention_pair(i, False)
                attention_pair(PAIRS - 1, True)

                n_s5 = [0]

                def s5(inst, linked=True):
                    inst.then_inc(s5_dve.sem, 1)
                    n_s5[0] += 1
                    if linked:
                        wait(dve, s5_dve, l, n_s5[0])

                wait(dve, s5_loaded, l, 16 * 14)
                wait(dve, s5_pe, l, 1)
                s5(dve.tensor_copy(a_t[:, :, :], ps[:, 0, 0:2 * G].rearrange("p (i g) -> p i g", i=2)), False)
                s5(dve.tensor_copy(d_t[:, :], ps[:, 0, 2 * G:3 * G]), False)
                s5(dve.tensor_copy(c_st[:, :, :], ps[:, 1, :].rearrange("p (g m) -> p g m", m=M)), False)
                s5(dve.tensor_copy(c_sw[:, :, :], ps[:, 2, :].rearrange("p (g m) -> p g m", m=M)))
                ar, ai = a_t[:, 0, :], a_t[:, 1, :]
                v = [sm[:, t, :] for t in range(S_SCI + 1)]
                wait(dve, s5_act, l, 1)
                s5(dve.tensor_tensor(v[S_AD], ar, v[S_DT], ALU.mult))
                s5(dve.tensor_scalar(v[S_AD8], v[S_AD], float(CH), None, ALU.mult))
                assert n_s5[0] == S5_EXP_READY
                s5(dve.tensor_tensor(v[0], ai, v[S_DT], ALU.mult))
                for a, factor in ((0, None), (2, float(CH)), (4, 16.0)):
                    if factor:
                        s5(dve.tensor_scalar(v[a], v[a - 2], factor, None, ALU.mult))
                    reduce_angle(s5, v[a], v[S_K], v[a])
                    s5(dve.tensor_scalar(v[a + 1], v[a], 0.5, None, ALU.mult))
                assert n_s5[0] == S5_ANGLES_READY
                s5(dve.tensor_scalar(c_n[:, :, :], c_st[:, :, :], nsgn[:, :], None, ALU.mult), False)
                wait(dve, s5_act, l, 3)
                cosines = trig[:, 1::2, :]
                s5(dve.tensor_tensor(cosines, cosines, cosines, ALU.mult))
                s5(dve.tensor_scalar(cosines, cosines, -2.0, 1.0, ALU.mult, ALU.add))
                pw_re, pw_im = pw[:, 0, :, :], pw[:, 1, :, :]
                s5(dve.memset(pw[:, 0, :, 0:1], 1.0), False)
                s5(dve.memset(pw[:, 1, :, 0:1], 0.0), False)
                s5(dve.tensor_tensor(pw_re[:, :, 1], v[S_MAG], trig[:, 1, :], ALU.mult), False)
                s5(dve.tensor_tensor(pw_im[:, :, 1], v[S_MAG], trig[:, 0, :], ALU.mult), False)
                for a, rot in ((2, rot1), (4, rot16)):
                    s5(dve.memset(rot[:, 0, :, 0:1], 1.0), False)
                    s5(dve.memset(rot[:, 1, :, 0:1], 0.0), False)
                    s5(dve.tensor_copy(rot[:, 0, :, 1], trig[:, a + 1, :]), False)
                    s5(dve.tensor_copy(rot[:, 1, :, 1], trig[:, a, :]))
                tmp = [z_tmp[:, t, :, :].rearrange("p g n -> p (g n)").rearrange("p (g n) -> p g n", g=G) for t in range(3)]

                def doubling(re, im, top):
                    m = 1
                    while m < top:
                        n = min(m, top - m)
                        one, nxt = slice(1, n + 1), slice(m + 1, m + n + 1)
                        fr, fi = (x_[:, :, m:m + 1].broadcast_to([P, G, n]) for x_ in (re, im))
                        for dst, x_a, x_b, op in ((re, re, im, ALU.subtract), (im, im, re, ALU.add)):
                            s5(dve.tensor_tensor(tmp[0][:, :, 0:n], x_a[:, :, one], fr, ALU.mult), False)
                            s5(dve.tensor_tensor(tmp[1][:, :, 0:n], x_b[:, :, one], fi, ALU.mult))
                            s5(dve.tensor_tensor(dst[:, :, nxt], tmp[0][:, :, 0:n], tmp[1][:, :, 0:n], op))
                        m += n

                doubling(pw_re, pw_im, CH)
                doubling(rot1[:, 0], rot1[:, 1], 15)
                doubling(rot16[:, 0], rot16[:, 1], 7)
                s5(dve.tensor_scalar(pw[:, 2, :, :], pw_re, nsgn[:, :], None, ALU.mult), False)
                s5(dve.tensor_scalar(pw[:, 3, :, :], pw_im, sgn[:, :], None, ALU.mult))
                for t in range(CH):
                    s5(dve.tensor_copy(pw_down[:, :, :, t], pw[:, :, :, CH - 1 - t]), False)
                s5(dve.tensor_scalar(v[S_NR], pw_re[:, :, 1], 1.0, None, ALU.subtract), False)
                s5(dve.tensor_tensor(v[S_T1], ar, ar, ALU.mult), False)
                s5(dve.tensor_tensor(v[S_T2], ai, ai, ALU.mult))
                s5(dve.tensor_tensor(v[S_T1], v[S_T1], v[S_T2], ALU.add))
                s5(dve.reciprocal(v[S_DEN], v[S_T1]))
                for dst, x_a, x_b, op in ((v[S_CR], v[S_NR], pw_im[:, :, 1], ALU.add),
                                          (v[S_CI], pw_im[:, :, 1], v[S_NR], ALU.subtract)):
                    s5(dve.tensor_tensor(v[S_T1], x_a, ar, ALU.mult), False)
                    s5(dve.tensor_tensor(v[S_T2], x_b, ai, ALU.mult))
                    s5(dve.tensor_tensor(v[S_T1], v[S_T1], v[S_T2], op))
                    s5(dve.tensor_tensor(dst, v[S_T1], v[S_DEN], ALU.mult))
                s5(dve.tensor_scalar(v[S_SCI], v[S_CI], sgn[:, :], None, ALU.mult))
                cr, sci = (v[t].unsqueeze(2).broadcast_to([P, G, M]) for t in (S_CR, S_SCI))
                for dst, x_a, x_b, op in ((bb, b_st, b_sw, ALU.add), (bb_sw, b_sw, b_st, ALU.subtract)):
                    s5(dve.tensor_tensor(tmp[0], x_a[:, :, :], cr, ALU.mult), False)
                    s5(dve.tensor_tensor(tmp[1], x_b[:, :, :], sci, ALU.mult))
                    s5(dve.tensor_tensor(dst[:, :, :], tmp[0], tmp[1], op))
                s5(dve.memset(pq[:, :, :, 0:1], 0.0))
                assert n_s5[0] == S5_DVE_STEPS, n_s5[0]

                apart(dve)
                with dve.Fori(0, 4) as i:
                    for j in range(2):
                        first_group = (2 * i + j) * 4
                        grp = bass.ds(first_group, 4)
                        at_rot = [18 * j]

                        def rot(inst, linked=True):
                            inst.then_inc(rot_step.sem, 1)
                            at_rot[0] += 1
                            if linked:
                                dve.wait_ge(rot_step.sem, rot_step.at(l, at_rot[0]) + 36 * i)

                        def fine(side):
                            return rot1[:, side, grp, :].unsqueeze(2).broadcast_to([P, 4, 8, 16])

                        def coarse(side):
                            return rot16[:, side, grp, :].unsqueeze(3).broadcast_to([P, 4, 8, 16])

                        def by_chunk(view):
                            return view.rearrange("p g (a b) -> p g a b", b=16)

                        t0, t1, t2 = (z_tmp[:, t, :, :] for t in range(3))
                        for side, (x_a, x_b), op in ((0, (0, 1), ALU.subtract), (1, (1, 0), ALU.add)):
                            rot(dve.tensor_tensor(by_chunk(t0), coarse(x_a), fine(0), ALU.mult), False)
                            rot(dve.tensor_tensor(by_chunk(t1), coarse(x_b), fine(1), ALU.mult))
                            rot(dve.tensor_tensor(rot_b[:, side, :, :], t0, t1, op))
                        def by_powers(table):
                            return pw[:, table, grp, 1:].unsqueeze(3).broadcast_to([P, 4, CH, M])

                        def by_step(view):
                            return view.rearrange("p g (j m) -> p g j m", m=M)

                        for dst, table, c_table in ((t0, 3, c_st), (t1, 0, c_sw)):
                            rot(dve.tensor_tensor(by_step(dst), by_powers(table),
                                                  c_table[:, grp, :].unsqueeze(2).broadcast_to([P, 4, CH, M]), ALU.mult))
                        rot(dve.tensor_tensor(m_2[:, j, :, :, :], by_step(t0), by_step(t1), ALU.subtract))
                        dve.wait_ge(toe_mm.sem, toe_mm.at(l, j + 1) + 2 * i)
                        for g in range(4):
                            last = dve.scalar_tensor_tensor(toe[:, j, g, :], ident[:, :], d_t[:, bass.ds(first_group + g, 1)],
                                                            ps[:, 2, g * P:(g + 1) * P], ALU.mult, ALU.add)
                        last.then_inc(toe_ready.sem, 1)
                        dve.wait_ge(v12_mm.sem, v12_mm.at(l, j + 1) + 2 * i)
                        for side, dst in ((0, t0), (1, t1)):
                            rot(dve.tensor_tensor(dst, rot_b[:, side, :, :], ps[:, 4 + side, :]
                                                  .rearrange("p (g c) -> p g c", g=4), ALU.mult), side == 1)
                        rot(dve.tensor_tensor(t2, t0, t1, ALU.add))
                        for g in range(4):
                            rot(dve.tensor_tensor_scan(out=g_sb[:, g, :],
                                                       data0=sm[:, S_MAG8, bass.ds(first_group + g, 1)].broadcast_to([P, NC]),
                                                       data1=z_tmp[:, 2, g, :], initial=0.0, op0=ALU.mult, op1=ALU.add),
                                g == 3)
                        dve.wait_ge(s5_pe.sem, s5_pe.at(l, j + 1) + 2 * i)
                        for side in range(2):
                            rot(dve.tensor_tensor(pq[:, side, :, 1:], rot_b[:, side, :, :], g_sb[:, :, :], ALU.mult), False)
                        assert at_rot[0] == 18 * (j + 1)
                for q in range(4):
                    wait(dve, y_hi_done, l, q + 1)
                    lo_of(y_lo[:, q, :], yt[:, q, :], y_hi[:, q, :]).then_inc(y_ready.sem, 1)
                for n in range(4):
                    wait(dve, glu_sig, l, n + 1)
                    dve.tensor_tensor(glu_s[:, n % 2, :], yt[:, n, :], glu_s[:, n % 2, :], ALU.mult).then_inc(glu_mul.sem, 1)
                    wait(dve, yg_hi_done, l, n + 1)
                    lo_of(yg_lo[:, n, :], glu_s[:, n % 2, :], yg_hi[:, n, :]).then_inc(yg_ready.sem, 1)
                apart(dve)
                with dve.Fori(0, 4) as i:
                    for j in range(2):
                        dve.wait_ge(unit_used.sem, unit_used.at(l, U_MERGE + j + 1) + 2 * i)
                        dve.wait_ge(gl_loaded.sem, gl_loaded.at(l, 32 * (j + 1)) + 64 * i)
                        dve.tensor_tensor(m_ab[:, 0, :], pair(4 * j), gl[:, 0, :], ALU.mult).then_inc(mg_step.sem, 1)
                        dve.tensor_tensor(m_ab[:, 1, :], pair(4 * j + 2), gl[:, 1, :], ALU.mult).then_inc(mg_free.sem, 1)
                        dve.wait_ge(mg_step.sem, mg_step.at(l, 2 * j + 1) + 4 * i)
                        dve.wait_ge(mg_free.sem, mg_free.at(l, j + 1) + 2 * i)
                        dve.tensor_tensor(m_sum[:, :], m_ab[:, 0, :], m_ab[:, 1, :], ALU.add).then_inc(mg_step.sem, 1)
                        dve.wait_ge(mg_hi_done.sem, mg_hi_done.at(l, j + 1) + 2 * i)
                        tile = bass.ds(2 * i + j, 1)
                        lo_of(mg_lo[:, tile, :].rearrange("p o n -> p (o n)"), m_sum[:, :],
                              mg_hi[:, tile, :].rearrange("p o n -> p (o n)")).then_inc(mg_ready.sem, 1)
                wait(dve, x_back, l, 16)
                apart(dve)
                with dve.Fori(0, 2) as i:
                    for j in range(4):
                        dve.wait_ge(unit_used.sem, unit_used.at(l, U_OUT + j + 1) + 4 * i)
                        tile = bass.ds(4 * i + j, 1)
                        x_tile = x_sb[:, tile, :].rearrange("p o n -> p (o n)")
                        dve.scalar_tensor_tensor(x_tile, pair(2 * (j % 2)), mod[:, 2, tile], x_tile, ALU.mult, ALU.add)\
                            .then_inc(wo_ev.sem, 1)
                        for k in (2 * j, 2 * j + 1):
                            ada_product(l, 4 * KT + k, k, KT * i)
                    modulation(l, 4, i, mod[:, bass.ds(i, 1), :].rearrange("p o k -> p (o k)"),
                               cols[:, bass.ds(1 - l, 1), bass.ds(i * KT, KT)].rearrange("p o k -> p (o k)"))
                wait(dve, mod_ready, l, 6)
                apart(dve)
                dve.scalar_tensor_tensor(a1[:, :], mod[:, 1, :], 1.0,
                                         cols[:, bass.ds(1 - l, 1), ROW_N1:ROW_N1 + KT].rearrange("p o k -> p (o k)"),
                                         ALU.add, ALU.mult).then_inc(a1_ready.sem, 1)
                wait(dve, a2_ready, l, 1)
                norm(l, 1, a2)

                def up_part(n, q, c_static, c_reg, buf):
                    for a in range(2):
                        dve.wait_ge(unit_used.sem, unit_used.at(l, n + 2 * a + 2) + 2 * q)
                        dve.wait_ge(silu_done.sem, silu_done.at(l, 2 * c_static + a + 1) + 2 * c_reg)
                        dve.tensor_tensor(silu[:, a, :], silu[:, a, :], pair(4 * a + 2), ALU.mult).then_inc(up_done.sem, 1)
                        dve.wait_ge(hid_hi_done.sem, hid_hi_done.at(l, 2 * c_static + a + 1) + 2 * c_reg)
                        lo_of(hid_lo[:, buf, a, :], silu[:, a, :], hid_hi[:, buf, a, :]).then_inc(hid_ready.sem, 1)

                def down_part(n, q, c_static, c_reg):
                    for t in range(KT):
                        if t % 4 < 3:
                            dve.wait_ge(dn_mm.sem, dn_mm.at(l, 6 * c_static + 3 * (t // 4) + t % 4 + 1) + 6 * c_reg)
                        else:
                            dve.wait_ge(unit_used.sem, unit_used.at(l, n + t // 4 + 1) + 2 * q)
                        dve.wait_ge(dn_ev.sem, dn_ev.at(l, 8 * (c_static - 1) + t + 1) + 8 * c_reg)
                        dve.scalar_tensor_tensor(x_sb[:, t, :], pair(2 * (t % 2)), mod[:, 5, t:t + 1], x_sb[:, t, :],
                                                 ALU.mult, ALU.add).then_inc(dn_ev.sem, 1)

                up_part(U_FFN, 0, 0, 0, 0)
                apart(dve)
                with dve.Fori(0, (CHUNKS - 1) // 2) as i:
                    for cc in range(2):
                        n = U_FFN + 4 + 6 * cc
                        up_part(n, 6 * i, 1 + cc, 2 * i, 1 - cc)
                        down_part(n + 4, 6 * i, cc, 2 * i)
                down_part(UNITS - 2, 0, CHUNKS - 1, 0)

            wait(dve, std_ready, DEPTH, 1)
            dve.reciprocal(rstd[:, 0, :], std[:, 0, :]).then_inc(rstd_ready.sem, 1)
            wait(dve, rb_ready, DEPTH, 1)
            for k in range(KT):
                dve.scalar_tensor_tensor(fin[:, k, :], x_sb[:, k, :], cols[:, 0, ROW_FG + k:ROW_FG + k + 1], rb[:, :],
                                         ALU.mult, ALU.mult).then_inc(fin_t.sem, 1)


INPUTS = ("x", "c", "positions", "w_ada", "b_ada", "norm1_g", "w_in", "ssm_a_re", "ssm_a_im", "ssm_log_dt",
          "ssm_b_re", "ssm_b_im", "ssm_c_re", "ssm_c_im", "ssm_d", "w_glu", "b_glu", "w_a_out", "q_norm_g",
          "w_uq", "kv_norm_g", "w_uk", "w_uv", "w_b_out", "w_out", "norm2_g", "w_gate", "w_up", "w_down",
          "final_g")


def kernel(**inputs):
    import concourse.bacc as bacc
    from concourse.bass_utils import run_bass_kernel_spmd

    nc = bacc.Bacc("TRN2", target_bir_lowering=False, num_devices=1)
    arrays = {f"in_{name}": np.ascontiguousarray(inputs[name]) for name in INPUTS}
    arrays["in_rope_const"] = rope_rows()
    args = [nc.dram_tensor(name, a.shape, mybir.dt.from_np(a.dtype), kind="ExternalInput").ap()
            for name, a in arrays.items()]
    out = nc.dram_tensor("out", arrays["in_x"].shape, F32, kind="ExternalOutput").ap()
    trunk(nc, *args, out)
    return run_bass_kernel_spmd(nc, [arrays], core_ids=[0]).results[0]["out"]
```

```python
from contextlib import ExitStack
import math

import numpy as np
import concourse.bass as bass
from concourse import mybir
from concourse.alu_op_type import AluOpType as ALU

ACT = mybir.ActivationFunctionType
F32 = mybir.dt.float32
F32R = mybir.dt.float32r
BF16 = mybir.dt.bfloat16
I32 = mybir.dt.int32

P = 128
EPS = 1e-6
QK_NOPE, QK_ROPE, V_DIM = 64, 32, 64
QK_DIM = QK_NOPE + QK_ROPE
MASKED = 1e30
TWO_PI_PARTS = (6.28125, 0.0019350051879882812, 3.0199159819567e-07)
ROUND = 12582912.0
MAX_ANGLE = 3.1415925
ROPE_ROWS = 6
CONSTS = 19
DVE_CONSTS = 7
S_MAG, S_MAG8, S_AD, S_AD8, S_DT, S_K, S_T1, S_T2, S_NR, S_DEN, S_CR, S_CI, S_SCI = range(6, 19)
S5_EXP_READY, S5_ANGLES_READY, S5_DVE_STEPS = 6, 30, 104
ROW_B_ADA, ROW_N1, ROW_N2, ROW_BGLU, ROW_QN, ROW_KVN, ROW_C, ROW_FG, ROWS = 0, 48, 56, 64, 68, 70, 71, 79, 87


class Count:

    def __init__(self, sem, per_layer, before=0):
        self.sem, self.per_layer, self.before = sem, per_layer, before

    def at(self, l, n):
        return l * self.per_layer + (n + self.before)


def rope_rows():
    r = np.arange(P)
    freq = (10000.0 ** (-np.arange(0, QK_ROPE, 2, dtype=np.float32).astype(np.float64) / QK_ROPE)).astype(np.float32)
    first_half = (r % QK_ROPE) < QK_ROPE // 2
    scale = QK_DIM ** -0.5
    t = np.zeros((P, ROPE_ROWS), np.float32)
    t[:, 0] = freq[r % (QK_ROPE // 2)]
    t[:, 1] = np.where((r >= 64) & (r < 96), -scale, 0)
    t[:, 2] = np.where(r >= 96, np.where(first_half, scale, -scale), 0)
    t[:, 3] = np.where(r < 64, -scale, 0)
    t[:, 4] = (r < 64).astype(np.float32)
    t[:, 5] = np.where(r >= 64, np.where(first_half, -1, 1), 0)
    return t


def trunk(nc, x, c, positions, w_ada, b_ada, norm1_g, w_in, ssm_a_re, ssm_a_im, ssm_log_dt, ssm_b_re,
          ssm_b_im, ssm_c_re, ssm_c_im, ssm_d, w_glu, b_glu, w_a_out, q_norm_g, w_uq, kv_norm_g, w_uk,
          w_uv, w_b_out, w_out, norm2_g, w_gate, w_up, w_down, final_g, rope_const, out):
    DEPTH, D, _ = w_ada.shape
    SEQ = x.shape[1]
    KT = D // P
    TT = SEQ // P
    HALF = SEQ // 2
    SSM = w_glu.shape[1]
    G, N_STATE, M = ssm_b_re.shape[1:]
    CH = 8
    NC = SEQ // CH
    Q_LORA, KV_LORA = w_uq.shape[1], w_uk.shape[1]
    HEADS = w_uk.shape[2] // QK_NOPE
    PAIRS = HEADS // 2
    FT = w_gate.shape[2] // P
    CHUNKS = FT // 2
    SPLIT = (0, SSM, SSM + Q_LORA, SSM + Q_LORA + KV_LORA, SSM + Q_LORA + KV_LORA + QK_ROPE)
    assert (D, SEQ, SSM, G, N_STATE, M, Q_LORA, KV_LORA, HEADS) == (1024, 1024, 512, 32, 64, 16, 256, 128, 8)
    assert CH * M == P and FT % 2 == 0 and CHUNKS % 2 == 1

    U_U = 0
    U_GATE = 4
    U_CKV, U_CQ, U_KR = 20, 21, 23
    LATENTS = ((2,), (0, 1))
    LATENT_ORDER = (2, 0, 1)
    U_HEAD = 24
    U_GLU = 32
    U_MERGE = 34
    U_OUT = 42
    U_FFN = 50
    UNITS = U_FFN + 3 * FT
    assert UNITS % 2 == 0

    xs_dram = nc.dram_tensor("xs_scratch", (P, KT, SEQ), F32, kind="Internal").ap()
    gate_dram = nc.dram_tensor("gate_scratch", (2 * KT, P, SEQ), F32, kind="Internal").ap()
    u_dram = nc.dram_tensor("u_scratch", (P, G, CH, M), F32, kind="Internal").ap()

    ctx = ExitStack()
    with ctx:
        base = (nc.sbuf_base + 63) // 64 * 64
        where = [base]
        itemsize = {F32: 4, F32R: 4, BF16: 2, I32: 4}

        def sb(name, shape, dt=F32):
            size = itemsize[dt] * int(np.prod(shape[1:]))
            t = nc.alloc_sbuf_tensor_at(name, list(shape), dt, offset=where[0])
            where[0] += (size + 31) // 32 * 32
            assert where[0] <= nc.sbuf_usable_end, (name, where[0])
            return t

        ident = sb("ident", [P, P])
        ones_col = sb("ones_col", [P, 1])
        mean_col = sb("mean_col", [P, 1])
        eps_col = sb("eps_col", [P, 1])
        sgn = sb("sgn", [P, 1])
        nsgn = sb("nsgn", [P, 1])
        rope_sb = sb("rope_sb", [P, ROPE_ROWS])
        cols = sb("cols", [P, DEPTH, ROWS])
        pcol = sb("pcol", [P, ROWS])
        c_act = sb("c_act", [P, KT])
        mod = sb("mod", [P, 6, KT])
        a1 = sb("a1", [P, KT])
        a2 = sb("a2", [P, KT])
        std = sb("std", [P, 2, TT])
        rstd = sb("rstd", [P, 2, TT])
        neg_max = sb("neg_max", [P, 2])
        row_sum = sb("row_sum", [P, 2])
        row_inv = sb("row_inv", [P, 2])
        mask = sb("mask", [P, TT, SEQ], BF16)
        tq = sb("tq", [P, SEQ])
        tk = sb("tk", [P, SEQ])
        raw = sb("raw", [P, 2, 1024])
        whi = sb("whi", [P, 2, 1024], F32R)
        wlo = sb("wlo", [P, 2, 1024], F32R)
        b_st = sb("b_st", [P, G, M])
        b_sw = sb("b_sw", [P, G, M])
        c_raw = sb("c_raw", [P, 2, 4, P])
        a_raw = sb("a_raw", [G, 2, 2, N_STATE])
        d_raw = sb("d_raw", [G, CH, M])
        ldt = sb("ldt", [P, G])
        zero = where[0]
        K = 1024

        def place(kib):
            where[0] = zero + kib * K

        place(0)
        ada_raw = sb("ada_raw", [P, 2, 1024])
        ada_acc = sb("ada_acc", [P, 1024])
        place(12)
        latn_hi = sb("latn_hi", [P, 3, SEQ], F32R)
        k_hi = sb("k_hi", [P, 2, SEQ], F32R)
        place(128)
        latn_lo = sb("latn_lo", [P, 3, SEQ], F32R)
        k_lo = sb("k_lo", [P, 2, SEQ], F32R)
        place(32)
        h_hi = sb("h_hi", [P, KT, SEQ], F32R)
        h_lo = sb("h_lo", [P, KT, SEQ], F32R)
        x_sb = sb("x_sb", [P, KT, SEQ])
        place(96)
        uc = sb("uc", [P, G, CH, M])
        place(96)
        lat = sb("lat", [P, 3, SEQ])
        lat_sq = sb("lat_sq", [P, 3, SEQ])
        lat_rb = sb("lat_rb", [P, 2, SEQ])
        place(108)
        kr_t = sb("kr_t", [P, 2, SEQ])
        place(128)
        sq_sum = sb("sq_sum", [P, SEQ])
        place(128)
        gst = sb("gst", [P, 2, SEQ])
        t_ring = sb("t_ring", [P, 2, SEQ])
        rb = sb("rb", [P, SEQ])
        place(0)
        v_hi = sb("v_hi", [P, TT, P], F32R)
        v_lo = sb("v_lo", [P, TT, P], F32R)
        q_f = sb("q_f", [P, SEQ])
        place(32)
        q_hi = sb("q_hi", [P, 2, SEQ], F32R)
        q_lo = sb("q_lo", [P, 2, SEQ], F32R)
        probs = sb("probs", [P, 3, SEQ])
        pt_hi = sb("pt_hi", [P, 2, TT, 2 * P], F32R)
        pt_lo = sb("pt_lo", [P, 2, TT, 2 * P], F32R)
        pt_f = sb("pt_f", [P, 2, HALF])
        assert where[0] <= zero + 96 * K
        place(96)
        o_hi = sb("o_hi", [P, PAIRS, SEQ], F32R)
        o_lo = sb("o_lo", [P, PAIRS, SEQ], F32R)
        place(0)
        yc = sb("yc", [P, CH, SSM])
        be = sb("be", [P, 2, 4, CH, M])
        m_v2 = sb("m_v2", [P, 2, 4, CH, M])
        m_1 = sb("m_1", [P, 2, 4, CH, M])
        m_2 = sb("m_2", [P, 2, 4, CH, M])
        m_tmp = sb("m_tmp", [P, 2, 4, CH, M])
        mt_1 = sb("mt_1", [P, 2, 4, P])
        mt_2 = sb("mt_2", [P, 2, 4, P])
        toe = sb("toe", [P, 2, 4, P])
        toe_col = sb("toe_col", [P, 4, M])
        shift = sb("shift", [P, P + (CH - 1) * M])
        ub = sb("ub", [P, 2, 4, P])
        ut = sb("ut", [P, 2, 4, NC])
        rot_b = sb("rot_b", [P, 2, 4, NC])
        z_tmp = sb("z_tmp", [P, 3, 4, NC])
        g_sb = sb("g_sb", [P, 4, NC])
        pq = sb("pq", [P, 2, 4, NC + 1])
        powers = sb("powers", [P, 2, 3, G, 16])
        pw_s = sb("pw_s", [P, 2, G, CH + 1])
        pw_down = sb("pw_down", [P, 4, G, CH])
        assert where[0] <= zero + 96 * K
        place(128)
        c_st = sb("c_st", [P, G, M])
        c_sw = sb("c_sw", [P, G, M])
        c_n = sb("c_n", [P, G, M])
        bb = sb("bb", [P, G, M])
        bb_sw = sb("bb_sw", [P, G, M])
        d_t = sb("d_t", [P, G])
        a_t = sb("a_t", [P, 2, G])
        sm = sb("sm", [P, 20, G])
        trig = sb("trig", [P, 6, G])
        assert where[0] <= zero + 148 * K
        place(16)
        yt = sb("yt", [P, 4, SEQ])
        y_hi = sb("y_hi", [P, 4, SEQ], F32R)
        y_lo = sb("y_lo", [P, 4, SEQ], F32R)
        glu_s = sb("glu_s", [P, 2, SEQ])
        place(0)
        yg_hi = sb("yg_hi", [P, 4, SEQ], F32R)
        place(128)
        yg_lo = sb("yg_lo", [P, 4, SEQ], F32R)
        m_sum = sb("m_sum", [P, SEQ])
        place(16)
        gl = sb("gl", [P, 2, SEQ])
        m_ab = sb("m_ab", [P, 2, SEQ])
        mg_hi = sb("mg_hi", [P, KT, SEQ], F32R)
        mg_lo = sb("mg_lo", [P, KT, SEQ], F32R)
        place(0)
        hid_hi = sb("hid_hi", [P, 2, 2, SEQ], F32R)
        hid_lo = sb("hid_lo", [P, 2, 2, SEQ], F32R)
        place(128)
        silu = sb("silu", [P, 2, SEQ])
        place(32)
        x_in = sb("x_in", [P, TT, D])
        prow = sb("prow", [P, DEPTH, P])
        pos_i = sb("pos_i", [P, SEQ], I32)
        pos_f = sb("pos_f", [P, SEQ])
        posq_i = sb("posq_i", [P, TT], I32)
        posq_i2 = sb("posq_i2", [P, TT], I32)
        posq_f = sb("posq_f", [P, 2, TT])
        ang = sb("ang", [P, SEQ])
        ang_k = sb("ang_k", [P, SEQ])
        half = sb("half", [P, SEQ])
        sin_t = sb("sin_t", [P, SEQ])
        assert where[0] <= zero + 96 * K
        place(12)
        pos_i2 = sb("pos_i2", [P, SEQ], I32)
        pos_lo = sb("pos_lo", [P, SEQ])
        mask_t = sb("mask_t", [P, SEQ])
        place(32)
        fin = sb("fin", [P, KT, SEQ])
        o_row = sb("o_row", [P, 2, D])

        ps = ctx.enter_context(nc.psum_tensor("ps", [P, 8, 512], F32))

        def pair(b, lo=0, hi=P):
            return ps[lo:hi, b:b + 2, :].rearrange("p a b -> p (a b)")

        credits = []

        def count(name, per_layer, before=0, credit=0):
            counter = Count(ctx.enter_context(nc.semaphore(name)), per_layer, before + credit)
            if credit:
                credits.append((counter, credit))
            return counter

        SLOT = 32 * (UNITS // 2)
        raw_loaded = [count("raw0_loaded", SLOT), count("raw1_loaded", SLOT)]
        w_hi_done = count("w_hi_done", UNITS)
        w_lo_done = count("w_lo_done", UNITS, credit=1)
        unit_used = count("unit_used", UNITS, credit=1)
        waited = count("waited", 0)
        const_loaded = count("const_loaded", 0)
        x_in_loaded = count("x_in_loaded", 0)
        pool_const = count("pool_const", 0)
        dve_const = count("dve_const", 0)
        act_const = count("act_const", 0)
        angles_ready = count("angles_ready", 0)
        cols_mm = count("cols_mm", 0)
        xt_mm = count("xt_mm", 0)
        xt_act = count("xt_act", 0)
        xt_dve = count("xt_dve", 0)
        x_spilled = count("x_spilled", 16)
        sq_ready = count("sq_ready", 2 * KT)
        sq_added = count("sq_added", 2 * (KT - 1))
        sq_mm = count("sq_mm", 2)
        std_ready = count("std_ready", 2)
        rstd_ready = count("rstd_ready", 2)
        rb_mm = count("rb_mm", 2)
        rb_ready = count("rb_ready", 2)
        t_ready = count("t_ready", 2 * KT)
        h_hi_done = count("h_hi_done", 2 * KT)
        h_ready = count("h_ready", 2 * KT, credit=1)
        pcol_ready = count("pcol_ready", 1)
        u_mm = count("u_mm", CH - 1)
        z_act = count("z_act", 4 + 2 * KT)
        u_ev_dve = count("u_ev_dve", 4)
        u_spilled = count("u_spilled", 16)
        gst_spilled = [count("gst0_spilled", 16 * KT, credit=1), count("gst1_spilled", 16 * KT, credit=1)]
        ada_loaded = [count("ada0_loaded", 16 * 24, 16 * 8), count("ada1_loaded", 16 * 24, 16 * 8)]
        ada_used = count("ada_used", 48, 16)
        mod_mm = count("mod_mm", 6, 2)
        mod_ready = count("mod_ready", 6, 2)
        a1_ready = count("a1_ready", 1, 1)
        a2_ready = count("a2_ready", 1)
        lat_sq_ready = count("lat_sq_ready", 3)
        lat_ss = count("lat_ss", 2)
        lat_std = count("lat_std", 2)
        lat_rstd = count("lat_rstd", 2)
        lat_rb_mm = count("lat_rb_mm", 2)
        lat_rb_ready = count("lat_rb_ready", 2)
        lat_t = count("lat_t", 3)
        lat_hi_done = count("lat_hi_done", 3)
        lat_ready = count("lat_ready", 3)
        kr_done = count("kr_done", 3)
        kr_hi_done = count("kr_hi_done", 2)
        kr_ready = count("kr_ready", 2)
        v_mm = count("v_mm", 2 * PAIRS)
        v_hi_done = count("v_hi_done", 2 * PAIRS)
        v_ready = count("v_ready", 2 * PAIRS)
        k_mm = count("k_mm", PAIRS)
        k_hi_done = count("k_hi_done", 2 * PAIRS)
        k_ready = count("k_ready", 2 * PAIRS)
        q_mm = count("q_mm", 2 * PAIRS)
        q_rot = count("q_rot", 2 * PAIRS)
        q_hi_done = count("q_hi_done", 2 * PAIRS)
        q_ready = count("q_ready", 2 * PAIRS)
        s_mm = count("s_mm", 16 * PAIRS)
        s_max = count("s_max", 16 * PAIRS)
        p_exp = count("p_exp", 16 * PAIRS, credit=1)
        p_inv = count("p_inv", 16 * PAIRS)
        p_ready = count("p_ready", 16 * PAIRS)
        pt_mm = count("pt_mm", 32 * PAIRS)
        pt_split = count("pt_split", 16 * PAIRS)
        pt_hi_done = count("pt_hi_done", 32 * PAIRS)
        pt_ready = [count("pt0_ready", 16 * PAIRS, credit=1),
                    count("pt1_ready", 16 * PAIRS, credit=1)]
        pv_mm = count("pv_mm", 8 * PAIRS, credit=1)
        o_hi_done = count("o_hi_done", 4 * PAIRS)
        o_ready = count("o_ready", 4 * PAIRS, credit=1)
        s5_loaded = count("s5_loaded", 16 * 14)
        s5_pe = count("s5_pe", 9, credit=1)
        s5_dve = count("s5_dve", S5_DVE_STEPS)
        s5_act = count("s5_act", 3)
        mat_step = count("mat_step", 9 * 8, credit=1)
        ub_loaded = [count("ub0_loaded", 16 * 4), count("ub1_loaded", 16 * 4)]
        s5_tr = count("s5_tr", 3 * 8)
        s5_tr_ev = count("s5_tr_ev", 3 * 8, credit=1)
        toe_col_mm = count("toe_col_mm", 8)
        toe_col_done = count("toe_col_done", 8)
        toe_mm = count("toe_mm", 8, credit=2)
        toe_ready = count("toe_ready", 8, credit=1)
        v12_mm = count("v12_mm", 8)
        rot_step = count("rot_step", 18 * 8, credit=1)
        y_gelu = count("y_gelu", 8, credit=1)
        yt_mm = count("yt_mm", 8)
        yt_ev = count("yt_ev", 8)
        y_hi_done = count("y_hi_done", 4)
        y_ready = count("y_ready", 4)
        glu_mm = count("glu_mm", 2)
        glu_sig = count("glu_sig", 4)
        glu_mul = count("glu_mul", 4, credit=1)
        yg_hi_done = count("yg_hi_done", 4)
        yg_ready = count("yg_ready", 4)
        gl_loaded = count("gl_loaded", 32 * KT)
        mg_free = count("mg_free", KT, credit=2)
        mg_step = count("mg_step", 2 * KT)
        mg_hi_done = count("mg_hi_done", KT)
        mg_ready = count("mg_ready", KT)
        x_back = count("x_back", 16)
        wo_ev = count("wo_ev", KT, credit=2)
        silu_done = count("silu_done", FT)
        up_done = count("up_done", FT)
        hid_hi_done = count("hid_hi_done", FT)
        hid_ready = count("hid_ready", FT, credit=1)
        dn_mm = count("dn_mm", 6 * CHUNKS)
        dn_ev = count("dn_ev", KT * CHUNKS, credit=KT)
        fin_t = count("fin_t", 0)
        fin_mm = count("fin_mm", 0)
        fin_ev = count("fin_ev", 0)
        out_done = [count("out0_done", 0), count("out1_done", 0)]

        def wait(eng, counter, l, n):
            eng.wait_ge(counter.sem, counter.at(l, n))

        def apart(eng):
            eng.sem_inc(waited.sem, 1)

        abar_powers = powers[:, :, 0, :, :]

        def raw_slot(n):
            return raw[:, n % 2, :]

        def unit_ready(eng, l, n, q=0):
            eng.wait_ge(w_lo_done.sem, w_lo_done.at(l, n + 1) + 2 * q)

        def head_pieces():
            def dst(a, b):
                return lambda t: t[:, 0:2 * P].rearrange("p (k n) -> p k n", k=2)[:, :, a:b]

            def src(a, b):
                return lambda t: t[:, 0:2 * QK_DIM].rearrange("p (k n) -> p k n", k=2)[:, :, a:b]
            return [(dst(0, 96), src(0, 96)), (dst(96, 112), src(80, 96)), (dst(112, 128), src(64, 80)),
                    (lambda t: t[:, 256:384], lambda t: t[:, 192:320])]

        PLAIN = [(lambda t: t, lambda t: t)]
        HEAD = head_pieces()

        def kr_pieces():
            def src(a, b):
                return lambda t: t[:, 0:KT * QK_ROPE].rearrange("p (k n) -> p k n", k=KT)[:, :, a:b]

            def dst(a, b):
                return lambda t: t.rearrange("p (k n) -> p k n", k=KT)[:, :, a:b]
            return [(dst(0, 32), src(0, 32)), (dst(32, 64), src(0, 32)),
                    (dst(64, 80), src(16, 32)), (dst(80, 96), src(0, 16)),
                    (dst(96, 112), src(16, 32)), (dst(112, 128), src(0, 16))]

        KR = kr_pieces()

        def split_hi(act, l, n, q=0, pieces=PLAIN):
            s = n % 2
            act.wait_ge(raw_loaded[s].sem, raw_loaded[s].at(l, 32 * (n // 2 + 1)) + 32 * q)
            act.wait_ge(unit_used.sem, unit_used.at(l, max(n - 1, 0)) + 2 * q)
            for dst, src in pieces:
                last = act.activation(dst(whi[:, s, :]), src(raw[:, s, :]), ACT.Copy)
            last.then_inc(w_hi_done.sem, 1)

        def split_lo(pool, l, n, q=0, pieces=PLAIN):
            s = n % 2
            pool.wait_ge(w_hi_done.sem, w_hi_done.at(l, n + 1) + 2 * q)
            for dst, src in pieces:
                last = pool.tensor_tensor(dst(wlo[:, s, :]), src(raw[:, s, :]), dst(whi[:, s, :].bitcast(F32)),
                                          ALU.subtract)
            last.then_inc(w_lo_done.sem, 1)

        def load_unit(sp, l, n, parts, q=0):
            s = n % 2
            sp.wait_ge(w_lo_done.sem, w_lo_done.at(l, max(n - 1, 0)) + 2 * q)
            assert len(parts) == 2
            for dst, src in parts:
                sp.dma_start(dst, src).then_inc(raw_loaded[s].sem, 16)

        def products(pe, outs, w_h, w_l, xs, first, last):
            for o, (x_h, _) in zip(outs, xs):
                pe.matmul(o, w_h, x_h, start=first, stop=False)
            for o, (_, x_l) in zip(outs, xs):
                pe.matmul(o, w_h, x_l, start=False, stop=False)
            return [pe.matmul(o, w_l, x_h, start=False, stop=last) for o, (x_h, _) in zip(outs, xs)]

        def halves(hi, lo, k):
            return [(hi[:, k, t * HALF:(t + 1) * HALF], lo[:, k, t * HALF:(t + 1) * HALF]) for t in range(2)]

        def tile_products(pe, s, bank, hi, lo, kts, n_cols=P, col=0, first=True, last=True):
            kts = list(kts)
            view_h = whi[:, s, :].rearrange("p (k n) -> p k n", n=n_cols)
            view_l = wlo[:, s, :].rearrange("p (k n) -> p k n", n=n_cols)
            for wk, xk in kts:
                end = products(pe, [ps[:, bank, :], ps[:, bank + 1, :]], view_h[:, wk, col:col + P],
                               view_l[:, wk, col:col + P], halves(hi, lo, xk),
                               first and wk == kts[0][0], last and wk == kts[-1][0])
            return end

        block = ctx.enter_context(nc.Block())

        @block.sync
        def _(sp):
            for dst, src in ((rope_sb[:, :], rope_const),
                             (prow[0:ROW_N1, 0, :], b_ada[0].rearrange("(r p) -> r p", p=P))):
                sp.dma_start(dst, src).then_inc(const_loaded.sem, 16)
            for l in range(DEPTH):
                rows = [(ROW_N1, norm1_g[l]), (ROW_N2, norm2_g[l]), (ROW_BGLU, b_glu[l]), (ROW_QN, q_norm_g[l]),
                        (ROW_KVN, kv_norm_g[l]), (ROW_C, c[0]), (ROW_FG, final_g)]
                if l:
                    rows.append((ROW_B_ADA, b_ada[l]))
                for r, v in rows:
                    n = v.shape[0] // P
                    sp.dma_start(prow[r:r + n, l, :], v.rearrange("(r p) -> r p", p=P)).then_inc(const_loaded.sem, 16)
            sp.dma_start(pos_i[:, :], positions[0].rearrange("(o n) -> o n", o=1).broadcast_to([P, SEQ]))\
                .then_inc(const_loaded.sem, 16)
            sp.dma_start(posq_i[:, :], positions[0].rearrange("(t p) -> p t", p=P), allow_slow_non_contiguous=True).then_inc(const_loaded.sem, 16)

            def load_ada(l, m, k, number):
                s = k % 2
                if number is not None:
                    sp.wait_ge(ada_used.sem, number)
                    apart(sp)
                sp.dma_start(ada_raw[:, s, :], w_ada[l][k * P:(k + 1) * P, m]).then_inc(ada_loaded[s].sem, 16)

            for t in range(TT):
                sp.dma_start(x_in[:, t, :], x[0, t * P:(t + 1) * P, :]).then_inc(x_in_loaded.sem, 16)
            for m in range(2):
                for k in range(KT):
                    n = m * KT + k
                    load_ada(0, slice(m * D, (m + 1) * D), k, n - 1 if n >= 2 else None)

            with sp.Fori(0, DEPTH) as l:
                w_in_l = w_in[l]

                def u_unit(n):
                    src = w_in_l[2 * n * P:(2 * n + 2) * P, 0:SSM]
                    return [(raw[:, n % 2, k * SSM:(k + 1) * SSM], src[k * P:(k + 1) * P, :]) for k in range(2)]

                def tile_unit(n, w, col, kts=KT):
                    src = w[:, col].rearrange("(k p) n -> p k n", p=P)
                    dst = raw[:, n % 2, 0:kts * P].rearrange("p (k n) -> p k n", k=kts)
                    h = kts // 2
                    return [(dst[:, 0:h, :], src[:, 0:h, :]), (dst[:, h:kts, :], src[:, h:kts, :])]

                load_unit(sp, l, 0, u_unit(0))
                load_unit(sp, l, 1, u_unit(1))
                wait(sp, glu_mul, l, 0)
                apart(sp)
                for half_of, (re, im) in enumerate(((ssm_b_re, ssm_b_im), (ssm_b_im, ssm_b_re))):
                    dst = (b_st, b_sw)[half_of]
                    sp.dma_start(dst[0:64, :, :], re[l].rearrange("g p m -> p g m")).then_inc(s5_loaded.sem, 16)
                    sp.dma_start(dst[64:P, :, :], im[l].rearrange("g p m -> p g m")).then_inc(s5_loaded.sem, 16)
                for half_of, (re, im) in enumerate(((ssm_c_re, ssm_c_im), (ssm_c_im, ssm_c_re))):
                    for side, v in enumerate((re, im)):
                        sp.dma_start(c_raw[:, half_of, :, side * 64:(side + 1) * 64],
                                     v[l].rearrange("(t g) m p -> (g m) t p", t=4)).then_inc(s5_loaded.sem, 16)
                for i, v in enumerate((ssm_a_re, ssm_a_im)):
                    for dup in range(2):
                        sp.dma_start(a_raw[:, i, dup, :], v[l]).then_inc(s5_loaded.sem, 16)
                sp.dma_start(ldt[:, :], ssm_log_dt[l].rearrange("(o g) -> o g", o=1).broadcast_to([P, G]))\
                    .then_inc(s5_loaded.sem, 16)
                sp.dma_start(d_raw[:, :, :], ssm_d[l].rearrange("(g o m) -> g o m", o=1, m=M)
                             .broadcast_to([G, CH, M])).then_inc(s5_loaded.sem, 16)
                load_unit(sp, l, 2, u_unit(2))
                load_unit(sp, l, 3, u_unit(3))
                wait(sp, dn_ev, l, 0)
                apart(sp)
                with sp.Fori(0, 4) as i:
                    for j in range(4):
                        load_unit(sp, l, U_GATE + j, tile_unit(j, w_in_l, bass.ds((i * 4 + j) * P + SPLIT[4], P)), 2 * i)
                        for k in (2 * j, 2 * j + 1):
                            load_ada(l, bass.ds((i + 2) * D, D), k, ada_used.at(l, k - 1) + KT * i)
                load_unit(sp, l, U_CKV, tile_unit(U_CKV, w_in_l, slice(SPLIT[2], SPLIT[2] + P)))
                for a in range(2):
                    load_unit(sp, l, U_CQ + a,
                              tile_unit(U_CQ + a, w_in_l, slice(SPLIT[1] + a * P, SPLIT[1] + (a + 1) * P)))
                src = w_in_l[:, SPLIT[3]:SPLIT[4]].rearrange("(k p) n -> p k n", p=P)
                dst = raw[:, U_KR % 2, 0:KT * QK_ROPE].rearrange("p (k n) -> p k n", k=KT)
                load_unit(sp, l, U_KR, [(dst[:, 0:4, :], src[:, 0:4, :]), (dst[:, 4:8, :], src[:, 4:8, :])])
                apart(sp)
                with sp.Fori(0, PAIRS) as i:
                    for j in range(2):
                        uq = w_uq[l][:, bass.ds((2 * i + j) * QK_DIM, QK_DIM)].rearrange("(k p) n -> p k n", p=P)
                        pair_w = (w_uk, w_uv)[j][l][:, bass.ds(i * P, P)]
                        load_unit(sp, l, U_HEAD + j,
                                  [(raw[:, j, 0:2 * QK_DIM].rearrange("p (k n) -> p k n", k=2), uq),
                                   (raw[:, j, 2 * QK_DIM:2 * QK_DIM + P], pair_w)], i)
                for a in range(2):
                    src = w_glu[l][:, 2 * a * P:(2 * a + 2) * P].rearrange("(k p) n -> p k n", p=P)
                    dst = raw[:, a, :].rearrange("p (k n) -> p k n", k=4)
                    load_unit(sp, l, U_GLU + a, [(dst[:, 0:2, :], src[:, 0:2, :]), (dst[:, 2:4, :], src[:, 2:4, :])])
                wait(sp, pv_mm, l, 8 * PAIRS)
                apart(sp)
                wait(sp, u_spilled, l, 16)
                apart(sp)
                with sp.Fori(0, 4) as i:
                    for j in range(2):
                        sp.wait_ge(s5_pe.sem, s5_pe.at(l, j) + 2 * i)
                        src = u_dram[:, bass.ds((2 * i + j) * 4, 4)].rearrange("c g j m -> c g (j m)")
                        sp.dma_start(ub[:, j, :, :], src).then_inc(ub_loaded[j].sem, 16)
                apart(sp)
                with sp.Fori(0, 4) as i:
                    for j in range(2):
                        col = bass.ds((2 * i + j) * P, P)
                        dst = raw[:, j, :].rearrange("p (k n) -> p k n", k=8)
                        load_unit(sp, l, U_MERGE + j,
                                  [(dst[:, 0:4, :], w_a_out[l][:, col].rearrange("(k p) n -> p k n", p=P)),
                                   (dst[:, 4:8, :], w_b_out[l][:, col].rearrange("(k p) n -> p k n", p=P))], i)
                        if j == 0:
                            wait(sp, glu_mul, l, 4)
                            wait(sp, gst_spilled[0], l, 16 * KT)
                            wait(sp, gst_spilled[1], l, 16 * KT)
                        sp.wait_ge(mg_free.sem, mg_free.at(l, j) + 2 * i)
                        for side in range(2):
                            src = gate_dram[bass.ds(2 * i + (j + side * KT), 1)].rearrange("o p n -> (o p) n")
                            sp.dma_start(gl[:, side, :], src).then_inc(gl_loaded.sem, 16)
                apart(sp)
                with sp.Fori(0, 2) as i:
                    for j in range(4):
                        load_unit(sp, l, U_OUT + j, tile_unit(j, w_out[l], bass.ds((i * 4 + j) * P, P)), 2 * i)
                        if j == 1:
                            wait(sp, unit_used, l, U_OUT)
                        for k in ((), range(0, 4), (4, 5), (6, 7))[j]:
                            load_ada(1 - l, bass.ds(i * D, D), k, ada_used.at(l, 4 * KT + k - 1) + KT * i)

                def ffn_unit(n, w, col):
                    return tile_unit(n, w[l], col)

                def down_unit(n, rows, d):
                    src = w_down[l][rows, d * 4 * P:(d + 1) * 4 * P].rearrange("(k p) n -> k p n", p=P)
                    return [(raw[:, n % 2, k * 4 * P:(k + 1) * 4 * P], src[k]) for k in range(2)]

                for a in range(2):
                    for w_i, w in enumerate((w_gate, w_up)):
                        n = U_FFN + 2 * a + w_i
                        load_unit(sp, l, n, ffn_unit(n, w, slice(a * P, (a + 1) * P)))
                apart(sp)
                with sp.Fori(0, (CHUNKS - 1) // 2) as i:
                    for cc in range(2):
                        n = U_FFN + 4 + 6 * cc
                        for a in range(2):
                            for w_i, w in enumerate((w_gate, w_up)):
                                col = bass.ds((i * 4 + (2 + 2 * cc + a)) * P, P)
                                load_unit(sp, l, n + 2 * a + w_i, ffn_unit(n + 2 * a + w_i, w, col), 6 * i)
                        for d in range(2):
                            rows = bass.ds((i * 4 + 2 * cc) * P, 2 * P)
                            load_unit(sp, l, n + 4 + d, down_unit(n + 4 + d, rows, d), 6 * i)
                for d in range(2):
                    rows = slice((FT - 2) * P, FT * P)
                    load_unit(sp, l, UNITS - 2 + d, down_unit(d, rows, d))
            for t in range(TT):
                sp.wait_ge(fin_ev.sem, t + 1)
                sp.dma_start(out[0, t * P:(t + 1) * P, :], o_row[:, t % 2, :]).then_inc(out_done[t % 2].sem, 16)
            for s in out_done:
                sp.wait_ge(s.sem, 16 * (TT // 2))

        @block.gpsimd
        def _(pool):
            pool.memset(ident[:, :], 0.0).then_inc(pool_const.sem, 1)
            pool.wait_ge(pool_const.sem, 1)
            pool.affine_select(out=ident[:, :], in_=ident[:, :], compare_op=ALU.not_equal, fill=1.0, base=0,
                               pattern=[[-1, P]], channel_multiplier=1).then_inc(pool_const.sem, 1)

            def add_squares(l, occ, k):
                n = (KT - 1) * occ + k
                wait(pool, sq_ready, l, KT * occ + k + 1)
                if k > 1:
                    wait(pool, sq_added, l, n - 1)
                pool.tensor_tensor(sq_sum[:, :], t_ring[:, 0, :] if k == 1 else sq_sum[:, :], t_ring[:, k % 2, :],
                                   ALU.add).then_inc(sq_added.sem, 1)

            for k in range(1, KT):
                add_squares(0, 0, k)
            with pool.Fori(0, DEPTH) as l:
                for n in range(U_GATE):
                    split_lo(pool, l, n)
                apart(pool)
                with pool.Fori(0, 4) as i:
                    for j in range(4):
                        split_lo(pool, l, U_GATE + j, 2 * i)
                for n in (U_CKV, U_CQ, U_CQ + 1):
                    split_lo(pool, l, n)
                split_lo(pool, l, U_KR, 0, KR)

                split_lo(pool, l, U_HEAD, 0, HEAD)
                split_lo(pool, l, U_HEAD + 1, 0, HEAD)
                wait(pool, w_lo_done, l, U_HEAD + 2)
                for head in range(2):
                    wait(pool, kr_hi_done, l, head + 1)
                    pool.tensor_tensor(k_lo[64:P, head, :], kr_t[64:P, 0, :], k_hi[64:P, head, :].bitcast(F32),
                                       ALU.subtract).then_inc(kr_ready.sem, 1)
                wait(pool, kr_ready, l, 2)

                def attention_pair(i, last_pair):
                    for tile in range(16):
                        if tile in (0, 3):
                            if last_pair:
                                split_lo(pool, l, U_GLU + tile // 3)
                            else:
                                split_lo(pool, l, U_HEAD + 2 + tile // 3, i, HEAD)
                        pool.wait_ge(pt_hi_done.sem, pt_hi_done.at(l, 2 * tile + 2) + 32 * i)
                        apart(pool)
                        at = (slice(None), tile // 2 % 2, slice(4, 8), slice((tile % 2) * P, (tile % 2 + 1) * P))
                        whole = pt_f[:, tile % 2, :].rearrange("p (k n) -> p k n", k=4)
                        pool.tensor_copy(pt_hi[at], whole).then_inc(pt_split.sem, 1)
                        pool.wait_ge(pt_split.sem, pt_split.at(l, tile + 1) + 16 * i)
                        pool.tensor_tensor(pt_lo[at], whole, pt_hi[at].bitcast(F32), ALU.subtract)\
                            .then_inc(pt_ready[1].sem, 1)

                apart(pool)
                with pool.Fori(0, PAIRS - 1) as i:
                    attention_pair(i, False)
                attention_pair(PAIRS - 1, True)

                wait(pool, s5_dve, l, S5_DVE_STEPS)
                apart(pool)
                with pool.Fori(0, 4) as i:
                    for j in range(2):
                        pool.wait_ge(toe_mm.sem, toe_mm.at(l, j - 1) + 2 * i)
                        grp = bass.ds((i * 2 + j) * 4, 4)
                        step = [9 * j]

                        def by_powers(v, powers):
                            return v[:, grp, powers].unsqueeze(3).broadcast_to([P, 4, CH, M])

                        def by_channels(v):
                            return v[:, grp, :].unsqueeze(2).broadcast_to([P, 4, CH, M])

                        def combine(dst, p_a, v_a, p_b, v_b, powers, op):
                            pool.wait_ge(mat_step.sem, mat_step.at(l, step[0]) + 18 * i)
                            pool.tensor_tensor(m_tmp[:, 0], by_powers(p_a, powers), by_channels(v_a), ALU.mult)\
                                .then_inc(mat_step.sem, 1)
                            pool.tensor_tensor(m_tmp[:, 1], by_powers(p_b, powers), by_channels(v_b), ALU.mult)\
                                .then_inc(mat_step.sem, 1)
                            pool.wait_ge(mat_step.sem, mat_step.at(l, step[0] + 2) + 18 * i)
                            pool.tensor_tensor(dst, m_tmp[:, 0], m_tmp[:, 1], op).then_inc(mat_step.sem, 1)
                            step[0] += 3

                        down = slice(0, CH)
                        re, im, nre, sim = (pw_down[:, t] for t in range(4))
                        combine(be[:, j, :, :, :], re, bb, sim, bb_sw, down, ALU.add)
                        combine(m_v2[:, j], nre, bb_sw, im, bb, down, ALU.add)
                        up = slice(1, CH + 1)
                        (re, im), (nre, sim) = ((t[:, 0], t[:, 1]) for t in (abar_powers, pw_s))
                        pool.wait_ge(s5_pe.sem, s5_pe.at(l, j) + 2 * i)
                        combine(m_1[:, j], nre, c_st, im, c_sw, up, ALU.subtract)
                apart(pool)
                with pool.Fori(0, 4) as i:
                    for j in range(2):
                        split_lo(pool, l, U_MERGE + j, i)
                split_lo(pool, l, U_OUT)
                split_lo(pool, l, U_OUT + 1)
                for n in range(KT):
                    split_lo(pool, l, U_OUT + n + 2)
                    if n:
                        add_squares(l, 1, n)
                apart(pool)
                with pool.Fori(0, CHUNKS - 1) as i:
                    for j in range(6):
                        split_lo(pool, l, U_FFN + 2 + j, 3 * i)
                for n in range(UNITS - 4, UNITS):
                    split_lo(pool, l, n)
                for k in range(1, KT):
                    add_squares(l, 2, k)

        @block.tensor
        def _(pe):
            pe.wait_ge(pool_const.sem, 2)
            pe.wait_ge(const_loaded.sem, 16 * CONSTS)
            for d in range(DEPTH):
                last = pe.transpose(ps[:, 0, d * P:d * P + ROWS], prow[0:ROWS, d, :], ident[0:ROWS, 0:ROWS])
            last.then_inc(cols_mm.sem, 1)
            pe.wait_ge(x_in_loaded.sem, 16 * TT)
            for k in range(KT):
                b = 2 + 2 * (k % 2)
                if k >= 2:
                    pe.wait_ge((xt_act, xt_dve)[k % 2].sem, k // 2)
                for t in range(TT):
                    last = pe.transpose(ps[:, b + t // 4, (t % 4) * P:(t % 4 + 1) * P],
                                        x_in[:, t, k * P:(k + 1) * P], ident[:, 0:P])
                last.then_inc(xt_mm.sem, 1)

            def mod_products():
                for n in range(KT):
                    last = pe.matmul(ps[:, 7, n:n + 1], ada_acc[:, n * P:(n + 1) * P], ones_col[:, :],
                                     start=True, stop=True)
                last.then_inc(mod_mm.sem, 1)

            def mean_squares(l, occ):
                wait(pe, sq_added, l, (KT - 1) * (occ + 1))
                for t in range(TT):
                    last = pe.matmul(ps[:, 6, t:t + 1], sq_sum[:, t * P:(t + 1) * P], mean_col[:, :],
                                     start=True, stop=True)
                last.then_inc(sq_mm.sem, 1)

            def norm_scale(l, occ):
                wait(pe, rstd_ready, l, occ + 1)
                for t in range(TT):
                    last = pe.matmul(ps[:, 4 + t // 4, (t % 4) * P:(t % 4 + 1) * P],
                                     rstd[:, 0, t:t + 1].broadcast_to([P, P]), ident[:, 0:P], start=True, stop=True)
                last.then_inc(rb_mm.sem, 1)

            for m in range(2):
                pe.wait_ge(ada_used.sem, KT * (m + 1))
                pe.wait_ge(mod_ready.sem, m)
                mod_products()

            with pe.Fori(0, DEPTH) as l:
                mean_squares(l, 0)
                norm_scale(l, 0)
                wait(pe, rb_ready, l, 1)
                wait(pe, mod_ready, l, 0)
                for n in range(U_GATE):
                    unit_ready(pe, l, n)
                    for kk in range(2):
                        k = 2 * n + kk
                        wait(pe, h_ready, l, k + 1)
                        w_h, w_l = (w[:, n % 2, kk * SSM:(kk + 1) * SSM] for w in (whi, wlo))
                        for j in range(CH):
                            x_h, x_l = h_hi[:, k, j::CH], h_lo[:, k, j::CH]
                            pe.matmul(ps[:, j, :], x_h, w_h, start=(k == 0), stop=False)
                            pe.matmul(ps[:, j, :], x_h, w_l, start=False, stop=False)
                            last = pe.matmul(ps[:, j, :], x_l, w_h, start=False, stop=(k == KT - 1))
                            if k == KT - 1 and j < CH - 1:
                                last.then_inc(u_mm.sem, 1)
                    last.then_inc(unit_used.sem, 1)
                wait(pe, u_ev_dve, l, 4)
                apart(pe)
                with pe.Fori(0, 4) as i:
                    for j in range(4):
                        b = 2 * (j % 2)
                        unit_ready(pe, l, U_GATE + j, 2 * i)
                        pe.wait_ge(z_act.sem, z_act.at(l, j + 3) + 4 * i)
                        end = tile_products(pe, j % 2, b, h_hi, h_lo, [(k, k) for k in range(KT)])
                        end[1].then_inc(unit_used.sem, 1)
                    pe.wait_ge(ada_used.sem, ada_used.at(l, KT) + KT * i)
                    pe.wait_ge(mod_ready.sem, mod_ready.at(l, 0) + i)
                    mod_products()
                wait(pe, z_act, l, 4 + 2 * KT)
                wait(pe, mod_ready, l, 4)

                def latent_unit(u):
                    unit_ready(pe, l, u)
                    end = tile_products(pe, u % 2, 2 * (u - U_CKV), h_hi, h_lo, [(k, k) for k in range(KT)])
                    end[1].then_inc(unit_used.sem, 1)

                def latent_squares(side):
                    wait(pe, lat_sq_ready, l, 1 + 2 * side)
                    tiles = LATENTS[side]
                    for a in tiles:
                        for t in range(TT):
                            last = pe.matmul(ps[:, 2 * side, t:t + 1], lat_sq[:, a, t * P:(t + 1) * P], mean_col[:, :],
                                             start=(a == tiles[0] and t == 0), stop=(a == tiles[-1]),
                                             skip_group_check=True)
                    last.then_inc(lat_ss.sem, 1)

                def latent_scale(side):
                    wait(pe, lat_rstd, l, side + 1)
                    for t in range(TT):
                        last = pe.matmul(ps[:, 2 * side + t // 4, (t % 4) * P:(t % 4 + 1) * P],
                                         rstd[:, side, t:t + 1].broadcast_to([P, P]), ident[:, 0:P],
                                         start=True, stop=True)
                    last.then_inc(lat_rb_mm.sem, 1)

                latent_unit(U_CKV)
                latent_unit(U_CQ)
                latent_squares(0)
                latent_unit(U_CQ + 1)
                latent_scale(0)
                latent_squares(1)
                latent_scale(1)
                latent_unit(U_KR)

                even, odd = U_HEAD % 2, 1 - U_HEAD % 2

                def queries(s, bank):
                    w_h, w_l = whi[:, s, :], wlo[:, s, :]
                    for k in range(2):
                        end = products(pe, [ps[:, bank, :], ps[:, bank + 1, :]], w_h[:, k * P:(k + 1) * P],
                                       w_l[:, k * P:(k + 1) * P], halves(latn_hi, latn_lo, k), k == 0, k == 1)
                    end[1].then_inc(q_mm.sem, 1)

                def even_queries(i, ahead):
                    unit_ready(pe, l, U_HEAD + 2 * ahead, i)
                    if ahead:
                        pe.wait_ge(p_exp.sem, p_exp.at(l, 15) + 16 * i)
                    queries(even, 0)

                def both_keys(i, ahead):
                    if ahead:
                        pe.wait_ge(p_exp.sem, p_exp.at(l, 16) + 16 * i)
                    for t in range(2):
                        last = products(pe, [ps[:, 2 + t, :]], whi[:, even, 256:384], wlo[:, even, 256:384],
                                        [halves(latn_hi, latn_lo, 2)[t]], True, True)[0]
                    last.then_inc(k_mm.sem, 1)

                def attention_pair(i, last_pair):
                    def scores(g):
                        head = g // 8
                        q = slice((g % 8) * P, (g % 8 + 1) * P)
                        b = 2 * (g % 2)
                        if g >= 2:
                            pe.wait_ge(p_exp.sem, p_exp.at(l, g - 1) + 16 * i)
                        for t in range(2):
                            kk = slice(t * HALF, (t + 1) * HALF)
                            first = pe.matmul(ps[:, b + t, :], q_hi[:, head, q], k_hi[:, head, kk], start=True, stop=False)
                            if t == 0 and g in (0, 3):
                                first.then_inc(unit_used.sem, 1)
                            pe.matmul(ps[:, b + t, :], q_hi[:, head, q], k_lo[:, head, kk], start=False, stop=False)
                            last = pe.matmul(ps[:, b + t, :], q_lo[:, head, q], k_hi[:, head, kk], start=False, stop=True)
                        last.then_inc(s_mm.sem, 1)

                    def transposes(g):
                        pe.wait_ge(p_ready.sem, p_ready.at(l, g + 1) + 16 * i)
                        for t in range(2):
                            if g:
                                if t == 0:
                                    pe.wait_ge(pt_ready[0].sem, pt_ready[0].at(l, g) + 16 * i)
                                else:
                                    pe.wait_ge(pt_hi_done.sem, pt_hi_done.at(l, 2 * g) + 32 * i)
                            for k in range(4):
                                kt = 4 * t + k
                                last = pe.transpose(ps[:, 4 + t, k * P:(k + 1) * P], probs[:, g % 3, kt * P:(kt + 1) * P],
                                                    ident[:, 0:P])
                            last.then_inc(pt_mm.sem, 1)

                    def outputs(n, part):
                        m = n // 2
                        if part == 0:
                            if n % 2 == 0 and m >= 2:
                                pe.wait_ge(o_ready.sem, o_ready.at(l, m - 1) + 4 * i)
                            for ready in pt_ready:
                                pe.wait_ge(ready.sem, ready.at(l, 2 * (n + 1)) + 16 * i)
                        out_ = ps[:, 6 + m % 2, (n % 2) * 2 * P:(n % 2 + 1) * 2 * P]
                        for k in range(4 * part, 4 * part + 4):
                            last = products(pe, [out_], v_hi[:, k, :], v_lo[:, k, :],
                                            [(pt_hi[:, n % 2, k, :], pt_lo[:, n % 2, k, :])],
                                            k == 0, k == TT - 1)[0]
                        if part:
                            last.then_inc(pv_mm.sem, 1)

                    def values():
                        unit_ready(pe, l, U_HEAD + 1, i)
                        for ready in pt_ready:
                            pe.wait_ge(ready.sem, ready.at(l, 0) + 16 * i)
                        for t in range(TT):
                            tok = slice(t * P, (t + 1) * P)
                            bank = ps[:, 4 + t // 4, (t % 4) * P:(t % 4 + 1) * P]
                            pe.matmul(bank, latn_hi[:, 2, tok], whi[:, odd, 256:384], start=True, stop=False)
                            pe.matmul(bank, latn_hi[:, 2, tok], wlo[:, odd, 256:384], start=False, stop=False)
                            last = pe.matmul(bank, latn_lo[:, 2, tok], whi[:, odd, 256:384], start=False, stop=True)
                            if t % 4 == 3:
                                last.then_inc(v_mm.sem, 1)

                    for g in range(20):
                        if 2 <= g <= 17:
                            if g == 2:
                                pe.wait_ge(v_ready.sem, v_ready.at(l, 2) + 2 * i)
                            transposes(g - 2)
                        if g < 2:
                            pe.wait_ge(q_ready.sem, q_ready.at(l, 1) + 2 * i)
                            pe.wait_ge(k_ready.sem, k_ready.at(l, 2) + 2 * i)
                        if g == 8:
                            wait(pe, kr_ready, l, 2)
                            pe.wait_ge(q_ready.sem, q_ready.at(l, 2) + 2 * i)
                        if g < 16:
                            scores(g)
                        if g == 0:
                            values()
                        if g == 1:
                            pe.wait_ge(o_ready.sem, o_ready.at(l, 0) + 4 * i)
                            queries(odd, 6)
                        if g == 16 and not last_pair:
                            even_queries(i, 1)
                        if g == 17 and not last_pair:
                            both_keys(i, 1)
                        if g >= 4:
                            if g == 4:
                                pe.wait_ge(q_rot.sem, q_rot.at(l, 2) + 2 * i)
                            outputs((g - 4) // 2, g % 2)

                wait(pe, lat_rb_ready, l, 2)
                wait(pe, lat_ready, l, 3)
                even_queries(0, 0)
                both_keys(0, 0)
                wait(pe, kr_ready, l, 1)
                apart(pe)
                with pe.Fori(0, PAIRS - 1) as i:
                    attention_pair(i, False)
                attention_pair(PAIRS - 1, True)

                wait(pe, o_ready, l, 4 * PAIRS)
                wait(pe, s5_loaded, l, 16 * 14)
                apart(pe)
                for i in range(2):
                    pe.transpose(ps[:, 0, i * G:(i + 1) * G], a_raw[:, i, :, :].rearrange("g a p -> g (a p)"),
                                 ident[0:G, 0:G])
                pe.transpose(ps[:, 0, 2 * G:3 * G], d_raw[:, :, :].rearrange("g j m -> g (j m)"), ident[0:G, 0:G])
                for s in range(2):
                    for t in range(4):
                        last = pe.transpose(ps[:, 1 + s, t * P:(t + 1) * P], c_raw[:, s, t, :], ident[:, 0:P])
                last.then_inc(s5_pe.sem, 1)
                wait(pe, s5_dve, l, S5_DVE_STEPS)
                apart(pe)
                def batch_inputs(b, i):
                    j = b % 2
                    pe.wait_ge(mat_step.sem, mat_step.at(l, 9 * b + 6) + 18 * i)
                    pe.wait_ge(s5_tr_ev.sem, s5_tr_ev.at(l, 3 * b) + 6 * i)
                    for side in range(2):
                        for g in range(4):
                            src = (be, m_v2)[side][:, j, g, :, :]
                            last = pe.transpose(ps[:, side, g * P:(g + 1) * P],
                                                src.rearrange("p j m -> p (j m)"), ident[:, 0:P])
                        last.then_inc(s5_tr.sem, 1)
                    pe.wait_ge(ub_loaded[j].sem, ub_loaded[j].at(l, 16 * (b // 2 + 1)) + 16 * i)
                    for g in range(4):
                        last = pe.transpose(ps[:, 3, g * P:(g + 1) * P], ub[:, j, g, :], ident[:, 0:P])
                    last.then_inc(s5_tr.sem, 1)
                    pe.wait_ge(toe_ready.sem, toe_ready.at(l, b) + 2 * i)
                    for g in range(4):
                        last = pe.matmul(ps[:, 2, g * M:(g + 1) * M], be[:, j, g, :, :].rearrange("p j m -> p (j m)"),
                                         c_n[:, bass.ds((i * 2 + b) * 4 + g, 1), :].rearrange("p o m -> p (o m)"),
                                         start=True, stop=True)
                    last.then_inc(toe_col_mm.sem, 1)
                    pe.wait_ge(s5_tr_ev.sem, s5_tr_ev.at(l, 3 * b + 3) + 6 * i)
                    pe.wait_ge(rot_step.sem, rot_step.at(l, 18 * b) + 36 * i)
                    for side, mt in enumerate((mt_1, mt_2)):
                        for g in range(4):
                            last = pe.matmul(ps[:, 4 + side, g * P:(g + 1) * P], mt[:, j, g, :], ut[:, j, g, :],
                                             start=True, stop=True)
                    last.then_inc(v12_mm.sem, 1)
                    pe.wait_ge(toe_col_done.sem, toe_col_done.at(l, b + 1) + 2 * i)
                    for jj in range(CH):
                        lo = (CH - 1 - jj) * M
                        last = pe.matmul(ps[:, 2, jj * 4 * M:(jj + 1) * 4 * M], shift[:, lo:lo + P],
                                         toe_col[:, :, :].rearrange("p g m -> p (g m)"), start=True, stop=True)
                    last.then_inc(toe_mm.sem, 1)

                def batch_outputs(b, i):
                    j = b % 2
                    pe.wait_ge(mat_step.sem, mat_step.at(l, 9 * b + 9) + 18 * i)
                    pe.wait_ge(toe_ready.sem, toe_ready.at(l, b + 1) + 2 * i)
                    pe.wait_ge(rot_step.sem, rot_step.at(l, 18 * b + 18) + 36 * i)
                    pe.wait_ge(y_gelu.sem, y_gelu.at(l, max(b - 1, 0)) + 2 * i)
                    for g in range(4):
                        o = ps[:, 6 + j, g * P:(g + 1) * P]
                        pe.matmul(o, ut[:, j, g, :], toe[:, j, g, :], start=True, stop=False)
                        pe.matmul(o, pq[:, 0, g, 0:NC], m_1[:, j, g, :, :].rearrange("p j m -> p (j m)"),
                                  start=False, stop=False)
                        last = pe.matmul(o, pq[:, 1, g, 0:NC], m_2[:, j, g, :, :].rearrange("p j m -> p (j m)"),
                                         start=False, stop=True)
                    last.then_inc(s5_pe.sem, 1)

                batch_inputs(0, 0)
                apart(pe)
                with pe.Fori(0, 3) as i:
                    for b in range(2):
                        batch_inputs(b + 1, i)
                        batch_outputs(b, i)
                batch_inputs(1, 3)
                batch_outputs(0, 3)
                batch_outputs(1, 3)
                wait(pe, y_gelu, l, 8)
                for q in range(4):
                    for s in range(2):
                        for jj in range(4):
                            last = pe.transpose(ps[:, 2 * q + s, jj * P:(jj + 1) * P],
                                                yc[:, 4 * s + jj, q * P:(q + 1) * P], ident[:, 0:P])
                        last.then_inc(yt_mm.sem, 1)
                wait(pe, y_ready, l, 4)
                for a in range(2):
                    unit_ready(pe, l, U_GLU + a)
                    for nn in range(2):
                        end = tile_products(pe, a, 4 * a + 2 * nn, y_hi, y_lo, [(k, k) for k in range(4)],
                                            n_cols=2 * P, col=nn * P)
                        end[1].then_inc((glu_mm, unit_used)[nn].sem, 1)
                wait(pe, yg_ready, l, 4)
                apart(pe)
                with pe.Fori(0, 4) as i:
                    for j in range(2):
                        unit_ready(pe, l, U_MERGE + j, i)
                        pe.wait_ge(mg_free.sem, mg_free.at(l, j - 1) + 2 * i)
                        tile_products(pe, j, 4 * j, yg_hi, yg_lo, [(k, k) for k in range(4)])
                        end = tile_products(pe, j, 4 * j + 2, o_hi, o_lo, [(4 + k, k) for k in range(4)])
                        end[1].then_inc(unit_used.sem, 1)
                wait(pe, mg_ready, l, KT)
                for n in range(KT):
                    unit_ready(pe, l, U_OUT + n)
                    wait(pe, wo_ev, l, n - 1)
                    end = tile_products(pe, n % 2, 2 * (n % 2), mg_hi, mg_lo, [(k, k) for k in range(KT)])
                    end[1].then_inc(unit_used.sem, 1)
                    if n in (3, 7):
                        m = n // 4
                        wait(pe, ada_used, l, (5 + m) * KT)
                        wait(pe, mod_ready, l, 4 + m)
                        mod_products()
                mean_squares(l, 1)
                norm_scale(l, 1)

                def up_products(n, q, c_static, c_reg, tiles=(0, 1)):
                    for a in tiles:
                        for w_i in range(2):
                            b = 4 * a + 2 * w_i
                            u = n + 2 * a + w_i
                            unit_ready(pe, l, u, q)
                            if c_reg is not None:
                                if a == 0:
                                    pe.wait_ge(up_done.sem, up_done.at(l, 2 * c_static - 1) + c_reg * 2)
                                    pe.wait_ge(dn_ev.sem, dn_ev.at(l, 8 * (c_static - 2) + 7 + w_i) + c_reg * 8)
                                else:
                                    pe.wait_ge(up_done.sem, up_done.at(l, 2 * c_static) + c_reg * 2)
                            end = tile_products(pe, u % 2, b, h_hi, h_lo, [(k, k) for k in range(KT)])
                            end[1].then_inc(unit_used.sem, 1)

                def down_products(buf, n, q, c_static, c_reg, last_chunk):
                    pe.wait_ge(hid_ready.sem, hid_ready.at(l, 2 * c_static + 2) + c_reg * 2)
                    for d in range(2):
                        unit_ready(pe, l, n + d, q)
                        for nn in range(4):
                            t = 4 * d + nn
                            b = 2 * (t % 2)
                            if t < 2:
                                pe.wait_ge(up_done.sem, up_done.at(l, 2 * c_static + (2 if last_chunk else 3)) + c_reg * 2)
                                pe.wait_ge(dn_ev.sem, dn_ev.at(l, 8 * (c_static - 1) + 7 + t) + c_reg * 8)
                            else:
                                pe.wait_ge(dn_ev.sem, dn_ev.at(l, 8 * c_static + t - 1) + c_reg * 8)
                            s = (n + d) % 2
                            xs_h, xs_l = hid_hi[:, buf], hid_lo[:, buf]
                            for k in range(2):
                                col = k * 4 * P + nn * P
                                end = products(pe, [ps[:, b, :], ps[:, b + 1, :]], whi[:, s, col:col + P],
                                               wlo[:, s, col:col + P], halves(xs_h, xs_l, k), k == 0, k == 1)
                            end[1].then_inc((dn_mm if nn < 3 else unit_used).sem, 1)

                wait(pe, rb_ready, l, 2)
                wait(pe, mod_ready, l, 6)
                for w_i in range(2):
                    unit_ready(pe, l, U_FFN + w_i)
                for k in range(KT):
                    wait(pe, h_ready, l, KT + k + 1)
                    for w_i in range(2):
                        end = tile_products(pe, (U_FFN + w_i) % 2, 2 * w_i, h_hi, h_lo, [(k, k)],
                                            first=(k == 0), last=(k == KT - 1))
                        if k == KT - 1:
                            end[1].then_inc(unit_used.sem, 1)
                up_products(U_FFN, 0, 0, None, (1,))
                apart(pe)
                with pe.Fori(0, (CHUNKS - 1) // 2) as i:
                    for cc in range(2):
                        n = U_FFN + 4 + 6 * cc
                        up_products(n, 6 * i, 1 + cc, i * 2)
                        down_products(cc, n + 4, 6 * i, cc, i * 2, False)
                down_products(0, UNITS - 2, 0, CHUNKS - 1, 0, True)

            mean_squares(DEPTH, 0)
            norm_scale(DEPTH, 0)
            for t in range(TT):
                if t == 0:
                    pe.wait_ge(fin_t.sem, KT)
                if t >= 2:
                    pe.wait_ge(fin_ev.sem, t - 1)
                b = 2 * (t % 2)
                for k in range(KT):
                    last = pe.transpose(ps[:, b + k // 4, (k % 4) * P:(k % 4 + 1) * P], fin[:, k, t * P:(t + 1) * P],
                                        ident[:, 0:P])
                last.then_inc(fin_mm.sem, 1)

        @block.scalar
        def _(act):
            def copy(dst, src):
                return act.activation(dst, src, ACT.Copy)

            act.wait_ge(dve_const.sem, DVE_CONSTS + 1)
            act.activation(c_act[:, :], cols[:, 0, ROW_C:ROW_C + KT], ACT.Silu).then_inc(act_const.sem, 1)
            for k in range(0, KT, 2):
                act.wait_ge(xt_mm.sem, k + 1)
                copy(x_sb[:, k, :], pair(2)).then_inc(xt_act.sem, 1)
            act.wait_ge(angles_ready.sem, 1)
            act.activation(sin_t[:, :], ang[:, :], ACT.Sin).then_inc(act_const.sem, 1)
            act.activation(ang_k[:, :], half[:, :], ACT.Sin).then_inc(act_const.sem, 1)

            def squares(l, ahead, k):
                if k < 2:
                    wait(act, h_ready, l, 2 * KT * ahead)
                else:
                    wait(act, sq_added, l, 2 * (KT - 1) * ahead + max(k - 2, 1))
                wait(act, dn_ev, l, KT * CHUNKS * ahead + k + 1 - KT)
                act.activation(t_ring[:, k % 2, :], x_sb[:, k, :], ACT.Square).then_inc(sq_ready.sem, 1)

            def norm(l, occ, shift):
                wait(act, sq_mm, l, occ + 1)
                act.activation(std[:, 0, :], ps[:, 6, 0:TT], ACT.Sqrt, bias=eps_col[:, :]).then_inc(std_ready.sem, 1)
                wait(act, rb_mm, l, occ + 1)
                copy(rb[:, :], pair(4)).then_inc(rb_ready.sem, 1)
                if shift is not None:
                    for k in range(KT):
                        wait(act, t_ready, l, KT * occ + k + 1)
                        act.activation(h_hi[:, k, :], t_ring[:, k % 2, :], ACT.Identity,
                                       bias=mod[:, shift, k:k + 1]).then_inc(h_hi_done.sem, 1)

            act.wait_ge(xt_act.sem, KT // 2)
            act.wait_ge(xt_dve.sem, KT // 2)
            for k in range(KT):
                squares(0, 0, k)
            with act.Fori(0, DEPTH) as l:
                split_hi(act, l, 0)
                split_hi(act, l, 1)
                act.dma_start(xs_dram, x_sb[:, :, :]).then_inc(x_spilled.sem, 16)
                norm(l, 0, 0)
                for n in range(3):
                    split_hi(act, l, n + 2)
                wait(act, x_spilled, l, 16)
                for j in range(4):
                    wait(act, u_mm, l, j + 1)
                    copy(uc[:, :, j, :], ps[:, j, :].rearrange("p (g m) -> p g m", m=M)).then_inc(z_act.sem, 1)
                split_hi(act, l, 5)
                wait(act, z_act, l, 4)
                wait(act, u_ev_dve, l, 4)
                act.dma_start(u_dram, uc[:, :, :, :]).then_inc(u_spilled.sem, 16)
                apart(act)
                with act.Fori(0, 4) as i:
                    for j in range(4):
                        split_hi(act, l, U_GATE + j + 2, 2 * i)
                        act.wait_ge(unit_used.sem, unit_used.at(l, U_GATE + j + 1) + 4 * i)
                        act.wait_ge(gst_spilled[j % 2].sem, gst_spilled[j % 2].at(l, 16 * (j // 2)) + 32 * i)
                        act.activation(gst[:, j % 2, :], pair(2 * (j % 2)), ACT.Sigmoid).then_inc(z_act.sem, 1)
                        act.wait_ge(z_act.sem, z_act.at(l, 5 + j) + 4 * i)
                        act.dma_start(gate_dram[bass.ds(4 * i + j, 1)].rearrange("o p n -> (o p) n"), gst[:, j % 2, :])\
                            .then_inc(gst_spilled[j % 2].sem, 16)
                wait(act, u_spilled, l, 16)
                def latent(n):
                    a = LATENT_ORDER[n]
                    wait(act, unit_used, l, U_CKV + n + 1)
                    copy(lat[:, a, :], pair(2 * n))
                    act.activation(lat_sq[:, a, :], pair(2 * n), ACT.Square,
                                   scale=math.sqrt(D / (Q_LORA, Q_LORA, KV_LORA)[a])).then_inc(lat_sq_ready.sem, 1)

                def latent_rms(side):
                    wait(act, lat_ss, l, side + 1)
                    act.activation(std[:, side, :], ps[:, 2 * side, 0:TT], ACT.Sqrt, bias=eps_col[:, :])\
                        .then_inc(lat_std.sem, 1)

                def latent_scale(side):
                    wait(act, lat_rb_mm, l, side + 1)
                    copy(lat_rb[:, side, :], pair(2 * side)).then_inc(lat_rb_ready.sem, 1)

                def latent_hi(n):
                    wait(act, lat_t, l, n + 1)
                    copy(latn_hi[:, LATENT_ORDER[n], :], lat[:, LATENT_ORDER[n], :]).then_inc(lat_hi_done.sem, 1)

                split_hi(act, l, U_CKV + 2)
                latent(0)
                split_hi(act, l, U_CKV + 3, 0, KR)
                latent(1)
                latent_rms(0)
                split_hi(act, l, U_CKV + 4, 0, HEAD)
                latent(2)
                latent_scale(0)
                latent_rms(1)
                latent_hi(0)
                latent_scale(1)
                latent_hi(1)
                latent_hi(2)
                split_hi(act, l, U_HEAD + 1, 0, HEAD)

                def rotary_key(head):
                    wait(act, kr_done, l, 3)
                    copy(k_hi[64:P, head, :], kr_t[64:P, 0, :]).then_inc(kr_hi_done.sem, 1)

                def even_queries_and_keys(i, ahead):
                    act.wait_ge(q_rot.sem, q_rot.at(l, 2 * ahead + 1) + 2 * i)
                    copy(q_hi[:, 0, :], q_f[:, :]).then_inc(q_hi_done.sem, 1)
                    act.wait_ge(k_mm.sem, k_mm.at(l, ahead + 1) + i)
                    for head in range(2):
                        copy(k_hi[0:64, head, :], pair(2, 64 * head, 64 * head + 64)).then_inc(k_hi_done.sem, 1)

                def attention_pair(i, last_pair):
                    def head_output(m):
                        rows = slice(64 * (m // 2), 64 * (m // 2) + 64)
                        cols_ = slice((m % 2) * HALF, (m % 2 + 1) * HALF)
                        act.wait_ge(pv_mm.sem, pv_mm.at(l, 2 * (m + 1)) + 8 * i)
                        copy(o_hi[rows, bass.ds(i, 1), cols_].rearrange("p o n -> p (o n)"), ps[rows, 6 + m % 2, :])\
                            .then_inc(o_hi_done.sem, 1)

                    for g in range(18):
                        if g >= 2:
                            tile = g - 2
                            if tile >= 4 and tile % 2 == 0:
                                act.wait_ge(pv_mm.sem, pv_mm.at(l, tile // 2 - 1) + 8 * i)
                            act.wait_ge(pt_mm.sem, pt_mm.at(l, 2 * tile + 1) + 32 * i)
                            copy(pt_hi[:, tile // 2 % 2, 0:4, (tile % 2) * P:(tile % 2 + 1) * P],
                                 ps[:, 4, :].rearrange("p (k n) -> p k n", k=4)).then_inc(pt_hi_done.sem, 1)
                            act.wait_ge(pt_mm.sem, pt_mm.at(l, 2 * tile + 2) + 32 * i)
                            if tile >= 2:
                                act.wait_ge(pt_ready[1].sem, pt_ready[1].at(l, tile - 1) + 16 * i)
                            copy(pt_f[:, tile % 2, :], ps[:, 5, :]).then_inc(pt_hi_done.sem, 1)
                        if 1 <= g <= 16:
                            r = g - 1
                            act.wait_ge(p_inv.sem, p_inv.at(l, r + 1) + 16 * i)
                            act.activation(probs[:, r % 3, :], probs[:, r % 3, :], ACT.Copy,
                                           scale=row_inv[:, r % 2:r % 2 + 1]).then_inc(p_ready.sem, 1)
                        if g < 16:
                            act.wait_ge(s_max.sem, s_max.at(l, g + 1) + 16 * i)
                            if g >= 3:
                                act.wait_ge(pt_mm.sem, pt_mm.at(l, 2 * (g - 2)) + 32 * i)
                            act.activation(probs[:, g % 3, :], pair(2 * (g % 2)), ACT.Exp, bias=neg_max[:, g % 2:g % 2 + 1],
                                           scale=-1.0, accum_out=row_sum[:, g % 2:g % 2 + 1]).then_inc(p_exp.sem, 1)
                        if g == 0:
                            for t in range(2):
                                act.wait_ge(v_mm.sem, v_mm.at(l, t + 1) + 2 * i)
                                copy(v_hi[:, 4 * t:4 * t + 4, :], ps[:, 4 + t, :].rearrange("p (k n) -> p k n", k=4))\
                                    .then_inc(v_hi_done.sem, 1)
                        if g == 2:
                            act.wait_ge(q_rot.sem, q_rot.at(l, 2) + 2 * i)
                            copy(q_hi[:, 1, :], q_f[:, :]).then_inc(q_hi_done.sem, 1)
                        if g in (1, 4):
                            if last_pair:
                                split_hi(act, l, U_GLU + g // 4)
                            else:
                                split_hi(act, l, U_HEAD + 2 + g // 4, i, HEAD)
                        if g >= 8 and g % 4 == 0:
                            head_output((g - 8) // 4)
                    if not last_pair:
                        even_queries_and_keys(i, 1)
                    head_output(3)

                rotary_key(0)
                even_queries_and_keys(0, 0)
                rotary_key(1)
                apart(act)
                with act.Fori(0, PAIRS - 1) as i:
                    attention_pair(i, False)
                attention_pair(PAIRS - 1, True)

                wait(act, s5_loaded, l, 16 * 14)
                wait(act, s5_pe, l, 1)
                act.activation(sm[:, S_DT, :], ldt[:, :], ACT.Exp).then_inc(s5_act.sem, 1)
                wait(act, s5_dve, l, S5_EXP_READY)
                act.activation(sm[:, S_MAG:S_MAG + 2, :], sm[:, S_AD:S_AD + 2, :], ACT.Exp).then_inc(s5_act.sem, 1)
                wait(act, s5_dve, l, S5_ANGLES_READY)
                act.activation(trig[:, :, :], sm[:, 0:6, :], ACT.Sin).then_inc(s5_act.sem, 1)
                def batch_inputs(b, i):
                    for s, (dst, bank) in enumerate(((mt_1, 0), (mt_2, 1), (ut, 3))):
                        act.wait_ge(s5_tr.sem, s5_tr.at(l, 3 * b + s + 1) + 6 * i)
                        copy(dst[:, b % 2, :, :], ps[:, bank, :].rearrange("p (g n) -> p g n", g=4))\
                            .then_inc(s5_tr_ev.sem, 1)
                    act.wait_ge(toe_col_mm.sem, toe_col_mm.at(l, b + 1) + 2 * i)
                    copy(toe_col[:, :, :], ps[:, 2, 0:4 * M].rearrange("p (g m) -> p g m", g=4))\
                        .then_inc(toe_col_done.sem, 1)

                def batch_outputs(b, i):
                    act.wait_ge(s5_pe.sem, s5_pe.at(l, b + 2) + 2 * i)
                    act.activation(yc[:, :, bass.ds((2 * i + b) * 4 * M, 4 * M)].rearrange("p j (g m) -> p j g m", m=M),
                                   ps[:, 6 + b % 2, :].rearrange("p (g j m) -> p j g m", g=4, m=M),
                                   ACT.Gelu_apprx_tanh).then_inc(y_gelu.sem, 1)

                batch_inputs(0, 0)
                apart(act)
                with act.Fori(0, 3) as i:
                    for b in range(2):
                        batch_inputs(b + 1, i)
                        batch_outputs(b, i)
                batch_inputs(1, 3)
                batch_outputs(0, 3)
                batch_outputs(1, 3)
                for q in range(4):
                    for s in range(2):
                        wait(act, yt_mm, l, 2 * q + s + 1)
                        copy(yt[:, q, :].rearrange("p (c j) -> p j c", j=CH)[:, 4 * s:4 * s + 4, :],
                             ps[:, 2 * q + s, :].rearrange("p (j c) -> p j c", j=4)).then_inc(yt_ev.sem, 1)
                for q in range(4):
                    wait(act, yt_ev, l, 2 * q + 2)
                    copy(y_hi[:, q, :], yt[:, q, :]).then_inc(y_hi_done.sem, 1)
                def glu_hi(n):
                    wait(act, glu_mul, l, n + 1)
                    copy(yg_hi[:, n, :], glu_s[:, n % 2, :]).then_inc(yg_hi_done.sem, 1)

                for n in range(4):
                    if n % 2:
                        if n == 1:
                            split_hi(act, l, U_MERGE)
                        wait(act, unit_used, l, U_GLU + n // 2 + 1)
                    else:
                        wait(act, glu_mm, l, n // 2 + 1)
                    if n >= 2:
                        wait(act, yg_ready, l, n - 1)
                    act.activation(glu_s[:, n % 2, :], pair(2 * n), ACT.Sigmoid,
                                   bias=pcol[:, ROW_BGLU + n:ROW_BGLU + n + 1]).then_inc(glu_sig.sem, 1)
                    if n:
                        glu_hi(n - 1)
                glu_hi(3)
                split_hi(act, l, U_MERGE + 1)
                apart(act)
                with act.Fori(0, 4) as i:
                    for j in range(2):
                        split_hi(act, l, U_MERGE + j + 2, i)
                        act.wait_ge(mg_step.sem, mg_step.at(l, 2 * j + 2) + 4 * i)
                        copy(mg_hi[:, bass.ds(2 * i + j, 1), :].rearrange("p o n -> p (o n)"), m_sum[:, :])\
                            .then_inc(mg_hi_done.sem, 1)
                wait(act, unit_used, l, U_OUT)
                wait(act, x_spilled, l, 16)
                act.dma_start(x_sb[:, :, :], xs_dram).then_inc(x_back.sem, 16)
                for n in range(KT):
                    split_hi(act, l, U_OUT + n + 2)
                    wait(act, wo_ev, l, n + 1)
                    if n >= 2:
                        wait(act, sq_added, l, KT - 1 + max(n - 2, 1))
                    act.activation(t_ring[:, n % 2, :], x_sb[:, n, :], ACT.Square).then_inc(sq_ready.sem, 1)
                norm(l, 1, 3)

                def up_part(n, q, c_static, c_reg, buf):
                    for a in range(2):
                        split_hi(act, l, n + 2 * a + 2, q)
                        act.wait_ge(unit_used.sem, unit_used.at(l, n + 2 * a + 1) + 2 * q)
                        act.wait_ge(hid_ready.sem, hid_ready.at(l, max(2 * (c_static - 1) + a + 1, 0)) + 2 * c_reg)
                        act.activation(silu[:, a, :], pair(4 * a), ACT.Silu).then_inc(silu_done.sem, 1)
                        split_hi(act, l, n + 2 * a + 3, q)
                        act.wait_ge(up_done.sem, up_done.at(l, 2 * c_static + a + 1) + 2 * c_reg)
                        copy(hid_hi[:, buf, a, :], silu[:, a, :]).then_inc(hid_hi_done.sem, 1)

                up_part(U_FFN, 0, 0, 0, 0)
                apart(act)
                with act.Fori(0, (CHUNKS - 1) // 2) as i:
                    for cc in range(2):
                        n = U_FFN + 4 + 6 * cc
                        up_part(n, 6 * i, 1 + cc, 2 * i, 1 - cc)
                        for d in range(2):
                            split_hi(act, l, n + 6 + d, 6 * i)
                for k in range(KT):
                    squares(l, 1, k)

            norm(DEPTH, 0, None)
            for t in range(TT):
                act.wait_ge(fin_mm.sem, t + 1)
                if t >= 2:
                    act.wait_ge(out_done[t % 2].sem, 16 * (t // 2))
                copy(o_row[:, t % 2, :], pair(2 * (t % 2))).then_inc(fin_ev.sem, 1)

        @block.vector
        def _(dve):
            def lo_of(out, value, hi):
                return dve.tensor_tensor(out, value, hi.bitcast(F32), ALU.subtract)

            dve.memset(ones_col[:, :], 1.0).then_inc(dve_const.sem, 1)
            dve.memset(mean_col[:, :], 1.0 / D).then_inc(dve_const.sem, 1)
            dve.memset(eps_col[:, :], EPS).then_inc(dve_const.sem, 1)
            for rows, v in ((slice(0, 64), -1.0), (slice(64, P), 1.0)):
                dve.memset(sgn[rows, :], v).then_inc(dve_const.sem, 1)
                dve.memset(nsgn[rows, :], -v).then_inc(dve_const.sem, 1)
            for counter, n in credits:
                dve.sem_inc(counter.sem, n)
            dve.wait_ge(cols_mm.sem, 1)
            dve.tensor_copy(cols[:, :, :], ps[:, 0, 0:DEPTH * P].rearrange("p (d r) -> p d r", d=DEPTH)[:, :, 0:ROWS])\
                .then_inc(dve_const.sem, 1)

            def ada_product(l, n, k, at_q=0):
                s = k % 2
                dve.wait_ge(ada_loaded[s].sem, ada_loaded[s].at(l, 16 * (n // 2 + 1)) + 8 * at_q)
                dve.wait_ge(ada_used.sem, ada_used.at(l, n) + at_q)
                if k == 0:
                    last = dve.tensor_scalar(ada_acc[:, :], ada_raw[:, s, :], c_act[:, 0:1], None, ALU.mult)
                else:
                    last = dve.scalar_tensor_tensor(ada_acc[:, :], ada_raw[:, s, :], c_act[:, k:k + 1], ada_acc[:, :],
                                                    ALU.mult, ALU.add)
                last.then_inc(ada_used.sem, 1)

            def modulation(l, n, at_q, dst, bias):
                dve.wait_ge(mod_mm.sem, mod_mm.at(l, n + 1) + at_q)
                apart(dve)
                dve.tensor_tensor(dst, ps[:, 7, 0:KT], bias, ALU.add).then_inc(mod_ready.sem, 1)

            dve.wait_ge(pool_const.sem, 2)
            dve.wait_ge(act_const.sem, 1)
            dve.wait_ge(dve_const.sem, DVE_CONSTS + 1)
            dve.wait_ge(const_loaded.sem, 16 * CONSTS)
            steps = [DVE_CONSTS + 1]

            def link(inst):
                inst.then_inc(dve_const.sem, 1)
                steps[0] += 1
                dve.wait_ge(dve_const.sem, steps[0])

            def reduce_angle(counted, src, tmp, dst):
                counted(dve.tensor_scalar(tmp, src, 1.0 / (2 * math.pi), ROUND, ALU.mult, ALU.add))
                counted(dve.tensor_scalar(tmp, tmp, ROUND, None, ALU.subtract))
                for part in TWO_PI_PARTS:
                    counted(dve.scalar_tensor_tensor(dst, tmp, -part, src, ALU.mult, ALU.add))
                    src = dst
                counted(dve.tensor_scalar(dst, dst, MAX_ANGLE, -MAX_ANGLE, ALU.min, ALU.max))

            link(dve.tensor_copy(pos_f[:, :], pos_i[:, :]))
            link(dve.tensor_scalar(ang[:, :], pos_f[:, :], rope_sb[:, 0:1], None, ALU.mult))
            reduce_angle(link, ang[:, :], ang_k[:, :], ang[:, :])
            link(dve.tensor_scalar(half[:, :], ang[:, :], 0.5, None, ALU.mult))
            dve.sem_inc(angles_ready.sem, 1)
            link(dve.tensor_scalar(pos_i2[:, :], pos_i[:, :], 16, None, ALU.arith_shift_right))
            link(dve.tensor_copy(pos_f[:, :], pos_i2[:, :]))
            link(dve.tensor_scalar(pos_i2[:, :], pos_i[:, :], 65535, None, ALU.bitwise_and))
            link(dve.tensor_copy(pos_lo[:, :], pos_i2[:, :]))
            link(dve.tensor_scalar(posq_i2[:, :], posq_i[:, :], 16, None, ALU.arith_shift_right))
            link(dve.tensor_copy(posq_f[:, 0, :], posq_i2[:, :]))
            link(dve.tensor_scalar(posq_i2[:, :], posq_i[:, :], 65535, None, ALU.bitwise_and))
            link(dve.tensor_copy(posq_f[:, 1, :], posq_i2[:, :]))

            for m in range(2):
                for k in range(KT):
                    ada_product(-1, 4 * KT + m * KT + k, k)
                    if m == 0 and k % 2:
                        dve.wait_ge(xt_mm.sem, k + 1)
                        dve.tensor_copy(x_sb[:, k, :], pair(4)).then_inc(xt_dve.sem, 1)
                    if k % 2 == 0:
                        t = (m * KT + k) // 2
                        link(dve.tensor_scalar(mask_t[:, :], pos_f[:, :], posq_f[:, 0, t:t + 1], 65536.0,
                                               ALU.subtract, ALU.mult))
                        link(dve.scalar_tensor_tensor(mask_t[:, :], pos_lo[:, :], posq_f[:, 1, t:t + 1], mask_t[:, :],
                                                      ALU.subtract, ALU.add))
                        link(dve.tensor_scalar(mask[:, t, :], mask_t[:, :], 0.0, MASKED, ALU.is_gt, ALU.mult))
                modulation(-1, 4 + m, 0, mod[:, m, :], cols[:, 0, ROW_B_ADA + m * KT:ROW_B_ADA + (m + 1) * KT])
            dve.wait_ge(mod_ready.sem, 2)
            dve.scalar_tensor_tensor(a1[:, :], mod[:, 1, :], 1.0, cols[:, 0, ROW_N1:ROW_N1 + KT], ALU.add, ALU.mult)\
                .then_inc(a1_ready.sem, 1)

            dve.wait_ge(act_const.sem, 3)
            link(dve.tensor_tensor(ang_k[:, :], ang_k[:, :], ang_k[:, :], ALU.mult))
            link(dve.tensor_scalar(ang_k[:, :], ang_k[:, :], -2.0, 1.0, ALU.mult, ALU.add))
            link(dve.tensor_scalar(tq[:, :], ang_k[:, :], rope_sb[:, 1:2], rope_sb[:, 3:4], ALU.mult, ALU.add))
            link(dve.scalar_tensor_tensor(tq[:, :], sin_t[:, :], rope_sb[:, 2:3], tq[:, :], ALU.mult, ALU.add))
            link(dve.tensor_scalar(tk[:, :], ang_k[:, :], rope_sb[:, 4:5], None, ALU.mult))
            link(dve.scalar_tensor_tensor(tk[:, :], sin_t[:, :], rope_sb[:, 5:6], tk[:, :], ALU.mult, ALU.add))

            def norm(l, occ, gain):
                wait(dve, std_ready, l, occ + 1)
                dve.reciprocal(rstd[:, 0, :], std[:, 0, :]).then_inc(rstd_ready.sem, 1)
                wait(dve, rb_ready, l, occ + 1)

                def scaled(k):
                    if k >= 2:
                        wait(dve, h_ready, l, KT * occ + k - 1)
                    dve.scalar_tensor_tensor(t_ring[:, k % 2, :], x_sb[:, k, :], gain[:, k:k + 1], rb[:, :],
                                             ALU.mult, ALU.mult).then_inc(t_ready.sem, 1)

                scaled(0)
                for k in range(KT):
                    if k + 1 < KT:
                        scaled(k + 1)
                    wait(dve, h_hi_done, l, KT * occ + k + 1)
                    dve.scalar_tensor_tensor(h_lo[:, k, :], t_ring[:, k % 2, :], mod[:, 3 * occ, k:k + 1],
                                             h_hi[:, k, :].bitcast(F32), ALU.add, ALU.subtract).then_inc(h_ready.sem, 1)

            with dve.Fori(0, DEPTH) as l:
                dve.tensor_copy(pcol[:, :], cols[:, bass.ds(l, 1), :].rearrange("p o r -> p (o r)")).then_inc(pcol_ready.sem, 1)
                wait(dve, a1_ready, l, 0)
                wait(dve, pcol_ready, l, 1)
                norm(l, 0, a1)
                wait(dve, x_spilled, l, 16)
                for j in range(4, CH):
                    if j < CH - 1:
                        wait(dve, u_mm, l, j + 1)
                    else:
                        wait(dve, unit_used, l, U_GATE)
                    dve.tensor_copy(uc[:, :, j, :], ps[:, j, :].rearrange("p (g m) -> p g m", m=M)).then_inc(u_ev_dve.sem, 1)
                apart(dve)
                with dve.Fori(0, 4) as i:
                    for k in range(KT):
                        ada_product(l, k, k, KT * i)
                    modulation(l, 0, i, mod[:, bass.ds(i + 2, 1), :].rearrange("p o k -> p (o k)"),
                               pcol[:, bass.ds((i + 2) * KT, KT)])
                wait(dve, mod_ready, l, 4)
                dve.scalar_tensor_tensor(a2[:, :], mod[:, 4, :], 1.0, pcol[:, ROW_N2:ROW_N2 + KT], ALU.add, ALU.mult)\
                    .then_inc(a2_ready.sem, 1)
                for s in range(2):
                    wait(dve, gst_spilled[s], l, 16 * KT)

                def latent_rms(side):
                    wait(dve, lat_std, l, side + 1)
                    dve.reciprocal(rstd[:, side, :], std[:, side, :]).then_inc(lat_rstd.sem, 1)

                def latent(n):
                    a, side = LATENT_ORDER[n], (n + 1) // 2
                    wait(dve, lat_rb_ready, l, side + 1)
                    dve.scalar_tensor_tensor(lat[:, a, :], lat[:, a, :], pcol[:, ROW_QN + a:ROW_QN + a + 1],
                                             lat_rb[:, side, :], ALU.mult, ALU.mult).then_inc(lat_t.sem, 1)

                def latent_lo(n):
                    a = LATENT_ORDER[n]
                    wait(dve, lat_hi_done, l, n + 1)
                    lo_of(latn_lo[:, a, :], lat[:, a, :], latn_hi[:, a, :]).then_inc(lat_ready.sem, 1)

                latent_rms(0)
                latent(0)
                latent_rms(1)
                latent_lo(0)
                latent(1)
                latent(2)
                latent_lo(1)
                latent_lo(2)
                wait(dve, unit_used, l, U_KR + 1)
                dve.tensor_tensor(kr_t[64:P, 0, :], pair(6, 0, 64), tk[0:64, :], ALU.mult).then_inc(kr_done.sem, 1)
                dve.tensor_tensor(kr_t[64:P, 1, :], pair(6, 64, P), tk[64:P, :], ALU.mult).then_inc(kr_done.sem, 1)
                wait(dve, kr_done, l, 2)
                dve.tensor_tensor(kr_t[64:P, 0, :], kr_t[64:P, 0, :], kr_t[64:P, 1, :], ALU.add).then_inc(kr_done.sem, 1)

                def queries(i, head, ahead=0):
                    dve.wait_ge(q_mm.sem, q_mm.at(l, 2 * ahead + head + 1) + 2 * i)
                    dve.tensor_tensor(q_f[:, :], pair(6 * head), tq[:, :], ALU.mult).then_inc(q_rot.sem, 1)

                def queries_lo(i, head, ahead=0):
                    dve.wait_ge(q_hi_done.sem, q_hi_done.at(l, 2 * ahead + head + 1) + 2 * i)
                    lo_of(q_lo[:, head, :], q_f[:, :], q_hi[:, head, :]).then_inc(q_ready.sem, 1)

                def keys_lo(i, ahead=0):
                    for head in range(2):
                        dve.wait_ge(k_hi_done.sem, k_hi_done.at(l, 2 * ahead + head + 1) + 2 * i)
                        lo_of(k_lo[0:64, head, :], pair(2, 64 * head, 64 * head + 64), k_hi[0:64, head, :])\
                            .then_inc(k_ready.sem, 1)

                def attention_pair(i, last_pair):
                    def head_output(m):
                        rows = slice(64 * (m // 2), 64 * (m // 2) + 64)
                        cols_ = slice((m % 2) * HALF, (m % 2 + 1) * HALF)
                        dve.wait_ge(o_hi_done.sem, o_hi_done.at(l, m + 1) + 4 * i)
                        lo_of(o_lo[rows, bass.ds(i, 1), cols_].rearrange("p o n -> p (o n)"), ps[rows, 6 + m % 2, :],
                              o_hi[rows, bass.ds(i, 1), cols_].rearrange("p o n -> p (o n)")).then_inc(o_ready.sem, 1)

                    for g in range(18):
                        if 1 <= g <= 16:
                            r = g - 1
                            dve.wait_ge(p_exp.sem, p_exp.at(l, r + 1) + 16 * i)
                            if r >= 2:
                                dve.wait_ge(p_ready.sem, p_ready.at(l, r - 1) + 16 * i)
                            dve.reciprocal(row_inv[:, r % 2:r % 2 + 1], row_sum[:, r % 2:r % 2 + 1]).then_inc(p_inv.sem, 1)
                        if g >= 2:
                            tile = g - 2
                            dve.wait_ge(pt_hi_done.sem, pt_hi_done.at(l, 2 * tile + 1) + 32 * i)
                            at = (slice(None), tile // 2 % 2, slice(0, 4), slice((tile % 2) * P, (tile % 2 + 1) * P))
                            lo_of(pt_lo[at], ps[:, 4, :].rearrange("p (k n) -> p k n", k=4), pt_hi[at])\
                                .then_inc(pt_ready[0].sem, 1)
                        if g < 16:
                            dve.wait_ge(s_mm.sem, s_mm.at(l, g + 1) + 16 * i)
                            apart(dve)
                            s = pair(2 * (g % 2))
                            dve.tensor_tensor_reduce(out=s, in0=s, in1=mask[:, g % TT, :], scale=1.0, scalar=3e38,
                                                     op0=ALU.add, op1=ALU.min, accum_out=neg_max[:, g % 2:g % 2 + 1])\
                                .then_inc(s_max.sem, 1)
                        if g == 0:
                            for t in range(2):
                                dve.wait_ge(v_hi_done.sem, v_hi_done.at(l, t + 1) + 2 * i)
                                lo_of(v_lo[:, 4 * t:4 * t + 4, :], ps[:, 4 + t, :].rearrange("p (k n) -> p k n", k=4),
                                      v_hi[:, 4 * t:4 * t + 4, :]).then_inc(v_ready.sem, 1)
                        if g == 2:
                            queries(i, 1)
                            queries_lo(i, 1)
                        if g == 17 and not last_pair:
                            queries(i, 0, 1)
                        if g >= 8 and g % 4 == 0:
                            head_output((g - 8) // 4)
                    if not last_pair:
                        queries_lo(i, 0, 1)
                        keys_lo(i, 1)
                    head_output(3)

                queries(0, 0)
                queries_lo(0, 0)
                keys_lo(0)
                apart(dve)
                with dve.Fori(0, PAIRS - 1) as i:
                    attention_pair(i, False)
                attention_pair(PAIRS - 1, True)

                n_s5 = [0]

                def s5(inst, linked=True):
                    inst.then_inc(s5_dve.sem, 1)
                    n_s5[0] += 1
                    if linked:
                        wait(dve, s5_dve, l, n_s5[0])

                wait(dve, s5_loaded, l, 16 * 14)
                wait(dve, s5_pe, l, 1)
                s5(dve.tensor_copy(a_t[:, :, :], ps[:, 0, 0:2 * G].rearrange("p (i g) -> p i g", i=2)), False)
                s5(dve.tensor_copy(d_t[:, :], ps[:, 0, 2 * G:3 * G]), False)
                s5(dve.tensor_copy(c_st[:, :, :], ps[:, 1, :].rearrange("p (g m) -> p g m", m=M)), False)
                s5(dve.tensor_copy(c_sw[:, :, :], ps[:, 2, :].rearrange("p (g m) -> p g m", m=M)))
                ar, ai = a_t[:, 0, :], a_t[:, 1, :]
                v = [sm[:, t, :] for t in range(S_SCI + 1)]
                wait(dve, s5_act, l, 1)
                s5(dve.tensor_tensor(v[S_AD], ar, v[S_DT], ALU.mult))
                s5(dve.tensor_scalar(v[S_AD8], v[S_AD], float(CH), None, ALU.mult))
                assert n_s5[0] == S5_EXP_READY
                s5(dve.tensor_tensor(v[0], ai, v[S_DT], ALU.mult))
                for a, factor in ((0, None), (2, float(CH)), (4, 16.0)):
                    if factor:
                        s5(dve.tensor_scalar(v[a], v[a - 2], factor, None, ALU.mult))
                    reduce_angle(s5, v[a], v[S_K], v[a])
                    s5(dve.tensor_scalar(v[a + 1], v[a], 0.5, None, ALU.mult))
                assert n_s5[0] == S5_ANGLES_READY
                s5(dve.tensor_scalar(c_n[:, :, :], c_st[:, :, :], nsgn[:, :], None, ALU.mult), False)
                wait(dve, s5_act, l, 3)
                cosines = trig[:, 1::2, :]
                s5(dve.tensor_tensor(cosines, cosines, cosines, ALU.mult))
                s5(dve.tensor_scalar(cosines, cosines, -2.0, 1.0, ALU.mult, ALU.add))
                s5(dve.memset(powers[:, 0, :, :, 0:1], 1.0), False)
                s5(dve.memset(powers[:, 1, :, :, 0:1], 0.0), False)
                for part, side in ((0, 1), (1, 0)):
                    s5(dve.tensor_tensor(powers[:, part, 0, :, 1], v[S_MAG], trig[:, side, :], ALU.mult), False)
                    s5(dve.tensor_copy(powers[:, part, 1:3, :, 1], trig[:, 2 + side::2, :]))
                tmp = [z_tmp[:, t, :, :].rearrange("p g n -> p (g n)").rearrange("p (g n) -> p g n", g=G) for t in range(3)]
                tmp3 = [t[:, :, :, :].rearrange("p a g n -> p (a g n)")[:, 0:3 * G * 8]
                        .rearrange("p (t g n) -> p t g n", t=3, g=G) for t in (mt_1, mt_2)]
                m = 1
                while m < 16:
                    n = min(m, 15 - m)
                    tabs = slice(0, 3) if m < 8 else slice(1, 2)
                    size = tabs.stop - tabs.start
                    one, nxt = slice(1, n + 1), slice(m + 1, m + n + 1)
                    fr, fi = (powers[:, part, tabs, :, m:m + 1].broadcast_to([P, size, G, n]) for part in range(2))
                    for part, (x_a, x_b), op in ((0, (0, 1), ALU.subtract), (1, (1, 0), ALU.add)):
                        s5(dve.tensor_tensor(tmp3[0][:, 0:size, :, 0:n], powers[:, x_a, tabs, :, one], fr, ALU.mult), False)
                        s5(dve.tensor_tensor(tmp3[1][:, 0:size, :, 0:n], powers[:, x_b, tabs, :, one], fi, ALU.mult))
                        s5(dve.tensor_tensor(powers[:, part, tabs, :, nxt], tmp3[0][:, 0:size, :, 0:n],
                                             tmp3[1][:, 0:size, :, 0:n], op))
                    m += n
                    if m == 15:
                        break
                pw_re, pw_im = abar_powers[:, 0], abar_powers[:, 1]
                s5(dve.tensor_scalar(pw_s[:, 0, :, :], pw_re[:, :, 0:CH + 1], nsgn[:, :], None, ALU.mult), False)
                s5(dve.tensor_scalar(pw_s[:, 1, :, :], pw_im[:, :, 0:CH + 1], sgn[:, :], None, ALU.mult))
                for t in range(CH):
                    s5(dve.tensor_copy(pw_down[:, 0:2, :, t], abar_powers[:, :, :, CH - 1 - t]), False)
                    s5(dve.tensor_copy(pw_down[:, 2:4, :, t], pw_s[:, :, :, CH - 1 - t]), False)
                s5(dve.tensor_scalar(v[S_NR], pw_re[:, :, 1], 1.0, None, ALU.subtract), False)
                s5(dve.tensor_tensor(v[S_T1], ar, ar, ALU.mult), False)
                s5(dve.tensor_tensor(v[S_T2], ai, ai, ALU.mult))
                s5(dve.tensor_tensor(v[S_T1], v[S_T1], v[S_T2], ALU.add))
                s5(dve.reciprocal(v[S_DEN], v[S_T1]))
                for dst, x_a, x_b, op in ((v[S_CR], v[S_NR], pw_im[:, :, 1], ALU.add),
                                          (v[S_CI], pw_im[:, :, 1], v[S_NR], ALU.subtract)):
                    s5(dve.tensor_tensor(v[S_T1], x_a, ar, ALU.mult), False)
                    s5(dve.tensor_tensor(v[S_T2], x_b, ai, ALU.mult))
                    s5(dve.tensor_tensor(v[S_T1], v[S_T1], v[S_T2], op))
                    s5(dve.tensor_tensor(dst, v[S_T1], v[S_DEN], ALU.mult))
                s5(dve.tensor_scalar(v[S_SCI], v[S_CI], sgn[:, :], None, ALU.mult))
                cr, sci = (v[t].unsqueeze(2).broadcast_to([P, G, M]) for t in (S_CR, S_SCI))
                for dst, x_a, x_b, op in ((bb, b_st, b_sw, ALU.add), (bb_sw, b_sw, b_st, ALU.subtract)):
                    s5(dve.tensor_tensor(tmp[0], x_a[:, :, :], cr, ALU.mult), False)
                    s5(dve.tensor_tensor(tmp[1], x_b[:, :, :], sci, ALU.mult))
                    s5(dve.tensor_tensor(dst[:, :, :], tmp[0], tmp[1], op))
                s5(dve.memset(pq[:, :, :, 0:1], 0.0), False)
                s5(dve.memset(shift[:, P:], 0.0), False)
                s5(dve.tensor_copy(shift[:, 0:P], ident[:, :]))
                assert n_s5[0] == S5_DVE_STEPS, n_s5[0]

                apart(dve)
                with dve.Fori(0, 4) as i:
                    for j in range(2):
                        first_group = (2 * i + j) * 4
                        grp = bass.ds(first_group, 4)
                        at_rot = [18 * j]

                        def rot(inst, linked=True):
                            inst.then_inc(rot_step.sem, 1)
                            at_rot[0] += 1
                            if linked:
                                dve.wait_ge(rot_step.sem, rot_step.at(l, at_rot[0]) + 36 * i)

                        def fine(side):
                            return powers[:, side, 1, grp, :].unsqueeze(2).broadcast_to([P, 4, 8, 16])

                        def coarse(side):
                            return powers[:, side, 2, grp, 0:8].unsqueeze(3).broadcast_to([P, 4, 8, 16])

                        def by_chunk(view):
                            return view.rearrange("p g (a b) -> p g a b", b=16)

                        t0, t1, t2 = (z_tmp[:, t, :, :] for t in range(3))
                        for side, (x_a, x_b), op in ((0, (0, 1), ALU.subtract), (1, (1, 0), ALU.add)):
                            rot(dve.tensor_tensor(by_chunk(t0), coarse(x_a), fine(0), ALU.mult), False)
                            rot(dve.tensor_tensor(by_chunk(t1), coarse(x_b), fine(1), ALU.mult))
                            rot(dve.tensor_tensor(rot_b[:, side, :, :], t0, t1, op))
                        def by_powers(table):
                            return table[:, grp, 1:CH + 1].unsqueeze(3).broadcast_to([P, 4, CH, M])

                        def by_step(view):
                            return view.rearrange("p g (j m) -> p g j m", m=M)

                        for dst, table, c_table in ((t0, pw_s[:, 1], c_st), (t1, abar_powers[:, 0], c_sw)):
                            rot(dve.tensor_tensor(by_step(dst), by_powers(table),
                                                  c_table[:, grp, :].unsqueeze(2).broadcast_to([P, 4, CH, M]), ALU.mult))
                        rot(dve.tensor_tensor(m_2[:, j, :, :, :], by_step(t0), by_step(t1), ALU.subtract))
                        dve.wait_ge(v12_mm.sem, v12_mm.at(l, j + 1) + 2 * i)
                        for side, dst in ((0, t0), (1, t1)):
                            rot(dve.tensor_tensor(dst, rot_b[:, side, :, :], ps[:, 4 + side, :]
                                                  .rearrange("p (g c) -> p g c", g=4), ALU.mult), side == 1)
                        rot(dve.tensor_tensor(t2, t0, t1, ALU.add))
                        for g in range(4):
                            rot(dve.tensor_tensor_scan(out=g_sb[:, g, :],
                                                       data0=sm[:, S_MAG8, bass.ds(first_group + g, 1)].broadcast_to([P, NC]),
                                                       data1=z_tmp[:, 2, g, :], initial=0.0, op0=ALU.mult, op1=ALU.add),
                                g == 3)
                        dve.wait_ge(toe_mm.sem, toe_mm.at(l, j + 1) + 2 * i)
                        for g in range(4):
                            last = dve.scalar_tensor_tensor(
                                toe[:, j, g, :].rearrange("p (j m) -> p j m", m=M),
                                ident[:, 0:P].rearrange("p (j m) -> p j m", m=M), d_t[:, bass.ds(first_group + g, 1)],
                                ps[:, 2, :].rearrange("p (j g m) -> p g j m", g=4, m=M)[:, g], ALU.mult, ALU.add)
                        last.then_inc(toe_ready.sem, 1)
                        dve.wait_ge(s5_pe.sem, s5_pe.at(l, j + 1) + 2 * i)
                        for side in range(2):
                            rot(dve.tensor_tensor(pq[:, side, :, 1:], rot_b[:, side, :, :], g_sb[:, :, :], ALU.mult), False)
                        assert at_rot[0] == 18 * (j + 1)
                for q in range(4):
                    wait(dve, y_hi_done, l, q + 1)
                    lo_of(y_lo[:, q, :], yt[:, q, :], y_hi[:, q, :]).then_inc(y_ready.sem, 1)
                for n in range(4):
                    wait(dve, glu_sig, l, n + 1)
                    dve.tensor_tensor(glu_s[:, n % 2, :], yt[:, n, :], glu_s[:, n % 2, :], ALU.mult).then_inc(glu_mul.sem, 1)
                    wait(dve, yg_hi_done, l, n + 1)
                    lo_of(yg_lo[:, n, :], glu_s[:, n % 2, :], yg_hi[:, n, :]).then_inc(yg_ready.sem, 1)
                apart(dve)
                with dve.Fori(0, 4) as i:
                    for j in range(2):
                        dve.wait_ge(unit_used.sem, unit_used.at(l, U_MERGE + j + 1) + 2 * i)
                        dve.wait_ge(gl_loaded.sem, gl_loaded.at(l, 32 * (j + 1)) + 64 * i)
                        dve.tensor_tensor(m_ab[:, 0, :], pair(4 * j), gl[:, 0, :], ALU.mult).then_inc(mg_step.sem, 1)
                        dve.tensor_tensor(m_ab[:, 1, :], pair(4 * j + 2), gl[:, 1, :], ALU.mult).then_inc(mg_free.sem, 1)
                        dve.wait_ge(mg_step.sem, mg_step.at(l, 2 * j + 1) + 4 * i)
                        dve.wait_ge(mg_free.sem, mg_free.at(l, j + 1) + 2 * i)
                        dve.tensor_tensor(m_sum[:, :], m_ab[:, 0, :], m_ab[:, 1, :], ALU.add).then_inc(mg_step.sem, 1)
                        dve.wait_ge(mg_hi_done.sem, mg_hi_done.at(l, j + 1) + 2 * i)
                        tile = bass.ds(2 * i + j, 1)
                        lo_of(mg_lo[:, tile, :].rearrange("p o n -> p (o n)"), m_sum[:, :],
                              mg_hi[:, tile, :].rearrange("p o n -> p (o n)")).then_inc(mg_ready.sem, 1)
                wait(dve, x_back, l, 16)
                apart(dve)
                with dve.Fori(0, 2) as i:
                    for j in range(4):
                        dve.wait_ge(unit_used.sem, unit_used.at(l, U_OUT + j + 1) + 4 * i)
                        tile = bass.ds(4 * i + j, 1)
                        x_tile = x_sb[:, tile, :].rearrange("p o n -> p (o n)")
                        dve.scalar_tensor_tensor(x_tile, pair(2 * (j % 2)), mod[:, 2, tile], x_tile, ALU.mult, ALU.add)\
                            .then_inc(wo_ev.sem, 1)
                        for k in (2 * j, 2 * j + 1):
                            ada_product(l, 4 * KT + k, k, KT * i)
                    modulation(l, 4, i, mod[:, bass.ds(i, 1), :].rearrange("p o k -> p (o k)"),
                               cols[:, bass.ds(1 - l, 1), bass.ds(i * KT, KT)].rearrange("p o k -> p (o k)"))
                wait(dve, mod_ready, l, 6)
                apart(dve)
                dve.scalar_tensor_tensor(a1[:, :], mod[:, 1, :], 1.0,
                                         cols[:, bass.ds(1 - l, 1), ROW_N1:ROW_N1 + KT].rearrange("p o k -> p (o k)"),
                                         ALU.add, ALU.mult).then_inc(a1_ready.sem, 1)
                wait(dve, a2_ready, l, 1)
                norm(l, 1, a2)

                def up_part(n, q, c_static, c_reg, buf):
                    for a in range(2):
                        dve.wait_ge(unit_used.sem, unit_used.at(l, n + 2 * a + 2) + 2 * q)
                        dve.wait_ge(silu_done.sem, silu_done.at(l, 2 * c_static + a + 1) + 2 * c_reg)
                        dve.tensor_tensor(silu[:, a, :], silu[:, a, :], pair(4 * a + 2), ALU.mult).then_inc(up_done.sem, 1)
                        dve.wait_ge(hid_hi_done.sem, hid_hi_done.at(l, 2 * c_static + a + 1) + 2 * c_reg)
                        lo_of(hid_lo[:, buf, a, :], silu[:, a, :], hid_hi[:, buf, a, :]).then_inc(hid_ready.sem, 1)

                def down_part(n, q, c_static, c_reg):
                    for t in range(KT):
                        if t % 4 < 3:
                            dve.wait_ge(dn_mm.sem, dn_mm.at(l, 6 * c_static + 3 * (t // 4) + t % 4 + 1) + 6 * c_reg)
                        else:
                            dve.wait_ge(unit_used.sem, unit_used.at(l, n + t // 4 + 1) + 2 * q)
                        dve.wait_ge(dn_ev.sem, dn_ev.at(l, 8 * (c_static - 1) + t + 1) + 8 * c_reg)
                        dve.scalar_tensor_tensor(x_sb[:, t, :], pair(2 * (t % 2)), mod[:, 5, t:t + 1], x_sb[:, t, :],
                                                 ALU.mult, ALU.add).then_inc(dn_ev.sem, 1)

                up_part(U_FFN, 0, 0, 0, 0)
                apart(dve)
                with dve.Fori(0, (CHUNKS - 1) // 2) as i:
                    for cc in range(2):
                        n = U_FFN + 4 + 6 * cc
                        up_part(n, 6 * i, 1 + cc, 2 * i, 1 - cc)
                        down_part(n + 4, 6 * i, cc, 2 * i)
                down_part(UNITS - 2, 0, CHUNKS - 1, 0)

            wait(dve, std_ready, DEPTH, 1)
            dve.reciprocal(rstd[:, 0, :], std[:, 0, :]).then_inc(rstd_ready.sem, 1)
            wait(dve, rb_ready, DEPTH, 1)
            for k in range(KT):
                dve.scalar_tensor_tensor(fin[:, k, :], x_sb[:, k, :], cols[:, 0, ROW_FG + k:ROW_FG + k + 1], rb[:, :],
                                         ALU.mult, ALU.mult).then_inc(fin_t.sem, 1)


INPUTS = ("x", "c", "positions", "w_ada", "b_ada", "norm1_g", "w_in", "ssm_a_re", "ssm_a_im", "ssm_log_dt",
          "ssm_b_re", "ssm_b_im", "ssm_c_re", "ssm_c_im", "ssm_d", "w_glu", "b_glu", "w_a_out", "q_norm_g",
          "w_uq", "kv_norm_g", "w_uk", "w_uv", "w_b_out", "w_out", "norm2_g", "w_gate", "w_up", "w_down",
          "final_g")


def kernel(**inputs):
    import concourse.bacc as bacc
    from concourse.bass_utils import run_bass_kernel_spmd

    nc = bacc.Bacc("TRN2", target_bir_lowering=False, num_devices=1)
    arrays = {f"in_{name}": np.ascontiguousarray(inputs[name]) for name in INPUTS}
    arrays["in_rope_const"] = rope_rows()
    args = [nc.dram_tensor(name, a.shape, mybir.dt.from_np(a.dtype), kind="ExternalInput").ap()
            for name, a in arrays.items()]
    out = nc.dram_tensor("out", arrays["in_x"].shape, F32, kind="ExternalOutput").ap()
    trunk(nc, *args, out)
    return run_bass_kernel_spmd(nc, [arrays], core_ids=[0]).results[0]["out"]
```
